# Optimizing a Trainium2 kernel written in Bass

```python
import jax
import jax.numpy as jnp
from jax import lax
import numpy as np

D_MODEL = 2048
BATCH = 1
SEQ = 256
DEPTH = 1

MIX_WIDTH = D_MODEL
ATT_WIDTH = MIX_WIDTH // 2
HGRN_WIDTH = MIX_WIDTH - ATT_WIDTH
HEAD_DIM = 128
N_ATT_HEADS = ATT_WIDTH // HEAD_DIM
N_KV_GROUPS = 2
HEADS_PER_GROUP = N_ATT_HEADS // N_KV_GROUPS
KV_WIDTH = N_KV_GROUPS * HEAD_DIM
CMP_BLOCK = 32
CMP_STRIDE = 16
SEL_BLOCK = 64
N_SEL = 16
WINDOW = 512
Q_BLOCK = 64
FORCE_BONUS = 1.0e4
ROPE_THETA = 10000.0
HGRN_HEAD_DIM = 128
N_HGRN_HEADS = HGRN_WIDTH // HGRN_HEAD_DIM
HGRN_CHUNK = 64
N_EXPERT_GROUPS = 4
EXPERTS_PER_GROUP = 8
N_EXPERTS = N_EXPERT_GROUPS * EXPERTS_PER_GROUP
EXPERT_TOP_K = 2
D_EXPERT = 512
IN_COLS = ATT_WIDTH + 6 * KV_WIDTH + 3 * N_ATT_HEADS + 4 * HGRN_WIDTH
EPS = 1e-6

kernel_name = 'hybrid_nsa_hgrn2_hmoe_block'

def rmsnorm(x, g):
    xf = x.astype(jnp.float32)
    y = xf * lax.rsqrt(jnp.mean(xf * xf, axis=-1, keepdims=True) + EPS)
    return (y * g.astype(jnp.float32)).astype(x.dtype)

def rope(t, pos):
    d = t.shape[-1]
    inv_freq = ROPE_THETA ** (-jnp.arange(0, d, 2, dtype=jnp.float32) / d)
    ang = pos.astype(jnp.float32)[:, :, None, None] * inv_freq
    cos, sin = jnp.cos(ang), jnp.sin(ang)
    tf = t.astype(jnp.float32)
    t1, t2 = tf[..., : d // 2], tf[..., d // 2:]
    return jnp.concatenate([t1 * cos - t2 * sin, t2 * cos + t1 * sin], axis=-1).astype(t.dtype)

def masked_softmax(s, mask):
    s = jnp.where(mask, s.astype(jnp.float32), -jnp.inf)
    m = jnp.max(s, axis=-1, keepdims=True)
    m = jnp.where(jnp.isfinite(m), m, 0.0)
    p = jnp.exp(s - m)
    return p / jnp.maximum(jnp.sum(p, axis=-1, keepdims=True), 1e-30)

def compress_blocks(t, pos_emb, w1, w2):
    B, S, G, d = t.shape
    nc = (S - CMP_BLOCK) // CMP_STRIDE + 1
    idx = (jnp.arange(nc) * CMP_STRIDE)[:, None] + jnp.arange(CMP_BLOCK)[None, :]
    blk = t[:, idx] + pos_emb[None, None, :, None, :]
    blk = blk.transpose(0, 1, 3, 2, 4).reshape(B, nc, G, CMP_BLOCK * d)
    return jax.nn.silu(blk @ w1) @ w2

def nsa_attention(q, k_cmp, v_cmp, k_slc, v_slc, k_win, v_win, gate_logits, pos,
                  pe_k, w1_k, w2_k, pe_v, w1_v, w2_v):
    B, S = q.shape[:2]
    G, H, d = N_KV_GROUPS, HEADS_PER_GROUP, HEAD_DIM
    scale = d ** -0.5
    t_idx = jnp.arange(S)
    qg = rope(q, pos).reshape(B, S, G, H, d)
    k_cmp, k_slc, k_win = rope(k_cmp, pos), rope(k_slc, pos), rope(k_win, pos)

    kc = compress_blocks(k_cmp, pe_k, w1_k, w2_k)
    vc = compress_blocks(v_cmp, pe_v, w1_v, w2_v)
    nc = kc.shape[1]
    c_start = jnp.arange(nc) * CMP_STRIDE
    c_mask = (c_start + CMP_BLOCK - 1)[None, :] <= t_idx[:, None]
    s_c = jnp.einsum('bsghd,bcgd->bghsc', qg, kc) * scale
    p_c = masked_softmax(s_c, c_mask)
    o_cmp = jnp.einsum('bghsc,bcgd->bsghd', p_c, vc.astype(jnp.float32))

    nsel = S // SEL_BLOCK
    n_top = min(N_SEL, nsel)
    j_start = jnp.arange(nsel) * SEL_BLOCK
    overlap = ((c_start[:, None] < j_start[None, :] + SEL_BLOCK)
               & (c_start[:, None] + CMP_BLOCK > j_start[None, :])).astype(jnp.float32)
    imp = jnp.einsum('bghsc,cj->bgsj', p_c, overlap)
    cur = (t_idx // SEL_BLOCK)[:, None]
    jj = jnp.arange(nsel)[None, :]
    forced = (jj == 0) | (jj == cur) | (jj == cur - 1)
    imp = jnp.where(jj <= cur, imp + jnp.where(forced, FORCE_BONUS, 0.0), -jnp.inf)
    _, sel_idx = lax.top_k(imp, n_top)

    kb = k_slc.reshape(B, nsel, SEL_BLOCK, G, d).transpose(0, 3, 1, 2, 4)
    vb = v_slc.reshape(B, nsel, SEL_BLOCK, G, d).transpose(0, 3, 1, 2, 4)
    kw = jnp.pad(k_win, ((0, 0), (WINDOW, 0), (0, 0), (0, 0)))
    vw = jnp.pad(v_win, ((0, 0), (WINDOW, 0), (0, 0), (0, 0)))
    b_ix = jnp.arange(B)[:, None, None, None]
    g_ix = jnp.arange(G)[None, :, None, None]
    in_blk = jnp.arange(SEL_BLOCK)
    w_off = jnp.arange(Q_BLOCK + WINDOW) - WINDOW

    def query_block(q0):
        tq = q0 + jnp.arange(Q_BLOCK)
        qb = lax.dynamic_slice_in_dim(qg, q0, Q_BLOCK, axis=1)
        ib = lax.dynamic_slice_in_dim(sel_idx, q0, Q_BLOCK, axis=2)
        ks = kb[b_ix, g_ix, ib]
        vs = vb[b_ix, g_ix, ib]
        s_s = jnp.einsum('bqghd,bgqnkd->bghqnk', qb, ks) * scale
        kpos = ib[..., None] * SEL_BLOCK + in_blk
        m_s = (kpos <= tq[None, None, :, None, None]).reshape(B, G, 1, Q_BLOCK, -1)
        p_s = masked_softmax(s_s.reshape(B, G, H, Q_BLOCK, -1), m_s).reshape(s_s.shape)
        o_s = jnp.einsum('bghqnk,bgqnkd->bqghd', p_s, vs.astype(jnp.float32))
        kwb = lax.dynamic_slice_in_dim(kw, q0, Q_BLOCK + WINDOW, axis=1)
        vwb = lax.dynamic_slice_in_dim(vw, q0, Q_BLOCK + WINDOW, axis=1)
        kpos_w = q0 + w_off
        dist = tq[:, None] - kpos_w[None, :]
        m_w = (dist >= 0) & (dist < WINDOW) & (kpos_w[None, :] >= 0)
        s_w = jnp.einsum('bqghd,bkgd->bghqk', qb, kwb) * scale
        p_w = masked_softmax(s_w, m_w)
        o_w = jnp.einsum('bghqk,bkgd->bqghd', p_w, vwb.astype(jnp.float32))
        return o_s, o_w

    o_s, o_w = lax.map(query_block, jnp.arange(S // Q_BLOCK) * Q_BLOCK)
    o_s = o_s.transpose(1, 0, 2, 3, 4, 5).reshape(B, S, G, H, d)
    o_w = o_w.transpose(1, 0, 2, 3, 4, 5).reshape(B, S, G, H, d)
    gt = jax.nn.sigmoid(gate_logits.astype(jnp.float32)).reshape(B, S, G, H, 3)
    o = gt[..., 0:1] * o_cmp + gt[..., 1:2] * o_s + gt[..., 2:3] * o_w
    return o.reshape(B, S, ATT_WIDTH).astype(q.dtype)

def hgrn2(q, f_logit, i, g, lb, g_norm):
    B, S, H, dk = q.shape
    nch = S // HGRN_CHUNK
    lb = lb.astype(jnp.float32).reshape(H, dk)
    f = lb + (1.0 - lb) * jax.nn.sigmoid(f_logit.astype(jnp.float32))
    log_f = jnp.log(f)
    k = 1.0 - f
    qf = jax.nn.silu(q.astype(jnp.float32))
    v = i.astype(jnp.float32)

    def to_chunks(t):
        return t.reshape(B, nch, HGRN_CHUNK, H, -1).transpose(1, 0, 3, 2, 4)

    causal = jnp.tril(jnp.ones((HGRN_CHUNK, HGRN_CHUNK), dtype=bool))

    def step(state, inp):
        qc, kc, vc, lc = inp
        bcum = jnp.cumsum(lc, axis=2)
        rel = jnp.where(causal[:, :, None], bcum[:, :, :, None, :] - bcum[:, :, None, :, :], -jnp.inf)
        a = jnp.einsum('bhid,bhjd,bhijd->bhij', qc, kc, jnp.exp(rel))
        o = (jnp.einsum('bhij,bhje->bhie', a, vc)
             + jnp.einsum('bhid,bhde->bhie', qc * jnp.exp(bcum), state))
        blast = bcum[:, :, -1:, :]
        state = (jnp.exp(blast[:, :, 0, :, None]) * state
                 + jnp.einsum('bhjd,bhje->bhde', kc * jnp.exp(blast - bcum), vc))
        return state, o

    s0 = jnp.zeros((B, H, dk, v.shape[-1]), jnp.float32)
    _, o = lax.scan(step, s0, (to_chunks(qf), to_chunks(k), to_chunks(v), to_chunks(log_f)))
    o = o.transpose(1, 0, 3, 2, 4).reshape(B, S, H, -1)
    o = o * lax.rsqrt(jnp.mean(o * o, axis=-1, keepdims=True) + EPS) * g_norm.astype(jnp.float32).reshape(H, -1)
    o = o * jax.nn.silu(g.astype(jnp.float32))
    return o.reshape(B, S, HGRN_WIDTH).astype(q.dtype)

def hybrid_mixer(h, pos, w_in, w_out, pe_k, w1_k, w2_k, pe_v, w1_v, w2_v, lb, g_norm):
    B, S, _ = h.shape
    proj = h @ w_in
    sizes = [ATT_WIDTH] + [KV_WIDTH] * 6 + [3 * N_ATT_HEADS] + [HGRN_WIDTH] * 4
    cuts = [int(v) for v in np.cumsum(sizes)[:-1]]
    parts = jnp.split(proj, cuts, axis=-1)
    q = parts[0].reshape(B, S, N_ATT_HEADS, HEAD_DIM)
    k_c, v_c, k_s, v_s, k_w, v_w = [p.reshape(B, S, N_KV_GROUPS, HEAD_DIM) for p in parts[1:7]]
    gate_logits = parts[7].reshape(B, S, N_ATT_HEADS, 3)
    hq, hf, hi, hg = [p.reshape(B, S, N_HGRN_HEADS, HGRN_HEAD_DIM) for p in parts[8:]]
    o_att = nsa_attention(q, k_c, v_c, k_s, v_s, k_w, v_w, gate_logits, pos,
                          pe_k, w1_k, w2_k, pe_v, w1_v, w2_v)
    o_rec = hgrn2(hq, hf, hi, hg, lb, g_norm)
    return jnp.concatenate([o_att, o_rec], axis=-1) @ w_out

def hier_moe(h, w_group, b_group, w_router, b_router, w_gate, w_up, w_down):
    B, S, D = h.shape
    T = B * S
    ht = h.reshape(T, D)
    lg = (ht @ w_group + b_group).astype(jnp.float32)
    pg = jax.nn.softmax(lg, axis=-1)
    _, gsel = lax.top_k(lg, 1)
    pg_sel = jnp.take_along_axis(pg, gsel, axis=-1)
    le = (ht @ w_router + b_router).astype(jnp.float32).reshape(T, N_EXPERT_GROUPS, EXPERTS_PER_GROUP)
    le_sel = jnp.take_along_axis(le, gsel[:, :, None], axis=1)[:, 0]
    pe = jax.nn.softmax(le_sel, axis=-1)
    topv, topi = lax.top_k(pe, EXPERT_TOP_K)
    topv = topv / jnp.sum(topv, axis=-1, keepdims=True)
    w_in_grp = jnp.sum(jax.nn.one_hot(topi, EXPERTS_PER_GROUP, dtype=jnp.float32) * topv[..., None], axis=1)
    cw = (jax.nn.one_hot(gsel[:, 0], N_EXPERT_GROUPS, dtype=jnp.float32)[:, :, None]
          * (w_in_grp * pg_sel)[:, None, :])
    y = jnp.zeros((T, D), jnp.float32)
    for gi in range(N_EXPERT_GROUPS):
        hid = (jax.nn.silu(jnp.einsum('td,edf->tef', ht, w_gate[gi]))
               * jnp.einsum('td,edf->tef', ht, w_up[gi]))
        y = y + jnp.einsum('tef,efd->td', hid * cw[:, gi, :, None], w_down[gi])
    return y.reshape(B, S, D).astype(h.dtype)

def setup_inputs(seed: int = 0) -> dict:
    key = jax.random.key(seed)
    ks = jax.random.split(key, 32)
    f32 = jnp.float32

    def nrm(k, shape, scale):
        return jax.random.normal(k, shape, f32) * scale

    L, D = DEPTH, D_MODEL
    offset = jax.random.randint(ks[2], (BATCH, 1), 0, 1024, dtype=jnp.int32)
    return {
        'x': nrm(ks[0], (BATCH, SEQ, D), 1.0),
        'c': nrm(ks[1], (BATCH, D), 1.0),
        'positions': offset + jnp.arange(SEQ, dtype=jnp.int32)[None, :],
        'w_ada': nrm(ks[3], (L, D, 6 * D), 0.5 * D ** -0.5),
        'b_ada': nrm(ks[4], (L, 6 * D), 0.02),
        'g_pre_mix': 1.0 + nrm(ks[5], (L, D), 0.05),
        'g_post_mix': 1.0 + nrm(ks[6], (L, D), 0.05),
        'g_pre_ffn': 1.0 + nrm(ks[7], (L, D), 0.05),
        'g_post_ffn': 1.0 + nrm(ks[8], (L, D), 0.05),
        'w_in': nrm(ks[9], (L, D, IN_COLS), D ** -0.5),
        'w_out': nrm(ks[10], (L, MIX_WIDTH, D), MIX_WIDTH ** -0.5),
        'cmp_pe_k': nrm(ks[11], (L, CMP_BLOCK, HEAD_DIM), 0.02),
        'cmp_w1_k': nrm(ks[12], (L, CMP_BLOCK * HEAD_DIM, HEAD_DIM), (CMP_BLOCK * HEAD_DIM) ** -0.5),
        'cmp_w2_k': nrm(ks[13], (L, HEAD_DIM, HEAD_DIM), HEAD_DIM ** -0.5),
        'cmp_pe_v': nrm(ks[14], (L, CMP_BLOCK, HEAD_DIM), 0.02),
        'cmp_w1_v': nrm(ks[15], (L, CMP_BLOCK * HEAD_DIM, HEAD_DIM), (CMP_BLOCK * HEAD_DIM) ** -0.5),
        'cmp_w2_v': nrm(ks[16], (L, HEAD_DIM, HEAD_DIM), HEAD_DIM ** -0.5),
        'hgrn_lb_logits': nrm(ks[17], (L + 1, HGRN_WIDTH), 0.5),
        'hgrn_g_norm': 1.0 + nrm(ks[18], (L, HGRN_WIDTH), 0.05),
        'w_group': nrm(ks[19], (L, D, N_EXPERT_GROUPS), D ** -0.5),
        'b_group': nrm(ks[20], (L, N_EXPERT_GROUPS), 0.01),
        'w_router': nrm(ks[21], (L, D, N_EXPERTS), D ** -0.5),
        'b_router': nrm(ks[22], (L, N_EXPERTS), 0.01),
        'w_gate': nrm(ks[23], (L, N_EXPERT_GROUPS, EXPERTS_PER_GROUP, D, D_EXPERT), D ** -0.5),
        'w_up': nrm(ks[24], (L, N_EXPERT_GROUPS, EXPERTS_PER_GROUP, D, D_EXPERT), D ** -0.5),
        'w_down': nrm(ks[25], (L, N_EXPERT_GROUPS, EXPERTS_PER_GROUP, D_EXPERT, D), D_EXPERT ** -0.5),
    }

def reference(x, c, positions, w_ada, b_ada, g_pre_mix, g_post_mix, g_pre_ffn, g_post_ffn,
              w_in, w_out, cmp_pe_k, cmp_w1_k, cmp_w2_k, cmp_pe_v, cmp_w1_v, cmp_w2_v,
              hgrn_lb_logits, hgrn_g_norm, w_group, b_group, w_router, b_router,
              w_gate, w_up, w_down):
    lb_table = jnp.cumsum(jax.nn.softmax(hgrn_lb_logits.astype(jnp.float32), axis=0), axis=0)
    for l in range(DEPTH):
        mod = (jax.nn.silu(c) @ w_ada[l] + b_ada[l])[:, None, :]
        sh1, sc1, gt1, sh2, sc2, gt2 = jnp.split(mod, 6, axis=-1)
        h = rmsnorm(x, g_pre_mix[l]) * (1.0 + sc1) + sh1
        y = hybrid_mixer(h, positions, w_in[l], w_out[l], cmp_pe_k[l], cmp_w1_k[l], cmp_w2_k[l],
                         cmp_pe_v[l], cmp_w1_v[l], cmp_w2_v[l], lb_table[l], hgrn_g_norm[l])
        x = x + gt1 * rmsnorm(y, g_post_mix[l])
        h = rmsnorm(x, g_pre_ffn[l]) * (1.0 + sc2) + sh2
        y = hier_moe(h, w_group[l], b_group[l], w_router[l], b_router[l], w_gate[l], w_up[l], w_down[l])
        x = x + gt2 * rmsnorm(y, g_post_ffn[l])
    return x


_drawn_inputs = setup_inputs


def setup_inputs(seed=0):
    import zlib

    import numpy as np

    out = dict(_drawn_inputs(seed))
    spreads = {}
    factors = {'g_post_ffn': 3.885,
     'cmp_pe_k': 64.0,
     'cmp_pe_v': 8.0,
     'b_group': 3.158,
     'b_router': 6.414}
    for name, (base, spread) in spreads.items():
        noise = np.random.default_rng([zlib.crc32(name.encode()), seed]).standard_normal(out[name].shape)
        drawn = base * np.exp(spread * noise) if base else spread * noise
        out[name] = jnp.asarray(drawn.astype(out[name].dtype))
    for name, factor in factors.items():
        out[name] = (out[name] * factor).astype(out[name].dtype)
    return out
```

```python
from contextlib import ExitStack

import numpy as np

import concourse.bass as bass
from concourse import mybir

ALU = mybir.AluOpType
ACT = mybir.ActivationFunctionType
AX = mybir.AxisListType.X
F32 = mybir.dt.float32
I32 = mybir.dt.int32
U32 = mybir.dt.uint32

P = 128
D = 2048
S = 256
TT = S // P
KT = D // P
NH = 8
HD = 128
KVG = 2
BLK = 512
NC_CMP = 15
CMP_LEN, CMP_STRIDE = 32, 16
NGRP, EPG = 4, 8
NE = NGRP * EPG
FE = 512
CAP = 64
EPS = 1e-6
SCALE = float(HD) ** -0.5
NEG = -1.0e30
TWO_PI_HI, TWO_PI_MID, TWO_PI_LO = 6.28125, 0.0019350051879882812, 3.019916050561733e-07
PI_SAFE = 3.1415925

HB = 6
ADA_BLOCKS = 6 * D // BLK
COL_V_SLC, COL_HQ, COL_HI = 1792, 2584, 4632
COL_GATES = 2560
N_GATES = 3 * NH
TQ, TKC, TVC, THQ, THF, TKS, TKW = 0, 8, 10, 12, 20, 28, 30
LEVELS = [128, 64, 32, 16, 8, 4, 2, 1]

C_ID, C_NEG, C_ROT, C_UP, C_LEV, C_CNEG, C_C01, C_IOTA, C_SUM, C_INVF = 0, 128, 256, 384, 512, 704, 736, 768, 832, 992
C_COLS = 993
V_C, V_BADA, V_GPRE1 = 0, 16, 112
V_GPRE2, V_GPOST1, V_LB0, V_LB1, V_PEK, V_PEV = 0, 16, 48, 56, 64, 96


def constant_table():
    t = np.zeros((P, C_COLS), np.float32)
    r = np.arange(P)
    t[:, C_ID:C_ID + P] = np.eye(P)
    t[:, C_NEG:C_NEG + P] = np.where(r[None, :] > r[:, None], NEG, 0.0)
    rot = np.zeros((P, P), np.float32)
    rot[r[64:], r[:64]] = -1.0
    rot[r[:64], r[64:]] = 1.0
    t[:, C_ROT:C_ROT + P] = rot
    t[:, C_UP:C_UP + P] = r[:, None] < r[None, :]
    j, i = (r % 32)[:, None], np.arange(32)[None, :]
    for n, s in enumerate([16, 8, 4, 2, 1]):
        t[:, C_LEV + 32 * n:C_LEV + 32 * n + 32] = (
            (j // (2 * s) == i // (2 * s)) & (j % (2 * s) < s) & (i % (2 * s) >= s))
    t[:, C_LEV + 160:C_LEV + 192] = i == j
    for tt in range(TT):
        tok = tt * P + r[:, None]
        c = np.arange(16)[None, :]
        seen = (c < NC_CMP) & (c * CMP_STRIDE + CMP_LEN - 1 <= tok)
        t[:, C_CNEG + 16 * tt:C_CNEG + 16 * tt + 16] = np.where(seen, 0.0, NEG)
        t[:, C_C01 + 16 * tt:C_C01 + 16 * tt + 16] = seen
    t[:, C_IOTA:C_IOTA + 64] = np.arange(64)[None, :]
    t[:, C_SUM:C_SUM + 160] = (r % 32)[:, None] == (np.arange(160) % 32)[None, :]
    inv = (np.float32(10000.0) ** (-np.arange(0, HD, 2, dtype=np.float32) / np.float32(HD))).astype(np.float32)
    t[:, C_INVF] = np.concatenate([inv, inv])
    return t


STAGES = {
    "tensor_stages": ["vectors_T", "gates_mm", "gates_T", "cmp_out", "gains_T", "cmp_scores", "pcT", "rec", "logits_mm",
                      "logits_T", "ranks", "over_sum"],
    "scalar_stages": ["silc_ready", "x_sd", "lb_exp", "trig", "h_ready_act", "gates_sig", "cmp_silu", "pc_exp", "forget_sig",
                      "q_and_g_silu", "forget_log", "rec_squares", "rec_sd", "y_squares", "y_sd", "x2_sd", "h2_ready_act",
                      "route_exp", "ysum_sd"],
    "vector_stages": ["vec_ready", "x_var", "xn_ready", "angles", "lb_logits", "aff1_ready", "h_ready_dve", "gates_ready",
                      "kc_ready", "vc_ready", "aff2_ready", "gains_ready", "gains_T_copied", "pc_shifted", "pc_ready",
                      "pcT_copied", "forget_ready", "decay_ready", "rec_var", "y_var", "x2_var", "xn2_ready", "h2_ready_dve",
                      "zeros_ready", "logits_biased", "group_shift", "chosen", "idx_ready", "over_counted", "over_read",
                      "combined", "ysum_var", "out0", "out1"],
    "gpsimd_stages": ["silc_zero", "ones_ready", "at_zero"],
}
STAGE_OF = {name: (sem, n + 1) for sem, names in STAGES.items() for n, name in enumerate(names)}


class Signal:

    def __init__(self, sem):
        self.sem = sem
        self.n = 0


class Lane:

    def __init__(self, eng, own):
        self.eng = eng
        self.own = own
        self.last = None

    def do(self, ins, sig=None):
        sig = sig or self.own
        ins.then_inc(sig.sem, 1)
        sig.n = sig.n + 1
        self.last = (sig, sig.n)

    def settle(self):
        sig, n = self.last
        self.eng.wait_ge(sig.sem, n)

    def begin_loop(self, i, per):
        self.bases = {s: s.n for s in per}
        self.per = per
        self.i = i
        for s in per:
            s.n = s.n + i * per[s]
        self.starts = {s: s.n for s in per}
        self.last = None

    def end_loop(self, iters):
        for s, k in self.per.items():
            s.n = self.bases[s] + iters * k
        self.last = (self.own, self.own.n)


def block_kernel(nc, a, out):
    y_rows = nc.dram_tensor("expert_rows", [NE * CAP + 1, D], F32, kind="Internal").ap()
    gain_rows = nc.dram_tensor("gain_rows", [2 * KT, P], F32, kind="Internal").ap()

    with ExitStack() as ctx:
        def sb(name, shape, dt=F32):
            return ctx.enter_context(nc.sbuf_tensor(name, shape, dt))

        sems = {}

        def sig(name):
            if name in STAGE_OF:
                stages, n = STAGE_OF[name]
                counted = sig(stages)
                assert counted.n == n - 1, name
                return counted
            if name not in sems:
                sems[name] = Signal(ctx.enter_context(nc.semaphore(name)))
            return sems[name]

        def wait(eng, name, n=1):
            if name in STAGE_OF:
                name, n = STAGE_OF[name]
            eng.wait_ge(sig(name).sem, n)

        def inc(ins, name):
            counted = sig(name)
            ins.then_inc(counted.sem, 1)
            counted.n = counted.n + 1

        ring = sb("ring", [P, HB, 8, BLK])
        RX = sb("RX", [P, 4096])
        RH = sb("RH", [P, 4096])
        RT = sb("RT", [P, 32, 256])
        RN = sb("RN", [P, 5120])
        RG = sb("RG", [P, 2, D])
        cst = sb("cst", [P, C_COLS])
        vec = sb("vec", [P, 2, P])
        vrow = RN[:, 0:256].rearrange("p (a b) -> p a b", a=2)
        silc = sb("silc", [P, KT, 32])
        part = sb("part", [P, BLK])
        mod = sb("mod", [P, 6 * KT])
        ones = sb("ones", [P, P])
        st = sb("st", [P, 64])
        gts = sb("gts", [P, TT, N_GATES])
        aff = sb("aff", [P, 4, KT])
        lbc = sb("lbc", [P, 4, NH])
        brt = sb("brt", [36, 1])
        rti = sb("rti", [P, 16], U32)
        cwo = sb("cwo", [P, TT, NE])
        wk = sb("wk", [P, TT, 2])
        idx = sb("idx", [P, 2 * TT], I32)
        flag = sb("flag", [P, 1], I32)

        x_t = RX[:, :].rearrange("p (t d) -> p t d", t=TT)
        hT = RH[:, :].rearrange("p (k t) -> p k t", k=KT)
        ident = cst[:, C_ID:C_ID + P]
        cosT, sinT = RX[:, 3584:3840], RX[:, 3840:4096]
        wrt = RN[:, 0:576].rearrange("p (k c) -> p k c", k=KT)
        wg24 = RG[:, 0, 1024:1408].rearrange("p (k c) -> p k c", k=KT)
        silf = silc[:, :, :].rearrange("p k c -> p (k c)")
        rt = silf[:, 0:256]
        onehots = silf[:, 256:384].rearrange("p (t k e) -> p t k e", t=TT, k=2)
        sel = silf[:, 384:448].rearrange("p (t e) -> p t e", t=TT)
        rank = silf[:, 448:512].rearrange("p (t e) -> p t e", t=TT)
        vtok = RN[:, 0:1024].rearrange("p (b t c) -> p b t c", b=2, t=TT)
        probs = RX[:, 0:1536].rearrange("p (r b c) -> p r b c", r=2, b=2)
        probsT = RX[:, 1536:3072].rearrange("p (r b c) -> p r b c", r=2, b=2)
        pcT = RX[:, 3072:3584].rearrange("p (g t) -> p g t", g=KVG)
        pcp = RX[:, 3584:4096].rearrange("p (t c) -> p t c", t=TT)
        w2 = RG[:, 1, 1024:1280].rearrange("p (v o) -> p v o", v=2)
        cmph = RG[:, 1, 1280:1600].rearrange("p (v o) -> p v o", v=2)
        vc4 = RG[:, 1, 1600:1856].rearrange("p (g o) -> p g o", g=KVG)
        kcT = RG[:, 1, 1856:1888].rearrange("p (g c) -> p g c", g=KVG)
        gcol = RG[:, 1, 1888:1920]
        gnorm = RG[:, 1, 0:1024]
        htok = RN[:, 1024:5120].rearrange("p (i t c) -> p i t c", i=4, t=TT)
        kT = RG[:, 0, :].rearrange("p (h t) -> p h t", h=NH)
        zf = RH[:, :].rearrange("p (r c) -> p r c", r=2)
        at = RX[:, 0:3072].rearrange("p (h c) -> p h c", h=NH)
        acc = RX[:, 3072:3584]
        acc_new = RX[:, 3584:4096]
        orec = RH[:, 0:2048].rearrange("p (t c) -> p t c", t=TT)
        scratch = RH[:, 2048:4096]
        y = RH[:, :].rearrange("p (t d) -> p t d", t=TT)
        xn2 = y
        h2T = RT[:, 0:KT, :]
        ysum = RT[:, KT:2 * KT, :].rearrange("p a b -> p (a b)").rearrange("p (t d) -> p t d", t=TT)
        tokT = RN[:, 0:2048].rearrange("p (k s) -> p k s", k=KT)
        onehot = RN[:, 2048:2304].rearrange("p (t s) -> p t s", t=TT)
        hid = RN[:, 2304:2816]
        sil = RN[:, 2816:3328]
        hidT = RN[:, 3328:3584]
        rows = RN[:, 3584:4608]
        dhid, dsil, dhidT = hid, sil, RN[:, 0:512]
        GB = [4, 5, 6]
        posi = RG[:, 0, 3 * S:4 * S].bitcast(I32)

        def gat(n):
            return ring[:, n, :, :].rearrange("p a b -> p (a b)")[:, 0:D]

        bank = [ctx.enter_context(nc.psum_tensor(f"bank{i}", [P, BLK], F32)) for i in range(8)]

        block = ctx.enter_context(nc.Block())

        def cols(w, c0, n=BLK):
            v = w.rearrange("(k p) c -> p k c", p=P)
            return [v[:, 0:8, bass.ds(c0, n)], v[:, 8:16, bass.ds(c0, n)]]

        def half(s):
            return ring[:, s, :, :]

        @block.sync
        def _(sp):
            def turn(t, halves):
                for s, src in enumerate(halves):
                    if src is None:
                        continue
                    if not (isinstance(t, int) and t == 0):
                        wait(sp, "ring_used", HB * (t - 1) + s + 1)
                    dst = half(s)
                    if src.shape[1] == CMP_LEN:
                        dst = ring[:, s, :, :].rearrange("p a b -> p (a b)").rearrange("p (a b) -> p a b", a=CMP_LEN)
                    sp.dma_start(dst, src).then_inc(sig(f"landed{s}").sem, 16)

            ada, win, wout = a["w_ada"], a["w_in"], a["w_out"]

            def w1(w):
                return w.rearrange("(q p) o -> p q o", p=P)

            turn(0, cols(ada, 0) + cols(ada, BLK) + cols(ada, 2 * BLK))
            with sp.Fori(1, 3) as t:
                turn(t, cols(ada, t * (3 * BLK)) + cols(ada, t * (3 * BLK) + BLK) + cols(ada, t * (3 * BLK) + 2 * BLK))
            with sp.Fori(0, 3) as i:
                turn(i + 3, cols(ada, i * (2 * BLK) + 9 * BLK) + cols(win, i * BLK) + cols(ada, i * (2 * BLK) + 10 * BLK))
            turn(6, cols(ada, 15 * BLK) + cols(win, 3 * BLK) + cols(win, 4 * BLK))
            with sp.Fori(0, 4) as i:
                turn(i + 7, cols(ada, i * BLK + 16 * BLK) + cols(win, i * BLK + COL_HQ) + cols(win, i * BLK + COL_HI))
            turn(11, [w1(a["cmp_w1_k"]), w1(a["cmp_w1_v"])] + cols(ada, 20 * BLK) + cols(ada, 21 * BLK))
            turn(12, cols(ada, 22 * BLK) + cols(ada, 23 * BLK) + cols(wout, 0))
            turn(13, cols(wout, BLK) + cols(wout, 2 * BLK) + cols(wout, 3 * BLK))

            wg = a["w_gate"].rearrange("e (k p) c -> e p k c", p=P)
            wu = a["w_up"].rearrange("e (k p) c -> e p k c", p=P)
            wd = a["w_down"].rearrange("e (k p) c -> e p k c", p=P)

            def expert_halves(e):
                g, u, d = (w[bass.ds(e, 1)].rearrange("o p k c -> p (o k) c") for w in (wg, wu, wd))
                return [g[:, 0:8, :], u[:, 0:8, :], g[:, 8:16, :], u[:, 8:16, :], d[:, 0:2, :], d[:, 2:4, :]]

            def dst_of(s):
                return half(s) if s < 4 else ring[:, s, :, :].rearrange("p (k a) b -> p k (a b)", k=2)

            for s, src in enumerate(expert_halves(0)):
                wait(sp, "ring_used", HB * 13 + s + 1)
                sp.dma_start(dst_of(s), src).then_inc(sig(f"expert_landed{s}").sem, 16)
            with sp.Fori(1, NE) as e:
                for s, src in enumerate(expert_halves(e)):
                    wait(sp, "expert_used", (e - 1) * HB + (s + 1))
                    sp.dma_start(dst_of(s), src).then_inc(sig(f"expert_landed{s}").sem, 16)

            wait(sp, "flag_ready")
            over = nc.sync.value_load(flag[0:1, 0:1], min_val=0, max_val=2 * S)
            wait(sp, "expert_used", NE * HB)
            with sp.If(over > 0):
                wait(sp, "combined")
                with sp.Fori(0, NE) as e:
                    sp.wait_ge(sig("dense_used").sem, e + 1)
                    for s, src in enumerate(expert_halves(e)):
                        sp.dma_start(dst_of(s), src).then_inc(sig(f"dense_landed{s}").sem, 16)
                    for s in range(HB):
                        sp.wait_ge(sig(f"dense_landed{s}").sem, e * 16 + 16)
                    sp.sem_inc(sig("dense_here").sem, 1)
            with sp.Else():
                wait(sp, "combined")
            wait(sp, "out0")
            sp.dma_start(out[0:P, :], x_t[:, 0, :]).then_inc(sig("stored").sem, 16)
            wait(sp, "out1")
            sp.dma_start(out[P:S, :], x_t[:, 1, :]).then_inc(sig("stored").sem, 16)
            wait(sp, "stored", 32)

        @block.tensor
        def _(pe):
            mm = nc.tensor.matmul
            tr = nc.tensor.transpose

            def landed(s, t):
                pe.wait_ge(sig(f"landed{s}").sem, t * 16 + 16)

            def used(ins):
                ins.then_inc(sig("ring_used").sem, 1)

            wait(pe, "consts_in", 16)
            wait(pe, "vectors_in", 16 * 10)
            for v in range(2):
                last = tr(bank[0][:, v * P:(v + 1) * P], vrow[:, v, :], ident)
            inc(last, "vectors_T")

            def transpose_tokens(ready, src, tag):
                wait(pe, ready)
                for m in range(8):
                    if m >= 4:
                        wait(pe, f"{tag}_copied{m % 2}", (m - 4) // 2 + 1)
                    for j in range(4):
                        k, tt = 2 * m + j // 2, j % 2
                        last = tr(bank[1 + m % 4][:, j * P:(j + 1) * P], src[:, tt, k * P:(k + 1) * P], ident)
                    last.then_inc(sig(f"{tag}_T").sem, 1)

            transpose_tokens("xn_ready", x_t, "x1")
            wait(pe, "vec_ready")

            def ada_sum(t, slot, n):
                pe.wait_ge(sig("part_copied").sem, n) if not isinstance(n, int) or n > 0 else None
                for r in range(4):
                    if r % 2 == 0:
                        landed(2 * slot + r // 2, t)
                    for j in range(4):
                        k = 4 * r + j
                        last = mm(bank[0][32 * j:32 * j + 32, :], silc[:, k, :], ring[:, 2 * slot + k // 8, k % 8, :],
                                  start=r == 0, stop=r == 3, skip_group_check=True)
                    if r == 1:
                        used(last)
                used(last)

            def ada_cols(n):
                pe.wait_ge(sig("part_copied").sem, n + 1)
                if not isinstance(n, int) or n > 0:
                    pe.wait_ge(sig("mod_copied").sem, n)
                for j in range(4):
                    last = mm(bank[7][:, j * P:(j + 1) * P], part[:, j * P:(j + 1) * P], ones[:, :], start=True, stop=True)
                last.then_inc(sig("mod_cols").sem, 1)

            wait(pe, "silc_ready")
            wait(pe, "ones_ready")
            for slot in range(3):
                ada_sum(0, slot, slot)
                ada_cols(slot)
            with pe.Fori(1, 3) as t:
                for slot in range(3):
                    ada_sum(t, slot, t * 3 + slot)
                    ada_cols(t * 3 + slot)

            wait(pe, "h_ready_act")
            wait(pe, "h_ready_dve")

            def fill_feature_tile(s0, t, c, b, n, release):
                pe.wait_ge(sig(f"taken{b}").sem, n + 1)
                for k in range(KT):
                    if k % 8 == 0:
                        landed(s0 + k // 8, t)
                    last = mm(bank[b][:, 0:S], ring[:, s0 + k // 8, k % 8, c:c + P], hT[:, k, :], start=k == 0, stop=k == KT - 1)
                    if release and k == 7:
                        used(last)
                if not release:
                    last.then_inc(sig(f"full{b}").sem, 1)
                else:
                    used(last)

            def fill_token_tile(s0, t, c, w, tt, b, n, release, src, full=None):
                if n is not None:
                    pe.wait_ge(sig(f"taken{b}").sem, n + 1)
                for k in range(KT):
                    if k % 8 == 0:
                        landed(s0 + k // 8, t)
                    last = mm(bank[b][:, 0:w], src(k)[:, tt * P:(tt + 1) * P], ring[:, s0 + k // 8, k % 8, c:c + w],
                              start=k == 0, stop=k == KT - 1)
                    if release and k == 7:
                        used(last)
                if not release:
                    last.then_inc(sig(full or f"full{b}").sem, 1)
                else:
                    used(last)

            def h_tile(k):
                return hT[:, k, :]

            def feature_block(s0, t, n):
                for m in range(4):
                    fill_feature_tile(s0, t, m * P, 1 + m, n, m == 3)

            with pe.Fori(0, 3) as i:
                t = i + 3
                ada_sum(t, 0, i * 2 + 9)
                feature_block(2, t, i)
                ada_cols(i * 2 + 9)
                ada_sum(t, 2, i * 2 + 10)
                ada_cols(i * 2 + 10)
            ada_sum(6, 0, 15)
            for b2 in range(2):
                for m in range(4):
                    if m < 2:
                        fill_feature_tile(2 + 2 * b2, 6, m * P, 1 + m, 3 + b2, False)
                    else:
                        fill_token_tile(2 + 2 * b2, 6, 2 * P, 2 * P, m - 2, 1 + m, 3 + b2, m == 3, h_tile)
                if b2 == 0:
                    ada_cols(15)
            with pe.Fori(0, 4) as i:
                t = i + 7
                ada_sum(t, 0, i + 16)
                feature_block(2, t, i + 5)
                ada_cols(i + 16)
                for tt in range(TT):
                    fill_token_tile(4, t, 0, BLK, tt, 5 + tt, i, tt == 1, h_tile)

            wait(pe, "taken1", 10)
            wait(pe, "taken2", 10)
            wait(pe, "small_w_in", 16)
            for k in range(KT):
                last = mm(bank[1][0:N_GATES, 0:S], wg24[:, k, :], hT[:, k, :], start=k == 0, stop=k == KT - 1)
            inc(last, "gates_mm")
            wait(pe, "gates_sig")
            for tt in range(TT):
                last = tr(bank[2][:, tt * 32:tt * 32 + N_GATES], part[0:N_GATES, tt * P:(tt + 1) * P], ident[0:N_GATES, 0:N_GATES])
            inc(last, "gates_T")

            for n in range(7):
                c0 = 2 * n if n < 5 else TKS + 2 * (n - 5)
                if n >= 2:
                    wait(pe, "roped_mul", n - 1)
                else:
                    wait(pe, f"taken{3 + n}", 10)
                last = mm(bank[3 + n % 2][:, :], cst[:, C_ROT:C_ROT + P], RT[:, c0:c0 + 2, :], start=True, stop=True)
                last.then_inc(sig("swapped").sem, 1)

            wait(pe, "taken5", 5)
            wait(pe, "taken6", 5)
            for v in range(2):
                landed(v, 11)
                wait(pe, "blocks_ready", v + 1)
                blkv = RX[:, v * 1024:(v + 1) * 1024].rearrange("p (q c) -> p q c", q=CMP_LEN)
                w1v = ring[:, v, :, :].rearrange("p a b -> p (a b)").rearrange("p (q o) -> p q o", q=CMP_LEN)
                for r in range(8):
                    for j in range(4):
                        q = 4 * r + j
                        last = mm(bank[5 + v][32 * j:32 * j + 32, 0:P], blkv[:, q, :], w1v[:, q, :],
                                  start=r == 0, stop=r == 7, skip_group_check=True)
                used(last)
            for v in range(2):
                wait(pe, "cmp_part", v + 1)
                last = mm(bank[5 + v][:, 256:256 + 160], RX[:, 2048 + v * P:2048 + (v + 1) * P], cst[:, C_SUM:C_SUM + 160], start=True, stop=True)
                last.then_inc(sig("cmp_hid").sem, 1)
            wait(pe, "cmp_silu")
            wait(pe, "cmp_w2_in", 32)
            wait(pe, "roped_mul", 7)
            last = mm(bank[3][:, 0:P], w2[:, 0, :], cmph[:, 0, 0:P], start=True, stop=True)
            for g in range(KVG):
                last = mm(bank[4][:, g * P:(g + 1) * P], cmph[:, 1, 16 * g:16 * g + P], w2[:, 1, :], start=True, stop=True)
            inc(last, "cmp_out")

            for n, (t, slot) in enumerate([(11, 1), (11, 2), (12, 0), (12, 1)]):
                ada_sum(t, slot, 20 + n)
                ada_cols(20 + n)
            wait(pe, "gains_ready")
            last = tr(bank[1][0:2 * KT, 0:P], gcol, ident)
            inc(last, "gains_T")

            wait(pe, "roped", 7)
            wait(pe, "kc_ready")
            wait(pe, "vc_ready")
            wait(pe, "gates_ready")
            for tt in range(TT):
                for h in range(NH):
                    last = mm(bank[2][:, (tt * NH + h) * 16:(tt * NH + h + 1) * 16], RT[:, TQ + h, tt * P:(tt + 1) * P],
                              kcT[:, h // 4, 0:16], start=True, stop=True)
            inc(last, "cmp_scores")

            def scores(h):
                g = h // 4
                for br, tk in enumerate((TKS, TKW)):
                    b = 3 + 2 * (h % 2) + br
                    if h >= 2:
                        wait(pe, "exps", 2 * (h - 2) + br + 1)
                    for tt in range(TT):
                        c0, n = (0, P) if tt == 0 else (P, 2 * P)
                        mm(bank[b][:, c0:c0 + n], RT[:, TQ + h, tt * P:(tt + 1) * P], RT[:, tk + g, 0:n], start=True, stop=False)
                        last = mm(bank[b][:, c0 + n - P:c0 + n], ident, cst[:, C_NEG:C_NEG + P], start=False, stop=True)
                    last.then_inc(sig("scores").sem, 1)

            def probs_T(h):
                for br in range(2):
                    wait(pe, "probs", 2 * h + br + 1)
                    if h > 0:
                        wait(pe, f"probsT_copied{br}", h)
                    for c in range(3):
                        last = tr(bank[br + 1 if br == 0 else 7][:, c * P:(c + 1) * P], probs[:, h % 2, br, c * P:(c + 1) * P], ident)
                    last.then_inc(sig(f"probsT{br}").sem, 1)

            def values(h):
                g = h // 4
                if h >= 1:
                    wait(pe, "oT_copied", h)
                o = bank[0]
                mm(o[:, 0:S], vc4[32 * (h % 4):32 * (h % 4) + 32, g, :], pcT[32 * (h % 4):32 * (h % 4) + 32, g, :],
                   start=True, stop=False)
                for br in range(2):
                    wait(pe, f"probsT_copied{br}", h + 1)
                    v = vtok[:, br, :, g * P:(g + 1) * P]
                    mm(o[:, 0:S], v[:, 0, :], probsT[:, h % 2, br, 0:S], start=False, stop=False)
                    last = mm(o[:, P:S], v[:, 1, :], probsT[:, h % 2, br, S:S + P], start=False, stop=br == 1)
                last.then_inc(sig("oT").sem, 1)

            scores(0)
            wait(pe, "pc_ready")
            wait(pe, "gains_T_copied")
            wait(pe, "mod_copied", ADA_BLOCKS)
            for g in range(KVG):
                for tt in range(TT):
                    last = tr(bank[1][:, (2 * g + tt) * P:(2 * g + tt + 1) * P], pcp[:, tt, g * P:(g + 1) * P], ident)
            inc(last, "pcT")
            wait(pe, "pcT_copied")
            for h in range(NH):
                if h + 1 < NH:
                    scores(h + 1)
                probs_T(h)
                if h > 0:
                    values(h - 1)
            values(NH - 1)

            for n, s in enumerate(LEVELS + [0]):
                if s > 0:
                    wait(pe, "factors", n + 1)
                z = zf[:, n % 2, :].rearrange("p (h t) -> p h t", h=NH)
                if n >= 5:
                    wait(pe, "products_used", n - 1)
                if s == 128:
                    for h in range(NH):
                        last = mm(bank[1 + h // 4][:, (h % 4) * P:(h % 4 + 1) * P], z[:, h, 0:P], z[:, h, P:S], start=True, stop=True)
                elif s == 64:
                    for tt in range(TT):
                        for h in range(NH):
                            t0 = tt * P
                            last = mm(bank[3 + tt][0:64, h * 64:(h + 1) * 64], z[:, h, t0:t0 + 64], z[:, h, t0 + 64:t0 + P],
                                      start=True, stop=True)
                elif s == 32:
                    for h in range(NH):
                        for tt in range(TT):
                            for q in range(2):
                                t0 = tt * P + q * 64
                                last = mm(bank[5][64 * q:64 * q + 32, (tt * NH + h) * 32:(tt * NH + h + 1) * 32],
                                          z[:, h, t0:t0 + 32], z[:, h, t0 + 32:t0 + 64], start=True, stop=True,
                                          skip_group_check=True)
                else:
                    for h in range(NH):
                        for tt in range(TT):
                            for q in range(4):
                                t0 = tt * P + q * 32
                                kk = kT[:, h, t0:t0 + 32] if s == 0 else z[:, h, t0:t0 + 32]
                                qq = RT[:, THQ + h, t0:t0 + 32] if s == 0 else z[:, h, t0:t0 + 32]
                                last = mm(bank[6 + n % 2][32 * q:32 * q + 32, (tt * NH + h) * 32:(tt * NH + h + 1) * 32],
                                          kk, qq, start=True, stop=True, skip_group_check=True)
                last.then_inc(sig("products").sem, 1)
            wait(pe, "decay_ready")
            for tt in range(TT):
                for h in range(NH):
                    o = bank[1 + 2 * tt + h // 4][:, (h % 4) * P:(h % 4 + 1) * P]
                    for jt in range(tt + 1):
                        aT = at[:, h, tt * P:(tt + 1) * P] if jt == 0 else at[:, h, S:S + P]
                        last = mm(o, aT, htok[:, h // 4, jt, (h % 4) * P:(h % 4 + 1) * P], start=jt == 0, stop=jt == tt)
            inc(last, "rec")
            for tt in range(TT):
                for m in range(4):
                    wait(pe, "rec_gated", tt * NH + 2 * m + 2)
                    for j in range(2):
                        h = 2 * m + j
                        last = tr(bank[5 + m // 2][:, (m % 2) * 256 + j * P:(m % 2) * 256 + (j + 1) * P],
                                  orec[:, tt, h * P:(h + 1) * P], ident)
                    last.then_inc(sig("recT").sem, 1)
                if tt == 0:
                    wait(pe, "recT_copied", 2)

            wait(pe, "recT_copied", 4)

            def mixed(k):
                return RT[:, TQ + k, :] if k < NH else RT[:, THQ + k - NH, :]

            for n in range(4):
                t, s0 = (12, 4) if n == 0 else (13, 2 * (n - 1))
                for tt in range(TT):
                    b = (2 * n + tt) % 8
                    fill_token_tile(s0, t, 0, BLK, tt, b, None, tt == 1, mixed, "y_half")

            transpose_tokens("xn2_ready", xn2, "x2")
            wait(pe, "h2_ready_act")
            wait(pe, "h2_ready_dve")
            wait(pe, "router_in", 32)
            for k in range(KT):
                last = mm(bank[6][0:36, 0:S], wrt[:, k, :], h2T[:, k, :], start=k == 0, stop=k == KT - 1)
            inc(last, "logits_mm")
            wait(pe, "logits_biased")
            for tt in range(TT):
                last = tr(bank[7][:, tt * 64:tt * 64 + 36], part[0:36, tt * P:(tt + 1) * P], ident[0:36, 0:36])
            inc(last, "logits_T")
            wait(pe, "chosen")
            mm(bank[7][:, 128:160], cst[:, C_UP:C_UP + P], sel[:, 0, :], start=True, stop=True)
            mm(bank[7][:, 160:192], ones[:, :], sel[:, 0, :], start=True, stop=False)
            last = mm(bank[7][:, 160:192], cst[:, C_UP:C_UP + P], sel[:, 1, :], start=False, stop=True)
            inc(last, "ranks")
            wait(pe, "over_counted")
            inc(mm(bank[7][:, 192:193], ones[:, :], rt[:, 200:201], start=True, stop=True), "over_sum")

            def gather(n):
                pe.wait_ge(sig("onehot").sem, n)
                for m in range(4):
                    if m >= 3:
                        pe.wait_ge(sig("gathered_used").sem, (n - 1) * 4 + 1)
                    elif not isinstance(n, int):
                        pe.wait_ge(sig("gathered_used").sem, (n - 1) * 4)
                    for k in range(4 * m, 4 * m + 4):
                        for tt in range(TT):
                            last = mm(bank[GB[m % 3]][:, (k % 4) * P:(k % 4 + 1) * P], xn2[:, tt, k * P:(k + 1) * P],
                                      onehot[:, tt, :], start=tt == 0, stop=tt == TT - 1)
                    last.then_inc(sig("gathered").sem, 1)

            gather(1)
            wait(pe, "over_read")
            def pair(p, gather_next):
                for q in range(2):
                    e = p * 2 + q
                    if q == 0:
                        pe.wait_ge(sig("gathered_used").sem, p * 4 + 4)
                    for k in range(KT):
                        if k % 8 == 0:
                            for s in range(2):
                                pe.wait_ge(sig(f"expert_landed{2 * (k // 8) + s}").sem, e * 16 + 16)
                        for s in range(2):
                            last = mm(bank[0][64 * s:64 * s + 64, :], tokT[:, k, q * CAP:(q + 1) * CAP],
                                      ring[:, 2 * (k // 8) + s, k % 8, :], start=k == 0, stop=k == KT - 1, skip_group_check=True)
                            if k % 8 == 7:
                                last.then_inc(sig("expert_used").sem, 1)
                    if q == 1 and gather_next:
                        gather(p + 2)
                    pe.wait_ge(sig("hidden").sem, e + 1)
                    for f in range(4):
                        last = tr(bank[1][:, f * P:(f + 1) * P], hid[:, f * P:(f + 1) * P], ident)
                    last.then_inc(sig("hiddenT").sem, 1)
                    pe.wait_ge(sig("rows_copied").sem, e * 2 + 2)
                    pe.wait_ge(sig("hiddenT_copied").sem, e + 1)
                    for k in range(4):
                        if k % 2 == 0:
                            pe.wait_ge(sig(f"expert_landed{4 + k // 2}").sem, e * 16 + 16)
                        wdn = ring[:, 4 + k // 2, :, :].rearrange("p (k a) b -> p k (a b)", k=2)[:, k % 2, :]
                        for n in (0, 2, 1, 3):
                            last = mm(bank[2 + n % 2][64 * (n // 2):64 * (n // 2) + 64, :], hidT[:, k * CAP:(k + 1) * CAP],
                                      wdn[:, n * BLK:(n + 1) * BLK], start=k == 0, stop=k == 3, skip_group_check=True)
                        if k % 2 == 1:
                            last.then_inc(sig("expert_used").sem, 1)

            with pe.Fori(0, NE // 2 - 1) as p:
                pair(p, True)
            pair(NE // 2 - 1, False)

            wait(pe, "flag_ready")
            over = nc.tensor.value_load(flag[0:1, 0:1], min_val=0, max_val=2 * S)
            with pe.If(over > 0):
                wait(pe, "rows_copied", 2 * NE + 2)
                wait(pe, "gathered_used", 4 * (NE // 2))
                pe.sem_inc(sig("dense_used").sem, 1)
                with pe.Fori(0, NE) as e:
                    pe.wait_ge(sig("dense_here").sem, e + 1)
                    for tt in range(TT):
                        c = e * 2 + tt
                        for s in range(2):
                            for k in range(KT):
                                last = mm(bank[s][:, :], h2T[:, k, tt * P:(tt + 1) * P], ring[:, 2 * (k // 8) + s, k % 8, :],
                                          start=k == 0, stop=k == KT - 1)
                        last.then_inc(sig("dense_gu").sem, 1)
                        pe.wait_ge(sig("dense_hid").sem, c + 1)
                        for f in range(4):
                            last = tr(bank[2][:, f * P:(f + 1) * P], dhid[:, f * P:(f + 1) * P], ident)
                        last.then_inc(sig("dense_T").sem, 1)
                        pe.wait_ge(sig("dense_T_copied").sem, c + 1)
                        for n in range(4):
                            for k in range(4):
                                wdn = ring[:, 4 + k // 2, :, :].rearrange("p (k a) b -> p k (a b)", k=2)[:, k % 2, :]
                                last = mm(bank[4 + n][:, :], dhidT[:, k * P:(k + 1) * P], wdn[:, n * BLK:(n + 1) * BLK],
                                          start=k == 0, stop=k == 3)
                        last.then_inc(sig("dense_down").sem, 1)
                        pe.wait_ge(sig("dense_added").sem, c + 1)
                    pe.sem_inc(sig("dense_used").sem, 1)
            with pe.Else():
                pe.nop()
            pe.nop()

        @block.scalar
        def _(act):
            lane = Lane(act, sig("act_steps"))
            do, settle = lane.do, lane.settle
            fn = nc.scalar.activation

            act.dma_start(cst[:, :], a["consts"]).then_inc(sig("consts_in").sem, 16)
            for v, rows_ in enumerate([
                [("c", V_C), ("b_ada", V_BADA), ("g_pre_mix", V_GPRE1)],
                [("g_pre_ffn", V_GPRE2), ("g_post_mix", V_GPOST1), ("g_post_ffn", V_GPOST1 + KT), ("lb0", V_LB0),
                 ("lb1", V_LB1), ("cmp_pe_k", V_PEK), ("cmp_pe_v", V_PEV)],
            ]):
                for name, r0 in rows_:
                    src = a[name]
                    act.dma_start(vrow[r0:r0 + src.shape[0], v, :], src).then_inc(sig("vectors_in").sem, 16)
            for tt in range(TT):
                act.dma_start(x_t[:, tt, :], a["x"][tt * P:(tt + 1) * P, :]).then_inc(sig(f"x_in{tt}").sem, 16)
            act.dma_start(wg24[:, :, :], a["w_in"].rearrange("(k p) c -> p k c", p=P)[:, :, COL_GATES:COL_GATES + N_GATES])\
               .then_inc(sig("small_w_in").sem, 16)
            act.dma_start(brt[0:NGRP, :], a["b_group"]).then_inc(sig("brt_in").sem, 16)
            act.dma_start(brt[NGRP:36, :], a["b_router"]).then_inc(sig("brt_in").sem, 16)

            wait(act, "vec_ready")
            wait(act, "silc_zero")
            do(fn(silc[:, :, 0], vec[:, 0, V_C:V_C + KT], ACT.Silu), sig("silc_ready"))
            for tt in range(TT):
                wait(act, f"x_in{tt}", 16)
                do(fn(RH[:, tt * D:(tt + 1) * D], x_t[:, tt, :], ACT.Square, accum_out=st[:, tt:tt + 1]), sig("x_squares"))
            wait(act, "x_var")
            do(fn(st[:, 4:6], st[:, 2:4], ACT.Sqrt), sig("x_sd"))

            def copy_transposed(tag, dst):
                for m in range(0, 8, 2):
                    wait(act, f"{tag}_T", m + 1)
                    do(fn(dst[:, 2 * m:2 * m + 2, :], bank[1 + m % 4][:, :], ACT.Copy), sig(f"{tag}_copied0"))

            copy_transposed("x1", hT)
            wait(act, "lb_logits")
            do(fn(lbc[:, 0:2, :], lbc[:, 0:2, :], ACT.Exp), sig("lb_exp"))
            do(fn(sinT[:, :], sinT[:, :], ACT.Sin))
            do(fn(cosT[:, :], cosT[:, :], ACT.Sin), sig("trig"))

            def modulate(dst, which, ready):
                for k in (0, 1, 4, 5, 8, 9, 12, 13):
                    do(fn(dst[:, k, :], dst[:, k, :], ACT.Identity, bias=aff[:, 2 * which + 1, k:k + 1],
                          scale=aff[:, 2 * which, k:k + 1]), sig(ready) if k == 13 else None)

            wait(act, "aff1_ready")
            settle()
            modulate(hT, 0, "h_ready_act")

            for b in (1, 3, 5):
                act.sem_inc(sig(f"taken{b}").sem, 1)

            def take(b, n, dst, src):
                act.wait_ge(sig(f"full{b}").sem, n + 1)
                fn(dst, src, ACT.Copy).then_inc(sig(f"taken{b}").sem, 1)

            def feature_tiles(base, n):
                for m in (0, 2):
                    take(1 + m, n, RT[:, bass.ds(base + m, 1), :], bank[1 + m][:, 0:S])

            with act.Fori(0, 3) as i:
                feature_tiles(i * 4, i)
            for b2 in range(2):
                take(1, 3 + b2, RT[:, TKS + 2 * b2, :], bank[1][:, 0:S])
                take(3, 3 + b2, vtok[:, b2, 0, :], bank[3][:, 0:256])
            with act.Fori(0, 4) as i:
                feature_tiles(i * 4 + THQ, i + 5)
                take(5, i, htok[:, bass.ds(i, 1), 0, :], bank[5][:, :])

            wait(act, "gates_mm")
            wait(act, "mod_cols", 20)
            do(fn(part[0:N_GATES, 0:S], bank[1][0:N_GATES, 0:S], ACT.Sigmoid), sig("gates_sig"))

            wait(act, "cmp_hid", 2)
            for v in range(2):
                do(fn(cmph[:, v, :], bank[5 + v][:, 256:416], ACT.Silu), sig("cmp_silu") if v else None)
            wait(act, "pc_shifted")
            do(fn(rt[:, :], rt[:, :], ACT.Exp, scale=SCALE), sig("pc_exp"))

            def exps(h):
                for br in range(2):
                    wait(act, "maxima", h + 1)
                    if h >= 2:
                        wait(act, f"probsT{br}", h - 1)
                    b = 3 + 2 * (h % 2) + br
                    for tt in range(TT):
                        c0, n = (0, P) if tt == 0 else (P, 2 * P)
                        s0 = 24 + 12 * (h % 2) + 2 * br + tt
                        do(fn(probs[:, h % 2, br, c0:c0 + n], bank[b][:, c0:c0 + n], ACT.Exp, bias=st[:, s0:s0 + 1],
                              scale=SCALE, accum_out=st[:, s0 + 4:s0 + 5]), sig("exps") if tt else None)

            exps(0)
            for h in range(NH):
                if h + 1 < NH:
                    exps(h + 1)
                wait(act, "probsT0", h + 1)
                do(fn(probsT[:, h % 2, 0, :], bank[1][:, 0:384], ACT.Copy), sig("probsT_copied0"))
                if h > 0:
                    wait(act, "oT", h)
                    do(fn(RT[:, TQ + h - 1, :], bank[0][:, 0:S], ACT.Copy), sig("oT_copied"))
            wait(act, "oT", NH)
            do(fn(RT[:, TQ + NH - 1, :], bank[0][:, 0:S], ACT.Copy), sig("oT_copied"))

            wait(act, "taken2", 10)
            wait(act, "taken4", 10)
            fT = RT[:, THF:THF + NH, :]
            do(fn(fT, fT, ACT.Sigmoid), sig("forget_sig"))
            do(fn(RT[:, THQ:THQ + NH, :], RT[:, THQ:THQ + NH, :], ACT.Silu))
            wait(act, "taken6", 5)
            do(fn(htok[:, 2:4, :, :], htok[:, 2:4, :, :], ACT.Silu), sig("q_and_g_silu"))
            wait(act, "forget_ready")
            do(fn(fT, fT, ACT.Ln), sig("forget_log"))
            for n in range(8):
                wait(act, "spans", n + 1)
                do(fn(zf[:, n % 2, :], zf[:, n % 2, :], ACT.Exp), sig("decays"))
            wait(act, "rec")
            for tt in range(TT):
                for h in range(NH):
                    n = tt * NH + h
                    do(fn(scratch[:, n * P:(n + 1) * P], bank[1 + 2 * tt + h // 4][:, (h % 4) * P:(h % 4 + 1) * P], ACT.Square,
                          accum_out=st[:, n:n + 1]), sig("rec_squares") if n == 15 else None)
            wait(act, "rec_var")
            do(fn(st[:, 0:16], st[:, 0:16], ACT.Sqrt), sig("rec_sd"))
            for tt in range(TT):
                wait(act, "recT", 4 * tt + 2)
                do(fn(RT[:, THQ:THQ + 4, tt * P:(tt + 1) * P], bank[5][:, :].rearrange("p (h t) -> p h t", h=4), ACT.Copy),
                   sig("recT_copied"))

            for n in range(4):
                for tt in range(TT):
                    wait(act, "y_copied", 2 * n + tt + 1)
                    c0 = 1024 + (2 * n + tt) * BLK
                    do(fn(RN[:, c0:c0 + BLK], y[:, tt, n * BLK:(n + 1) * BLK], ACT.Square, accum_out=st[:, 20 + 4 * tt + n:21 + 4 * tt + n]),
                       sig("y_squares") if n == 3 and tt == 1 else None)
            wait(act, "y_var")
            do(fn(st[:, 2:4], st[:, 2:4], ACT.Sqrt), sig("y_sd"))
            for tt in range(TT):
                wait(act, "x2_ready", tt + 1)
                do(fn(y[:, tt, :], x_t[:, tt, :], ACT.Square, accum_out=st[:, 4 + tt:5 + tt]), sig("x2_squares"))
            wait(act, "x2_var")
            do(fn(st[:, 4:6], st[:, 4:6], ACT.Sqrt), sig("x2_sd"))
            copy_transposed("x2", h2T)
            wait(act, "aff2_ready")
            settle()
            modulate(h2T, 1, "h2_ready_act")

            wait(act, "group_shift")
            for tt in range(TT):
                do(fn(rt[:, 208 + 4 * tt:212 + 4 * tt], rt[:, 36 * tt:36 * tt + 4], ACT.Exp, bias=rt[:, 216 + tt:217 + tt],
                      accum_out=rt[:, 218 + tt:219 + tt]))
            do(fn(rt[:, 220:222], rt[:, 220:222], ACT.Exp), sig("route_exp"))

            wait(act, "zeros_ready")
            for s in range(2):
                act.dma_start(y_rows[NE * CAP:NE * CAP + 1, s * 1024:(s + 1) * 1024], ysum[0:1, 0, s * 1024:(s + 1) * 1024])\
                   .then_inc(sig("rows_stored").sem, 16)
            act.sem_inc(sig("rows_copied").sem, 1)

            with act.Fori(0, NE) as e:
                act.wait_ge(sig("expert_used").sem, e * HB + 4)
                fn(sil[64:128, :], bank[0][0:64, :], ACT.Silu).then_inc(sig("silu").sem, 1)
                act.wait_ge(sig("expert_used").sem, e * HB + 6)
                act.wait_ge(sig("rows_stored").sem, e * 32 + 32)
                fn(rows[:, 0:BLK], bank[2][:, :], ACT.Copy).then_inc(sig("rows_copied").sem, 1)
                act.wait_ge(sig("rows_copied").sem, e * 2 + 4)
                for s in range(2):
                    act.dma_start(y_rows[bass.ds(e * CAP, CAP), s * 1024:(s + 1) * 1024], rows[64 * s:64 * s + 64, :])\
                       .then_inc(sig("rows_stored").sem, 16)

            wait(act, "flag_ready")
            over = nc.scalar.value_load(flag[0:1, 0:1], min_val=0, max_val=2 * S)
            with act.If(over > 0):
                with act.Fori(0, NE) as e:
                    for tt in range(TT):
                        act.wait_ge(sig("dense_gu").sem, e * 2 + (tt + 1))
                        fn(dsil[:, :], bank[0][:, :], ACT.Silu).then_inc(sig("dense_silu").sem, 1)
            with act.Else():
                act.nop()
            act.nop()
            for tt in range(TT):
                wait(act, "ysum_ready")
                do(fn(ring[:, 4, :, :].rearrange("p a b -> p (a b)")[:, tt * D:(tt + 1) * D], ysum[:, tt, :], ACT.Square,
                      accum_out=st[:, 8 + tt:9 + tt]), sig("ysum_squares"))
            wait(act, "ysum_var")
            do(fn(st[:, 8:10], st[:, 8:10], ACT.Sqrt), sig("ysum_sd"))

        @block.gpsimd
        def _(pool):
            inc(nc.gpsimd.memset(silc[:, :, :], 0.0), "silc_zero")
            inc(nc.gpsimd.memset(ones[:, :], 1.0), "ones_ready")
            pool.dma_start(posi, a["positions"].to_broadcast([P, S])).then_inc(sig("positions_in").sem, 16)
            pool.dma_start(w2[:, 0, :], a["cmp_w2_k"]).then_inc(sig("cmp_w2_in").sem, 16)
            pool.dma_start(w2[:, 1, :], a["cmp_w2_v"]).then_inc(sig("cmp_w2_in").sem, 16)
            pool.dma_start(gnorm, a["hgrn_g_norm"].to_broadcast([P, 1024])).then_inc(sig("g_norm_in").sem, 16)
            wait(pool, "gains_T_copied")
            pool.dma_start(gain_rows, part[0:2 * KT, 0:P]).then_inc(sig("gains_out").sem, 16)
            wait(pool, "probsT0", NH)
            wait(pool, "probsT1", NH)
            wait(pool, "oT", NH)
            inc(nc.gpsimd.memset(at[:, :, :], 0.0), "at_zero")
            wait(pool, "gains_out", 16)
            wait(pool, "rec_gated", 16)
            for n in range(2):
                src = gain_rows[n * KT:(n + 1) * KT, :].rearrange("(o k) p -> o (k p)", o=1).to_broadcast([P, D])
                pool.dma_start(RG[:, n, :], src).then_inc(sig("gains_in").sem, 16)
            for tt in range(TT):
                pool.dma_start(x_t[:, tt, :], a["x"][tt * P:(tt + 1) * P, :]).then_inc(sig(f"x_again{tt}").sem, 16)
            pool.dma_start(wrt[:, :, 0:NGRP], a["w_group"].rearrange("(k p) c -> p k c", p=P)).then_inc(sig("router_in").sem, 16)
            pool.dma_start(wrt[:, :, NGRP:36], a["w_router"].rearrange("(k p) c -> p k c", p=P)).then_inc(sig("router_in").sem, 16)
            wait(pool, "idx_ready")
            wait(pool, "rows_stored", 32 * NE + 32)
            wait(pool, "expert_used", NE * HB)
            for tt in range(TT):
                for k in range(2):
                    n = 2 * tt + k
                    nc.gpsimd.indirect_dma_start(
                        out=gat(n), out_offset=None, in_=y_rows[:, :],
                        in_offset=bass.IndirectOffsetOnAxis(ap=idx[:, n:n + 1], axis=0)).then_inc(sig(f"rows_in{tt}").sem, 16)

        @block.vector
        def _(dve):
            lane = Lane(dve, sig("dve_steps"))
            do, settle = lane.do, lane.settle
            v = nc.vector
            ts, tt_op, stt = v.tensor_scalar, v.tensor_tensor, v.scalar_tensor_tensor

            def step(ins, name=None):
                do(ins, sig(name) if name else None)
                settle()

            def rstd(dst, squares, n, var, sd):
                step(ts(dst, squares, 1.0 / n, EPS, ALU.mult, ALU.add), var)

            wait(dve, "vectors_T")
            do(v.tensor_copy(vec[:, :, :], bank[0][:, 0:2 * P]), sig("vec_ready"))
            for b in (2, 4, 6):
                dve.sem_inc(sig(f"taken{b}").sem, 1)
            wait(dve, "x_squares", 2)
            step(ts(st[:, 2:4], st[:, 0:2], 1.0 / D, EPS, ALU.mult, ALU.add), "x_var")
            wait(dve, "x_sd")
            step(v.reciprocal(st[:, 6:8], st[:, 4:6]))
            for tt in range(TT):
                do(ts(x_t[:, tt, :], x_t[:, tt, :], st[:, 6 + tt:7 + tt], None, ALU.mult), sig("xn_ready") if tt else None)

            def copy_transposed(tag, dst):
                for m in range(1, 8, 2):
                    wait(dve, f"{tag}_T", m + 1)
                    do(v.tensor_copy(dst[:, 2 * m:2 * m + 2, :], bank[1 + m % 4][:, :]), sig(f"{tag}_copied1"))

            copy_transposed("x1", hT)

            wait(dve, "positions_in", 16)
            settle()
            angf, turns, turni = RG[:, 0, 0:S], RG[:, 0, S:2 * S], RG[:, 0, 2 * S:3 * S].bitcast(I32)
            step(v.tensor_copy(angf, posi))
            step(ts(angf, angf, cst[:, C_INVF:C_INVF + 1], None, ALU.mult))
            for dst, quarter, shift in ((sinT, 0.0, 0.0), (cosT, 0.25, float(np.pi / 2))):
                step(ts(turns, angf, float(1.0 / (2 * np.pi)), quarter, ALU.mult, ALU.add))
                step(v.tensor_copy(turni, turns))
                step(v.tensor_copy(turns, turni))
                step(stt(dst[:, :], turns, -TWO_PI_HI, angf, ALU.mult, ALU.add))
                step(stt(dst[:, :], turns, -TWO_PI_MID, dst[:, :], ALU.mult, ALU.add))
                step(stt(dst[:, :], turns, -TWO_PI_LO, dst[:, :], ALU.mult, ALU.add))
                step(ts(dst[:, :], dst[:, :], shift, PI_SAFE, ALU.add, ALU.min))
                step(ts(dst[:, :], dst[:, :], -PI_SAFE, None, ALU.max), "angles" if quarter else None)

            l0, l1 = vec[:, 1, V_LB0:V_LB0 + NH], vec[:, 1, V_LB1:V_LB1 + NH]
            lb, lb1 = lbc[:, 0, :], lbc[:, 1, :]
            step(tt_op(lbc[:, 2, :], l0, l1, ALU.max))
            step(tt_op(lb, l0, lbc[:, 2, :], ALU.subtract))
            step(tt_op(lb1, l1, lbc[:, 2, :], ALU.subtract), "lb_logits")

            def ada_part(n, used_value):
                dve.wait_ge(sig("ring_used").sem, used_value)
                if not isinstance(n, int) or n > 0:
                    dve.wait_ge(sig("mod_cols").sem, n)
                v.tensor_copy(part[:, :], bank[0][:, :]).then_inc(sig("part_copied").sem, 1)

            def ada_mod(n):
                dve.wait_ge(sig("mod_cols").sem, n + 1)
                v.tensor_copy(mod[:, bass.ds(n * 4, 4)], bank[7][:, :].rearrange("p (j c) -> p j c", j=4)[:, :, 0])\
                    .then_inc(sig("mod_copied").sem, 1)

            for slot in range(3):
                ada_part(slot, 2 * slot + 2)
                ada_mod(slot)
            with dve.Fori(1, 3) as t:
                for slot in range(3):
                    ada_part(t * 3 + slot, t * HB + (2 * slot + 2))
                    ada_mod(t * 3 + slot)

            def affine(which, gpre, c_shift, ready):
                bada = vec[:, 0, V_BADA:V_BADA + 6 * KT]
                scale, shift = aff[:, 2 * which, :], aff[:, 2 * which + 1, :]
                do(tt_op(shift, mod[:, c_shift:c_shift + KT], bada[:, c_shift:c_shift + KT], ALU.add))
                step(tt_op(scale, mod[:, c_shift + KT:c_shift + 2 * KT], bada[:, c_shift + KT:c_shift + 2 * KT], ALU.add))
                step(stt(scale, scale, 1.0, gpre, ALU.add, ALU.mult), ready)

            wait(dve, "mod_copied", 9)
            affine(0, vec[:, 0, V_GPRE1:V_GPRE1 + KT], 0, "aff1_ready")

            def modulate(dst, which, ready):
                for k in (2, 3, 6, 7, 10, 11, 14, 15):
                    do(ts(dst[:, k, :], dst[:, k, :], aff[:, 2 * which, k:k + 1], aff[:, 2 * which + 1, k:k + 1],
                          ALU.mult, ALU.add), sig(ready) if k == KT - 1 else None)

            modulate(hT, 0, "h_ready_dve")

            def take(b, value, dst, src):
                dve.wait_ge(sig("full2" if b == 2 else "ring_used").sem, value)
                v.tensor_copy(dst, src).then_inc(sig(f"taken{b}").sem, 1)

            def feature_tiles(base, n, t):
                take(2, n + 1, RT[:, bass.ds(base + 1, 1), :], bank[2][:, 0:S])
                take(4, t * HB + 4, RT[:, bass.ds(base + 3, 1), :], bank[4][:, 0:S])

            with dve.Fori(0, 3) as i:
                ada_part(i * 2 + 9, i * HB + (3 * HB + 2))
                feature_tiles(i * 4, i, i + 3)
                ada_mod(i * 2 + 9)
                ada_part(i * 2 + 10, i * HB + (3 * HB + 6))
                ada_mod(i * 2 + 10)
            ada_part(15, 6 * HB + 2)
            for b2 in range(2):
                take(2, 4 + b2, RT[:, TKS + 2 * b2 + 1, :], bank[2][:, 0:S])
                take(4, 6 * HB + 4 + 2 * b2, vtok[:, b2, 1, :], bank[4][:, 0:256])
                if b2 == 0:
                    ada_mod(15)
            with dve.Fori(0, 4) as i:
                ada_part(i + 16, i * HB + (7 * HB + 2))
                feature_tiles(i * 4 + THQ, i + 5, i + 7)
                ada_mod(i + 16)
                take(6, i * HB + (7 * HB + 6), htok[:, bass.ds(i, 1), 1, :], bank[6][:, :])

            wait(dve, "gates_T")
            step(v.tensor_copy(gts[:, :, :], bank[2][:, 0:64].rearrange("p (t c) -> p t c", t=TT)[:, :, 0:N_GATES]), "gates_ready")

            wait(dve, "trig")
            for b in (1, 3):
                wait(dve, f"taken{b}", 10)
            sin2, cos2 = (w[:, :].rearrange("p (o t) -> p o t", o=1).broadcast_to([P, 2, S]) for w in (sinT, cosT))
            for n in range(7):
                c0 = 2 * n if n < 5 else TKS + 2 * (n - 5)
                tmp = RX[:, 3072:3584].rearrange("p (a t) -> p a t", a=2)
                wait(dve, "swapped", n + 1)
                step(tt_op(tmp, bank[3 + n % 2][:, :].rearrange("p (a t) -> p a t", a=2), sin2, ALU.mult), "roped_mul")
                step(tt_op(RT[:, c0:c0 + 2, :], RT[:, c0:c0 + 2, :], cos2, ALU.mult))
                step(tt_op(RT[:, c0:c0 + 2, :], RT[:, c0:c0 + 2, :], tmp, ALU.add), "roped")

            for w, (src, pe0) in enumerate(((TKC, V_PEK), (TVC, V_PEV))):
                dst = RX[:, w * 1024:(w + 1) * 1024].rearrange("p (q g c) -> p q g c", q=CMP_LEN, g=KVG)
                step(v.memset(RX[:, w * 1024:(w + 1) * 1024], 0.0))
                for g in range(KVG):
                    strided = RT[:, src + g, :].rearrange("p (c q) -> p q c", q=CMP_STRIDE)
                    for hf in range(2):
                        pos = vec[:, 1, pe0 + 16 * hf:pe0 + 16 * hf + 16].rearrange("p (q o) -> p q o", o=1)\
                            .broadcast_to([P, CMP_STRIDE, NC_CMP])
                        do(tt_op(dst[:, 16 * hf:16 * hf + 16, g, 0:NC_CMP], strided[:, :, hf:hf + NC_CMP], pos, ALU.add),
                           sig("blocks_ready") if g == 1 and hf == 1 else None)
            for w in range(2):
                wait(dve, "ring_used", 11 * HB + 1 + w)
                do(v.tensor_copy(RX[:, 2048 + w * P:2048 + (w + 1) * P], bank[5 + w][:, 0:P]), sig("cmp_part"))
            wait(dve, "cmp_out")
            do(v.tensor_copy(kcT[:, :, :], bank[3][:, 0:32].rearrange("p (g c) -> p g c", g=KVG)), sig("kc_ready"))
            do(v.tensor_copy(vc4[:, :, :], bank[4][:, 0:2 * P].rearrange("p (g c) -> p g c", g=KVG)), sig("vc_ready"))

            for n, (t, slot) in enumerate([(11, 1), (11, 2), (12, 0), (12, 1)]):
                ada_part(20 + n, t * HB + 2 * slot + 2)
                ada_mod(20 + n)
            wait(dve, "mod_copied", ADA_BLOCKS)
            affine(1, vec[:, 1, V_GPRE2:V_GPRE2 + KT], 3 * KT, "aff2_ready")
            gain = gcol.rearrange("p (n k) -> p n k", n=2)
            both = mod[:, :].rearrange("p (n j) -> p n j", n=2)[:, :, 2 * KT:3 * KT]
            bada = vec[:, 0, V_BADA:V_BADA + 6 * KT].rearrange("p (n j) -> p n j", n=2)[:, :, 2 * KT:3 * KT]
            step(tt_op(gain, both, bada, ALU.add))
            step(tt_op(gain, gain, vec[:, 1, V_GPOST1:V_GPOST1 + 2 * KT].rearrange("p (n k) -> p n k", n=2), ALU.mult), "gains_ready")
            wait(dve, "gains_T")
            step(v.tensor_copy(part[0:2 * KT, 0:P], bank[1][0:2 * KT, 0:P]), "gains_T_copied")

            wait(dve, "cmp_scores")
            cs = rt[:, :].rearrange("p (t h c) -> p t h c", t=TT, h=NH)
            cs2 = rt[:, :].rearrange("p (n c) -> p n c", c=16)

            def per_block(c0):
                return cst[:, c0:c0 + 32].rearrange("p (t o c) -> p t o c", t=TT, o=1).broadcast_to([P, TT, NH, 16])

            def bcast(col):
                return st[:, col:col + 16].rearrange("p (n o) -> p n o", o=1).broadcast_to([P, 16, 16])

            step(tt_op(cs, bank[2][:, 0:256].rearrange("p (t h c) -> p t h c", t=TT, h=NH), per_block(C_CNEG), ALU.add))
            step(v.reduce_max(st[:, 48:64], cs2, AX))
            step(tt_op(cs2, cs2, bcast(48), ALU.subtract), "pc_shifted")
            wait(dve, "pc_exp")
            step(tt_op(cs, cs, per_block(C_C01), ALU.mult))
            step(v.reduce_sum(st[:, 48:64], cs2, AX))
            step(ts(st[:, 48:64], st[:, 48:64], 1e-30, None, ALU.max))
            step(v.reciprocal(st[:, 48:64], st[:, 48:64]))
            step(tt_op(st[:, 48:64].rearrange("p (t h) -> p t h", t=TT), st[:, 48:64].rearrange("p (t h) -> p t h", t=TT),
                       gts[:, :, :].rearrange("p t (h b) -> p t h b", b=3)[:, :, :, 0], ALU.mult))
            step(v.memset(pcp[:, :, :], 0.0))
            step(tt_op(pcp[:, :, :].rearrange("p t (h c) -> p (t h) c", c=32)[:, :, 0:16], cs2, bcast(48), ALU.mult), "pc_ready")
            def maxima(h):
                s0 = 24 + 12 * (h % 2)
                for br in range(2):
                    wait(dve, "scores", 2 * h + br + 1)
                    b = bank[3 + 2 * (h % 2) + br]
                    for tt in range(TT):
                        c0, n = (0, P) if tt == 0 else (P, 2 * P)
                        do(v.tensor_reduce(st[:, s0 + 2 * br + tt:s0 + 2 * br + tt + 1], b[:, c0:c0 + n], AX, ALU.max, negate=True))
                settle()
                step(ts(st[:, s0:s0 + 4], st[:, s0:s0 + 4], SCALE, None, ALU.mult), "maxima")

            maxima(0)
            wait(dve, "pcT")
            do(v.tensor_copy(pcT[:, :, :], bank[1][:, :].rearrange("p (g t) -> p g t", g=KVG)), sig("pcT_copied"))
            for h in range(NH):
                if h + 1 < NH:
                    maxima(h + 1)
                s0 = 24 + 12 * (h % 2)
                wait(dve, "exps", 2 * h + 2)
                step(v.reciprocal(st[:, s0 + 8:s0 + 12], st[:, s0 + 4:s0 + 8]))
                step(tt_op(st[:, s0 + 8:s0 + 12].rearrange("p (b t) -> p b t", b=2), st[:, s0 + 8:s0 + 12].rearrange("p (b t) -> p b t", b=2),
                           gts[:, :, 3 * h + 1:3 * h + 3].rearrange("p t b -> p b t"), ALU.mult))
                for br in range(2):
                    for tt in range(TT):
                        c0, n = (0, P) if tt == 0 else (P, 2 * P)
                        w = probs[:, h % 2, br, c0:c0 + n]
                        do(ts(w, w, st[:, s0 + 8 + 2 * br + tt:s0 + 9 + 2 * br + tt], None, ALU.mult), sig("probs") if tt else None)
                wait(dve, "probsT1", h + 1)
                do(v.tensor_copy(probsT[:, h % 2, 1, :], bank[7][:, 0:384]), sig("probsT_copied1"))

            wait(dve, "lb_exp")
            step(tt_op(lbc[:, 2, :], lb, lb1, ALU.add))
            step(v.reciprocal(lbc[:, 2, :], lbc[:, 2, :]))
            step(tt_op(lb, lb, lbc[:, 2, :], ALU.mult))
            step(ts(lb1, lb, -1.0, 1.0, ALU.mult, ALU.add))
            wait(dve, "forget_sig")
            fT = RT[:, THF:THF + NH, :]
            for h in range(NH):
                do(ts(fT[:, h, :], fT[:, h, :], lb1[:, h:h + 1], lb[:, h:h + 1], ALU.mult, ALU.add))
            settle()
            step(ts(kT[:, :, :], fT, -1.0, 1.0, ALU.mult, ALU.add), "forget_ready")
            wait(dve, "forget_log")
            wait(dve, "ones_ready")
            for h in range(NH):
                do(v.tensor_tensor_scan(out=fT[:, h, :], data0=ones[:, 0:1].broadcast_to([P, S]), data1=fT[:, h, :],
                                        initial=0.0, op0=ALU.mult, op1=ALU.add))
            settle()
            wait(dve, "q_and_g_silu")
            wait(dve, "g_norm_in", 16)
            for tt in range(TT):
                g_t = htok[:, 2:4, tt, :]
                do(tt_op(g_t, g_t, gnorm.rearrange("p (i c) -> p i c", i=2), ALU.mult))

            bsum = fT.rearrange("p h t -> p (h t)")
            kflat = kT[:, :, :].rearrange("p h t -> p (h t)")
            qflat = RT[:, THQ:THQ + NH, :].rearrange("p h t -> p (h t)")

            def halves(w, s):
                w2_ = w.rearrange("p (x u s) -> p x u s", u=2, s=s)
                return w2_[:, :, 0, :], w2_[:, :, 1, :]

            def spans(n):
                s = LEVELS[n]
                zl, zr = halves(zf[:, n % 2, :], s)
                bl, br = halves(bsum, s)
                mid = bl[:, :, s - 1:s].broadcast_to([P, NH * S // (2 * s), s])
                if n >= 2:
                    wait(dve, "products", n - 1)
                do(tt_op(zl, mid, bl, ALU.subtract))
                do(tt_op(zr, br, mid, ALU.subtract), sig("spans"))

            def factors(n):
                s = LEVELS[n]
                zl, zr = halves(zf[:, n % 2, :], s)
                wait(dve, "decays", n + 1)
                do(tt_op(zl, zl, halves(kflat, s)[0], ALU.mult))
                do(tt_op(zr, zr, halves(qflat, s)[1], ALU.mult), sig("factors"))

            def products(n):
                wait(dve, "products", n + 1)
                if n == 0:
                    wait(dve, "at_zero")
                    for b in range(2):
                        do(v.tensor_copy(at[:, 4 * b:4 * b + 4, P:2 * P], bank[1 + b][:, :].rearrange("p (h i) -> p h i", h=4)),
                           sig("products_used") if b else None)
                elif n == 1:
                    for tt in range(TT):
                        do(v.tensor_copy(at[0:64, :, tt * S + 64:tt * S + P], bank[3 + tt][0:64, :].rearrange("p (h i) -> p h i", h=NH)),
                           sig("products_used") if tt else None)
                elif n == 2:
                    for tt in range(TT):
                        for q in range(2):
                            src = bank[5][64 * q:64 * q + 32, tt * 256:(tt + 1) * 256].rearrange("p (h i) -> p h i", h=NH)
                            c0 = tt * S + 64 * q + 32
                            do(v.tensor_copy(at[64 * q:64 * q + 32, :, c0:c0 + 32], src), sig("products_used") if tt and q else None)
                else:
                    c0 = C_LEV + 32 * (n - 3)
                    mask = cst[:, c0:c0 + 32].rearrange("p (o i) -> p o i", o=1).broadcast_to([P, 16, 32])
                    src = bank[6 + n % 2][:, :].rearrange("p (m i) -> p m i", m=16)
                    dst = (acc if n == 3 else acc_new).rearrange("p (m i) -> p m i", m=16)
                    step(tt_op(dst, src, mask, ALU.mult), "products_used")
                    if n > 3:
                        step(tt_op(acc, acc, acc_new, ALU.add))

            spans(0)
            for n in range(8):
                if n + 1 < 8:
                    spans(n + 1)
                factors(n)
                if n > 0:
                    products(n - 1)
            products(7)
            products(8)
            for tt in range(TT):
                for q in range(4):
                    c0 = tt * S + 32 * q
                    do(v.tensor_copy(at[32 * q:32 * q + 32, :, c0:c0 + 32],
                                     acc[32 * q:32 * q + 32, tt * 256:(tt + 1) * 256].rearrange("p (h i) -> p h i", h=NH)),
                       sig("decay_ready") if tt and q == 3 else None)
            wait(dve, "rec_squares")
            step(ts(st[:, 0:16], st[:, 0:16], 1.0 / HD, EPS, ALU.mult, ALU.add), "rec_var")
            wait(dve, "rec_sd")
            step(v.reciprocal(st[:, 0:16], st[:, 0:16]))
            for tt in range(TT):
                for h in range(NH):
                    n = tt * NH + h
                    do(stt(orec[:, tt, h * P:(h + 1) * P], bank[1 + 2 * tt + h // 4][:, (h % 4) * P:(h % 4 + 1) * P],
                           st[:, n:n + 1], htok[:, 2 + h // 4, tt, (h % 4) * P:(h % 4 + 1) * P], ALU.mult, ALU.mult), sig("rec_gated"))
            for tt in range(TT):
                wait(dve, "recT", 4 * tt + 4)
                do(v.tensor_copy(RT[:, THQ + 4:THQ + 8, tt * P:(tt + 1) * P], bank[6][:, :].rearrange("p (h t) -> p h t", h=4)),
                   sig("recT_copied"))

            for n in range(4):
                for tt in range(TT):
                    if tt == 0:
                        wait(dve, "y_half", n + 1)
                    else:
                        wait(dve, "ring_used", 78 + 2 * n)
                    do(v.tensor_copy(y[:, tt, n * BLK:(n + 1) * BLK], bank[2 * n + tt][:, :]), sig("y_copied"))
            wait(dve, "y_squares")
            step(v.reduce_sum(st[:, 2:4], st[:, 20:28].rearrange("p (t n) -> p t n", t=TT), AX))
            step(ts(st[:, 2:4], st[:, 2:4], 1.0 / D, EPS, ALU.mult, ALU.add), "y_var")
            wait(dve, "y_sd")
            step(v.reciprocal(st[:, 2:4], st[:, 2:4]))
            wait(dve, "gains_in", 32)
            for tt in range(TT):
                wait(dve, f"x_again{tt}", 16)
                step(stt(y[:, tt, :], y[:, tt, :], st[:, 2 + tt:3 + tt], RG[:, 0, :], ALU.mult, ALU.mult))
                step(tt_op(x_t[:, tt, :], x_t[:, tt, :], y[:, tt, :], ALU.add), "x2_ready")
            wait(dve, "x2_squares", 2)
            step(ts(st[:, 4:6], st[:, 4:6], 1.0 / D, EPS, ALU.mult, ALU.add), "x2_var")
            wait(dve, "x2_sd")
            step(v.reciprocal(st[:, 4:6], st[:, 4:6]))
            for tt in range(TT):
                do(ts(xn2[:, tt, :], x_t[:, tt, :], st[:, 4 + tt:5 + tt], None, ALU.mult), sig("xn2_ready") if tt else None)
            copy_transposed("x2", h2T)
            settle()
            modulate(h2T, 1, "h2_ready_dve")
            step(v.memset(ysum[0:1, 0, :], 0.0), "zeros_ready")

            wait(dve, "logits_mm")
            wait(dve, "brt_in", 32)
            step(ts(part[0:36, 0:S], bank[6][0:36, 0:S], brt[:, 0:1], None, ALU.add), "logits_biased")
            wait(dve, "logits_T")
            step(v.tensor_copy(rt[:, 0:72].rearrange("p (t c) -> p t c", t=TT),
                               bank[7][:, 0:128].rearrange("p (t c) -> p t c", t=TT)[:, :, 0:36]))
            iota = cst[:, C_IOTA:C_IOTA + 64]
            step(v.memset(rt[:, 72:104], -3.0e38))
            top, sl = rt[:, 104:120], rt[:, 120:136]
            num = rt[:, 224:232]
            groups8 = rt[:, 72:88].rearrange("p (t c) -> p t c", t=TT)
            step(v.tensor_copy(groups8[:, :, 0:NGRP], rt[:, 0:72].rearrange("p (t c) -> p t c", t=TT)[:, :, 0:NGRP]))
            for tt in range(TT):
                do(v.max(top[:, 8 * tt:8 * tt + 8], groups8[:, tt, :]))
            settle()
            for tt in range(TT):
                do(v.max_index(rti[:, 8 * tt:8 * tt + 8], top[:, 8 * tt:8 * tt + 8], groups8[:, tt, :]))
            settle()
            two = top.rearrange("p (t c) -> p t c", t=TT)
            twoi = rti[:, :].rearrange("p (t c) -> p t c", t=TT)
            do(ts(rt[:, 216:218], two[:, :, 0], -1.0, None, ALU.mult))
            step(v.tensor_copy(num[:, 0:2], twoi[:, :, 0]))
            for tt in range(TT):
                le = rt[:, 36 * tt + 4:36 * tt + 36]
                step(ts(rt[:, 240:244], iota[:, 0:NGRP], num[:, tt:tt + 1], None, ALU.is_equal))
                step(ts(sl[:, 8 * tt:8 * tt + 8], le[:, 0:8], rt[:, 240:241], None, ALU.mult))
                for g in range(1, NGRP):
                    step(stt(sl[:, 8 * tt:8 * tt + 8], le[:, 8 * g:8 * g + 8], rt[:, 240 + g:241 + g], sl[:, 8 * tt:8 * tt + 8],
                             ALU.mult, ALU.add))
                step(v.max(top[:, 8 * tt:8 * tt + 8], sl[:, 8 * tt:8 * tt + 8]))
                step(v.max_index(rti[:, 8 * tt:8 * tt + 8], top[:, 8 * tt:8 * tt + 8], sl[:, 8 * tt:8 * tt + 8]))
            step(tt_op(rt[:, 220:222], two[:, :, 1], two[:, :, 0], ALU.subtract), "group_shift")
            for k in range(2):
                step(v.tensor_copy(num[:, 2 + 2 * k:4 + 2 * k], twoi[:, :, k]))
                step(stt(num[:, 2 + 2 * k:4 + 2 * k], num[:, 0:2], float(EPG), num[:, 2 + 2 * k:4 + 2 * k], ALU.mult, ALU.add))
            oh = onehots
            for tt in range(TT):
                for k in range(2):
                    do(ts(oh[:, tt, k, :], iota[:, 0:NE], num[:, 2 + 2 * k + tt:3 + 2 * k + tt], None, ALU.is_equal))
            settle()
            step(tt_op(sel[:, :, :], oh[:, :, 0, :], oh[:, :, 1, :], ALU.add), "chosen")
            wait(dve, "route_exp")
            step(v.reciprocal(rt[:, 218:220], rt[:, 218:220]))
            step(ts(rt[:, 222:224], rt[:, 220:222], 1.0, None, ALU.add))
            step(v.reciprocal(rt[:, 222:224], rt[:, 222:224]))
            step(tt_op(wk[:, :, 0], rt[:, 218:220], rt[:, 222:224], ALU.mult))
            step(tt_op(wk[:, :, 1], wk[:, :, 0], rt[:, 220:222], ALU.mult))
            wait(dve, "ranks")
            step(v.tensor_copy(rank[:, :, :], bank[7][:, 128:192].rearrange("p (t e) -> p t e", t=TT)))

            def onehot_pair(n, first):
                if not first:
                    dve.wait_ge(sig("gathered").sem, (n - 1) * 4)
                for tt in range(TT):
                    for q in range(2):
                        e = (n - 1) * 2 + q
                        ins = ts(onehot[:, tt, q * CAP:(q + 1) * CAP], iota, rank[:, tt, bass.ds(e, 1)], sel[:, tt, bass.ds(e, 1)],
                                 ALU.is_equal, ALU.mult)
                        if tt and q:
                            ins.then_inc(sig("onehot").sem, 1)

            onehot_pair(1, True)
            step(v.tensor_copy(rt[:, 0:1], rt[:, 218:219]))
            for k in range(2):
                step(tt_op(rt[:, 0:64].rearrange("p (t e) -> p t e", t=TT), oh[:, :, k, :], rank[:, :, :], ALU.mult))
                step(v.reduce_sum(rt[:, 64:66], rt[:, 0:64].rearrange("p (t e) -> p t e", t=TT), AX))
                step(ts(rt[:, 202 + 2 * k:204 + 2 * k], rt[:, 64:66], float(CAP), None, ALU.is_ge))
                step(stt(rt[:, 66:68], num[:, 2 + 2 * k:4 + 2 * k], float(CAP), rt[:, 64:66], ALU.mult, ALU.add))
                step(ts(rt[:, 68:70], rt[:, 66:68], -1.0, float(NE * CAP), ALU.mult, ALU.add))
                step(tt_op(rt[:, 68:70], rt[:, 68:70], rt[:, 202 + 2 * k:204 + 2 * k], ALU.mult))
                step(tt_op(idx[:, :].rearrange("p (t k) -> p t k", k=2)[:, :, k], rt[:, 66:68], rt[:, 68:70], ALU.add), "idx_ready" if k else None)
                step(tt_op(rt[:, 70:72], wk[:, :, k], rt[:, 202 + 2 * k:204 + 2 * k], ALU.mult))
                for tt in range(TT):
                    if k == 0:
                        step(ts(cwo[:, tt, :], oh[:, tt, 0, :], rt[:, 70 + tt:71 + tt], None, ALU.mult))
                    else:
                        step(stt(cwo[:, tt, :], oh[:, tt, 1, :], rt[:, 70 + tt:71 + tt], cwo[:, tt, :], ALU.mult, ALU.add))
            step(v.reduce_sum(rt[:, 200:201], rt[:, 202:206], AX), "over_counted")
            wait(dve, "over_sum")
            step(v.tensor_copy(flag[:, :], bank[7][:, 192:193]), "over_read")

            step(v.memset(hid[64:128, :], 0.0))
            dve.sem_inc(sig("rows_copied").sem, 1)
            dve.sem_inc(sig("flag_ready").sem, 1)

            def tokens(n, waits):
                for m in range(4):
                    dve.wait_ge(sig("gathered").sem, (n - 1) * 4 + (m + 1))
                    for k in range(4 * m, 4 * m + 4):
                        ins = ts(tokT[:, k, :], bank[GB[m % 3]][:, (k % 4) * P:(k % 4 + 1) * P], aff[:, 2, k:k + 1], aff[:, 3, k:k + 1],
                                 ALU.mult, ALU.add)
                    ins.then_inc(sig("gathered_used").sem, 1)

            def pair(p, gather_next):
                for q in range(2):
                    e = p * 2 + q
                    if q == 1 and gather_next:
                        onehot_pair(p + 2, False)
                    dve.wait_ge(sig("silu").sem, e + 1)
                    tt_op(hid[0:64, :], bank[0][64:128, :], sil[64:128, :], ALU.mult).then_inc(sig("hidden").sem, 1)
                    if q == 1 and gather_next:
                        tokens(p + 2, True)
                    dve.wait_ge(sig("hiddenT").sem, e + 1)
                    v.tensor_copy(hidT.rearrange("p (f s) -> p f s", f=4), bank[1][:, :].rearrange("p (f s) -> p f s", f=4)[:, :, 0:CAP]).then_inc(sig("hiddenT_copied").sem, 1)
                    dve.wait_ge(sig("expert_used").sem, e * HB + 6)
                    dve.wait_ge(sig("rows_stored").sem, e * 32 + 32)
                    v.tensor_copy(rows[:, BLK:2 * BLK], bank[3][:, :]).then_inc(sig("rows_copied").sem, 1)

            tokens(1, False)
            with dve.Fori(0, NE // 2 - 1) as p:
                pair(p, True)
            pair(NE // 2 - 1, False)

            for tt in range(TT):
                wait(dve, f"rows_in{tt}", 32)
                step(ts(ysum[:, tt, :], gat(2 * tt), wk[:, tt, 0:1], None, ALU.mult))
                step(stt(ysum[:, tt, :], gat(2 * tt + 1), wk[:, tt, 1:2], ysum[:, tt, :], ALU.mult, ALU.add),
                     "combined" if tt else None)
            over = nc.vector.value_load(flag[0:1, 0:1], min_val=0, max_val=2 * S)
            with dve.If(over > 0):
                with dve.Fori(0, NE) as e:
                    for tt in range(TT):
                        c = e * 2 + tt
                        dve.wait_ge(sig("dense_silu").sem, c + 1)
                        stt(dhid[:, :], bank[1][:, :], cwo[:, tt, bass.ds(e, 1)], dsil[:, :], ALU.mult, ALU.mult)\
                            .then_inc(sig("dense_hid").sem, 1)
                        dve.wait_ge(sig("dense_T").sem, c + 1)
                        v.tensor_copy(dhidT[:, :], bank[2][:, :]).then_inc(sig("dense_T_copied").sem, 1)
                        dve.wait_ge(sig("dense_down").sem, c + 1)
                        for n in range(4):
                            w = ysum[:, tt, n * BLK:(n + 1) * BLK]
                            ins = tt_op(w, w, bank[4 + n][:, :], ALU.add)
                        ins.then_inc(sig("dense_added").sem, 1)
                dve.wait_ge(sig("dense_added").sem, 2 * NE)
            with dve.Else():
                dve.nop()
            dve.sem_inc(sig("ysum_ready").sem, 1)
            wait(dve, "ysum_squares", 2)
            step(ts(st[:, 8:10], st[:, 8:10], 1.0 / D, EPS, ALU.mult, ALU.add), "ysum_var")
            wait(dve, "ysum_sd")
            step(v.reciprocal(st[:, 8:10], st[:, 8:10]))
            for tt in range(TT):
                step(stt(ysum[:, tt, :], ysum[:, tt, :], st[:, 8 + tt:9 + tt], RG[:, 1, :], ALU.mult, ALU.mult))
                step(tt_op(x_t[:, tt, :], x_t[:, tt, :], ysum[:, tt, :], ALU.add), f"out{tt}")


def kernel(**inputs):
    import concourse.bacc as _bacc
    from concourse.bass_utils import run_bass_kernel_spmd as _run

    lay = {k: np.ascontiguousarray(v) for k, v in inputs.items()}
    arrays = {
        "x": lay["x"][0],
        "positions": lay["positions"],
        "w_ada": lay["w_ada"][0],
        "w_in": lay["w_in"][0],
        "w_out": lay["w_out"][0],
        "c": lay["c"].reshape(KT, P),
        "b_ada": lay["b_ada"].reshape(6 * KT, P),
        "lb0": lay["hgrn_lb_logits"][0].reshape(NH, P),
        "lb1": lay["hgrn_lb_logits"][1].reshape(NH, P),
        "hgrn_g_norm": lay["hgrn_g_norm"],
        "b_group": lay["b_group"].reshape(NGRP, 1),
        "b_router": lay["b_router"].reshape(NE, 1),
        "w_gate": lay["w_gate"].reshape(NE, D, FE),
        "w_up": lay["w_up"].reshape(NE, D, FE),
        "w_down": lay["w_down"].reshape(NE, FE, D),
        "consts": constant_table(),
    }
    for name in ("g_pre_mix", "g_post_mix", "g_pre_ffn", "g_post_ffn"):
        arrays[name] = lay[name].reshape(KT, P)
    for name in ("cmp_pe_k", "cmp_w1_k", "cmp_w2_k", "cmp_pe_v", "cmp_w1_v", "cmp_w2_v", "w_group", "w_router"):
        arrays[name] = lay[name][0]
    nc = _bacc.Bacc("TRN2", target_bir_lowering=False, num_devices=1)
    feeds, aps = {}, {}
    for name, arr in arrays.items():
        feeds[f"in_{name}"] = np.ascontiguousarray(arr)
        aps[name] = nc.dram_tensor(f"in_{name}", arr.shape, mybir.dt.from_np(arr.dtype), kind="ExternalInput").ap()
    out = nc.dram_tensor("out_0", (S, D), F32, kind="ExternalOutput").ap()
    block_kernel(nc, aps, out)
    r = _run(nc, [feeds], core_ids=[0])
    return r.results[0]["out_0"].reshape(1, S, D)
```

```python
from contextlib import ExitStack

import numpy as np

import concourse.bass as bass
from concourse import mybir

ALU = mybir.AluOpType
ACT = mybir.ActivationFunctionType
AX = mybir.AxisListType.X
F32 = mybir.dt.float32
I32 = mybir.dt.int32
U32 = mybir.dt.uint32

P = 128
D = 2048
S = 256
TT = S // P
KT = D // P
NH = 8
HD = 128
KVG = 2
BLK = 512
NC_CMP = 15
CMP_LEN, CMP_STRIDE = 32, 16
NGRP, EPG = 4, 8
NE = NGRP * EPG
FE = 512
CAP = 64
EPS = 1e-6
SCALE = float(HD) ** -0.5
NEG = -1.0e30
TWO_PI_HI, TWO_PI_MID, TWO_PI_LO = 6.28125, 0.0019350051879882812, 3.019916050561733e-07
PI_SAFE = 3.1415925

HB = 6
ADA_BLOCKS = 6 * D // BLK
COL_V_SLC, COL_HQ, COL_HI = 1792, 2584, 4632
COL_GATES = 2560
N_GATES = 3 * NH
TQ, TKC, TVC, THQ, THF, TKS, TKW = 0, 8, 10, 12, 20, 28, 30
LEVELS = [128, 64, 32, 16, 8, 4, 2, 1]
ROPE_TILES = [(TKC, 9), (0, 1), (2, 3), (4, 5), (6, 7), (TKS, 13), (TKW, 17)]
LEVEL_TILES = [3, 4, 6, 7, 9, 10, 12, 13, 14]
REC_TILE = 16
EXP_AHEAD = 3
TILE_BANKS = [1, 2, 0, 7]

C_ID, C_NEG, C_ROT, C_UP, C_LEV, C_CNEG, C_C01, C_IOTA, C_SUM, C_INVF = 0, 128, 256, 384, 512, 704, 736, 768, 832, 992
C_COLS = 993
V_C, V_BADA, V_GPRE1 = 0, 16, 112
V_GPRE2, V_GPOST1, V_LB0, V_LB1, V_PEK, V_PEV = 0, 16, 48, 56, 64, 96


def constant_table():
    t = np.zeros((P, C_COLS), np.float32)
    r = np.arange(P)
    t[:, C_ID:C_ID + P] = np.eye(P)
    t[:, C_NEG:C_NEG + P] = np.where(r[None, :] > r[:, None], NEG, 0.0)
    rot = np.zeros((P, P), np.float32)
    rot[r[64:], r[:64]] = -1.0
    rot[r[:64], r[64:]] = 1.0
    t[:, C_ROT:C_ROT + P] = rot
    t[:, C_UP:C_UP + P] = r[:, None] < r[None, :]
    j, i = (r % 32)[:, None], np.arange(32)[None, :]
    for n, s in enumerate([16, 8, 4, 2, 1]):
        t[:, C_LEV + 32 * n:C_LEV + 32 * n + 32] = (
            (j // (2 * s) == i // (2 * s)) & (j % (2 * s) < s) & (i % (2 * s) >= s))
    t[:, C_LEV + 160:C_LEV + 192] = i == j
    for tt in range(TT):
        tok = tt * P + r[:, None]
        c = np.arange(16)[None, :]
        seen = (c < NC_CMP) & (c * CMP_STRIDE + CMP_LEN - 1 <= tok)
        t[:, C_CNEG + 16 * tt:C_CNEG + 16 * tt + 16] = np.where(seen, 0.0, NEG)
        t[:, C_C01 + 16 * tt:C_C01 + 16 * tt + 16] = seen
    t[:, C_IOTA:C_IOTA + 64] = np.arange(64)[None, :]
    t[:, C_SUM:C_SUM + 160] = (r % 32)[:, None] == (np.arange(160) % 32)[None, :]
    inv = (np.float32(10000.0) ** (-np.arange(0, HD, 2, dtype=np.float32) / np.float32(HD))).astype(np.float32)
    t[:, C_INVF] = np.concatenate([inv, inv])
    return t


STAGES = {
    "tensor_stages": ["vectors_T", "gates_mm", "gates_T", "rec", "cmp_out", "cmp_scores", "pcT", "gains_T", "logits_mm",
                      "logits_T", "ranks", "over_sum"],
    "scalar_stages": ["silc_ready", "x_sd", "h_ready_act", "gates_sig", "lb_exp", "trig", "forget_sig", "q_and_g_silu",
                      "forget_log", "rec_squares", "rec_sd", "cmp_silu", "pc_exp", "y_squares", "y_sd", "x2_sd",
                      "h2_ready_act", "route_exp", "ysum_sd0", "ysum_sd1"],
    "vector_stages": ["vec_ready", "x_var", "xn_ready", "aff1_ready", "h_ready_dve", "angles", "lb_logits", "gates_ready",
                      "forget_ready", "decay_ready", "rec_var", "kc_ready", "vc_ready", "pc_shifted", "pc_ready",
                      "pcT_copied", "aff2_ready", "gains_ready", "gains_T_copied", "y_var", "x2_var", "xn2_ready",
                      "h2_ready_dve", "logits_biased", "group_shift", "chosen", "over_counted",
                      "over_read", "ysum_var0", "out0", "ysum_var1", "out1"],
    "gpsimd_stages": ["silc_zero", "ones_ready", "at_zero", "ysum_zero"],
}
STAGE_OF = {name: (sem, n + 1) for sem, names in STAGES.items() for n, name in enumerate(names)}


class Signal:

    def __init__(self, sem):
        self.sem = sem
        self.n = 0


class Lane:

    def __init__(self, eng, own):
        self.eng = eng
        self.own = own
        self.last = None

    def do(self, ins, sig=None):
        sig = sig or self.own
        ins.then_inc(sig.sem, 1)
        sig.n = sig.n + 1
        self.last = (sig, sig.n)

    def settle(self):
        sig, n = self.last
        self.eng.wait_ge(sig.sem, n)

    def begin_loop(self, i, per):
        self.bases = {s: s.n for s in per}
        self.per = per
        self.i = i
        for s in per:
            s.n = s.n + i * per[s]
        self.starts = {s: s.n for s in per}
        self.last = None

    def end_loop(self, iters):
        for s, k in self.per.items():
            s.n = self.bases[s] + iters * k
        self.last = (self.own, self.own.n)


def block_kernel(nc, a, out):
    gain_rows = nc.dram_tensor("gain_rows", [2 * KT, P], F32, kind="Internal").ap()

    with ExitStack() as ctx:
        def sb(name, shape, dt=F32):
            return ctx.enter_context(nc.sbuf_tensor(name, shape, dt))

        sems = {}

        def sig(name):
            if name in STAGE_OF:
                stages, n = STAGE_OF[name]
                counted = sig(stages)
                assert counted.n == n - 1, name
                return counted
            if name not in sems:
                sems[name] = Signal(ctx.enter_context(nc.semaphore(name)))
            return sems[name]

        def wait(eng, name, n=1):
            if name in STAGE_OF:
                name, n = STAGE_OF[name]
            eng.wait_ge(sig(name).sem, n)

        def inc(ins, name):
            counted = sig(name)
            ins.then_inc(counted.sem, 1)
            counted.n = counted.n + 1

        ring = sb("ring", [P, HB, 8, BLK])
        RX = sb("RX", [P, 4096])
        RH = sb("RH", [P, 4096])
        RT = sb("RT", [P, 32, 256])
        RN = sb("RN", [P, 5120])
        RG = sb("RG", [P, 2, D])
        cst = sb("cst", [P, C_COLS])
        vec = sb("vec", [P, 2, P])
        vrow = RN[:, 0:256].rearrange("p (a b) -> p a b", a=2)
        silc = sb("silc", [P, KT, 32])
        part = sb("part", [P, BLK])
        mod = sb("mod", [P, 6 * KT])
        ones = sb("ones", [P, P])
        st = sb("st", [P, 64])
        gts = sb("gts", [P, TT, N_GATES])
        aff = sb("aff", [P, 4, KT])
        lbc = sb("lbc", [P, 4, NH])
        brt = sb("brt", [36, 1])
        rti = sb("rti", [P, 16], U32)
        cwo = sb("cwo", [P, TT, NE])
        wk = sb("wk", [P, TT, 2])
        flag = sb("flag", [P, 1], I32)

        x_t = RX[:, :].rearrange("p (t d) -> p t d", t=TT)
        hT = RH[:, :].rearrange("p (k t) -> p k t", k=KT)
        ident = cst[:, C_ID:C_ID + P]
        cosT, sinT = RX[:, 3584:3840], RX[:, 3840:4096]
        wrt = RN[:, 0:576].rearrange("p (k c) -> p k c", k=KT)
        wg24 = RG[:, 0, 1024:1408].rearrange("p (k c) -> p k c", k=KT)
        silf = silc[:, :, :].rearrange("p k c -> p (k c)")
        rt = silf[:, 0:256]
        onehots = silf[:, 256:384].rearrange("p (t k e) -> p t k e", t=TT, k=2)
        sel = silf[:, 384:448].rearrange("p (t e) -> p t e", t=TT)
        rank = silf[:, 448:512].rearrange("p (t e) -> p t e", t=TT)
        vtok = RN[:, 0:1024].rearrange("p (b t c) -> p b t c", b=2, t=TT)
        probs = RX[:, 0:1536].rearrange("p (r b c) -> p r b c", r=2, b=2)
        probsT = RX[:, 1536:3072].rearrange("p (r b c) -> p r b c", r=2, b=2)
        pcT = RX[:, 3072:3584].rearrange("p (g t) -> p g t", g=KVG)
        pcp = RX[:, 3584:4096].rearrange("p (t c) -> p t c", t=TT)
        w2 = RG[:, 1, 1024:1280].rearrange("p (v o) -> p v o", v=2)
        cmph = RG[:, 1, 1280:1600].rearrange("p (v o) -> p v o", v=2)
        vc4 = RG[:, 1, 1600:1856].rearrange("p (g o) -> p g o", g=KVG)
        kcT = RG[:, 1, 1856:1888].rearrange("p (g c) -> p g c", g=KVG)
        gcol = RG[:, 1, 1888:1920]
        gnorm = RG[:, 1, 0:1024]
        cmps = RX[:, 2304:2560]
        gsig = RX[0:N_GATES, 3072:3072 + S]
        htok = RN[:, 1024:5120].rearrange("p (i t c) -> p i t c", i=4, t=TT)
        kT = RG[:, 0, :].rearrange("p (h t) -> p h t", h=NH)
        zf = ring[:, 5, :, :].rearrange("p a b -> p (a b)").rearrange("p (r c) -> p r c", r=2)
        slot4 = ring[:, 4, :, :].rearrange("p a b -> p (a b)")
        at = RX[:, 0:3072].rearrange("p (h c) -> p h c", h=NH)
        acc, acc_new, scratch = slot4[:, 0:512], slot4[:, 512:1024], slot4[:, 1024:3072]
        orec = zf[:, :, 0:1024]
        y = RH[:, :].rearrange("p (t d) -> p t d", t=TT)
        xn2 = y
        h2T = RT[:, 0:KT, :]
        ysum = RT[:, KT:2 * KT, :].rearrange("p a b -> p (a b)").rearrange("p (t d) -> p t d", t=TT)
        tokT = RN[:, 0:2048].rearrange("p (k s) -> p k s", k=KT)
        onehot = RN[:, 2048:2304].rearrange("p (t s) -> p t s", t=TT)
        hid = RN[:, 2304:2816]
        sil = RN[:, 2816:3328]
        hidT = RN[:, 3328:3584]
        ohw = RN[:, 3584:3840].rearrange("p (t s) -> p t s", t=TT)
        ohwT = RN[:, 3840:4096]
        rows = RG[:, 0, :]
        cw = part[:, 0:2 * NE].rearrange("p (t e) -> p t e", t=TT)
        dhid, dsil, dhidT = hid, sil, RN[:, 0:512]
        GB = [4, 5, 6]
        posi = RG[:, 0, 3 * S:4 * S].bitcast(I32)

        bank = [ctx.enter_context(nc.psum_tensor(f"bank{i}", [P, BLK], F32)) for i in range(8)]

        block = ctx.enter_context(nc.Block())

        SHORT_TURNS, TURNS = (7, 8, 9), 15

        def used_count(t, s):
            return sum(4 if u in SHORT_TURNS else HB for u in range(t)) + s + 1

        def cols(w, c0, n=BLK):
            v = w.rearrange("(k p) c -> p k c", p=P)
            return [v[:, 0:8, bass.ds(c0, n)], v[:, 8:16, bass.ds(c0, n)]]

        def half(s):
            return ring[:, s, :, :]

        @block.sync
        def _(sp):
            def turn(t, halves):
                for s, src in enumerate(halves):
                    if src is None:
                        continue
                    if isinstance(t, int) and t == TURNS - 5 and s >= 4:
                        wait(sp, "recT_copied", 4)
                    elif isinstance(t, int) and t > 0:
                        wait(sp, "ring_used", used_count(t - 1, s))
                    elif not isinstance(t, int):
                        wait(sp, "ring_used", HB * (t - 1) + s + 1)
                    if isinstance(t, int) and t == 0 and s == 1:
                        wait(sp, "small_loads_sent")
                    dst = half(s)
                    if src.shape[1] == CMP_LEN:
                        dst = ring[:, s, :, :].rearrange("p a b -> p (a b)").rearrange("p (a b) -> p a b", a=CMP_LEN)
                    sp.dma_start(dst, src).then_inc(sig(f"landed{s}").sem, 16)

            ada, win, wout = a["w_ada"], a["w_in"], a["w_out"]

            def w1(w):
                return w.rearrange("(q p) o -> p q o", p=P)

            turn(0, cols(ada, 0) + cols(ada, BLK) + cols(ada, 2 * BLK))
            with sp.Fori(1, 3) as t:
                turn(t, cols(ada, t * (3 * BLK)) + cols(ada, t * (3 * BLK) + BLK) + cols(ada, t * (3 * BLK) + 2 * BLK))
            with sp.Fori(0, 4) as i:
                turn(i + 3, cols(ada, i * BLK + 9 * BLK) + cols(win, i * BLK + COL_HQ) + cols(win, i * BLK + COL_HI))
            turn(7, cols(win, 0) + cols(win, BLK))
            turn(8, cols(win, 2 * BLK) + cols(win, 3 * BLK))
            turn(9, cols(win, 4 * BLK) + [w1(a["cmp_w1_k"]), w1(a["cmp_w1_v"])])
            for t in range(10, 13):
                turn(t, [h for n in range(3) for h in cols(ada, (13 + 3 * (t - 10) + n) * BLK)])
            turn(13, cols(ada, 22 * BLK) + cols(ada, 23 * BLK) + cols(wout, 0))
            turn(14, cols(wout, BLK) + cols(wout, 2 * BLK) + cols(wout, 3 * BLK))

            wg = a["w_gate"].rearrange("e (k p) c -> e p k c", p=P)
            wu = a["w_up"].rearrange("e (k p) c -> e p k c", p=P)
            wd = a["w_down"].rearrange("e (k p) c -> e p k c", p=P)

            def expert_halves(e):
                g, u, d = (w[bass.ds(e, 1)].rearrange("o p k c -> p (o k) c") for w in (wg, wu, wd))
                return [g[:, 0:8, :], u[:, 0:8, :], g[:, 8:16, :], u[:, 8:16, :], d[:, 0:2, :], d[:, 2:4, :]]

            def dst_of(s):
                return half(s) if s < 4 else ring[:, s, :, :].rearrange("p (k a) b -> p k (a b)", k=2)

            for s, src in enumerate(expert_halves(0)):
                wait(sp, "ring_used", used_count(TURNS - 1, s))
                sp.dma_start(dst_of(s), src).then_inc(sig(f"expert_landed{s}").sem, 16)
            with sp.Fori(1, NE) as e:
                for s, src in enumerate(expert_halves(e)):
                    wait(sp, "expert_used", (e - 1) * HB + (s + 1))
                    sp.dma_start(dst_of(s), src).then_inc(sig(f"expert_landed{s}").sem, 16)

            wait(sp, "flag_ready")
            over = nc.sync.value_load(flag[0:1, 0:1], min_val=0, max_val=2 * S)
            wait(sp, "expert_used", NE * HB)
            with sp.If(over > 0):
                with sp.Fori(0, NE) as e:
                    sp.wait_ge(sig("dense_used").sem, e + 1)
                    for s, src in enumerate(expert_halves(e)):
                        sp.dma_start(dst_of(s), src).then_inc(sig(f"dense_landed{s}").sem, 16)
                    for s in range(HB):
                        sp.wait_ge(sig(f"dense_landed{s}").sem, e * 16 + 16)
                    sp.sem_inc(sig("dense_here").sem, 1)
            with sp.Else():
                sp.nop()
            wait(sp, "out0")
            sp.dma_start(out[0:P, :], x_t[:, 0, :]).then_inc(sig("stored").sem, 16)
            wait(sp, "out1")
            sp.dma_start(out[P:S, :], x_t[:, 1, :]).then_inc(sig("stored").sem, 16)
            wait(sp, "stored", 32)

        @block.tensor
        def _(pe):
            mm = nc.tensor.matmul
            tr = nc.tensor.transpose

            def landed(s, t):
                if s >= 4 and isinstance(t, int) and t > SHORT_TURNS[-1]:
                    t = t - len(SHORT_TURNS)
                pe.wait_ge(sig(f"landed{s}").sem, t * 16 + 16)

            def used(ins):
                ins.then_inc(sig("ring_used").sem, 1)

            wait(pe, "consts_in", 16)
            wait(pe, "vectors_in", 16 * 10)
            for v in range(2):
                last = tr(bank[0][:, v * P:(v + 1) * P], vrow[:, v, :], ident)
            inc(last, "vectors_T")

            def transpose_tokens(ready, src, tag):
                wait(pe, ready)
                for m in range(8):
                    if m >= 4:
                        wait(pe, f"{tag}_copied{m % 2}", (m - 4) // 2 + 1)
                    for j in range(4):
                        k, tt = 2 * m + j // 2, j % 2
                        last = tr(bank[1 + m % 4][:, j * P:(j + 1) * P], src[:, tt, k * P:(k + 1) * P], ident)
                    last.then_inc(sig(f"{tag}_T").sem, 1)

            wait(pe, "vec_ready")

            def ada_sum(t, slot, n, b=0):
                pe.wait_ge(sig("part_copied").sem, n) if not isinstance(n, int) or n > 0 else None
                for r in range(4):
                    if r % 2 == 0:
                        landed(2 * slot + r // 2, t)
                    for j in range(4):
                        k = 4 * r + j
                        last = mm(bank[b][32 * j:32 * j + 32, :], silc[:, k, :], ring[:, 2 * slot + k // 8, k % 8, :],
                                  start=r == 0, stop=r == 3, skip_group_check=True)
                    if r == 1:
                        used(last)
                used(last)

            def ada_cols(n):
                pe.wait_ge(sig("part_copied").sem, n + 1)
                if not isinstance(n, int) or n > 0:
                    pe.wait_ge(sig("mod_copied").sem, n)
                for j in range(4):
                    last = mm(bank[7][:, j * P:(j + 1) * P], part[:, j * P:(j + 1) * P], ones[:, :], start=True, stop=True)
                last.then_inc(sig("mod_cols").sem, 1)

            wait(pe, "silc_ready")
            wait(pe, "ones_ready")
            for slot in range(3):
                ada_sum(0, slot, slot)
                ada_cols(slot)
            transpose_tokens("xn_ready", x_t, "x1")
            with pe.Fori(1, 3) as t:
                for slot in range(3):
                    ada_sum(t, slot, t * 3 + slot)
                    ada_cols(t * 3 + slot)

            wait(pe, "h_ready_act")
            wait(pe, "h_ready_dve")
            wait(pe, "small_w_in", 16)
            for k in range(KT):
                last = mm(bank[5][0:N_GATES, 0:S], wg24[:, k, :], hT[:, k, :], start=k == 0, stop=k == KT - 1)
            inc(last, "gates_mm")


            def fill_feature_tile(s0, t, c, b, n, release, full=None):
                if n is not None:
                    pe.wait_ge(sig(f"taken{b}").sem, n + 1)
                for k in range(KT):
                    if k % 8 == 0:
                        landed(s0 + k // 8, t)
                    last = mm(bank[b][:, 0:S], ring[:, s0 + k // 8, k % 8, c:c + P], hT[:, k, :], start=k == 0, stop=k == KT - 1)
                    if release and k == 7:
                        used(last)
                if not release:
                    last.then_inc(sig(full or f"full{b}").sem, 1)
                else:
                    used(last)

            def fill_token_tile(s0, t, c, w, tt, b, n, release, src, full=None):
                if n is not None:
                    pe.wait_ge(sig(f"taken{b}").sem, n + 1)
                for k in range(KT):
                    if k % 8 == 0:
                        landed(s0 + k // 8, t)
                    last = mm(bank[b][:, 0:w], src(k)[:, tt * P:(tt + 1) * P], ring[:, s0 + k // 8, k % 8, c:c + w],
                              start=k == 0, stop=k == KT - 1)
                    if release and k == 7:
                        used(last)
                if not release:
                    last.then_inc(sig(full or f"full{b}").sem, 1)
                else:
                    used(last)

            def h_tile(k):
                return hT[:, k, :]

            def feature_block(s0, t, n):
                for m in range(4):
                    fill_feature_tile(s0, t, m * P, 1 + m, n, m == 3)

            with pe.Fori(0, 4) as i:
                t = i + 3
                ada_sum(t, 0, i + 9)
                feature_block(2, t, i)
                ada_cols(i + 9)
                for tt in range(TT):
                    fill_token_tile(4, t, 0, BLK, tt, 5 + tt, i, tt == 1, h_tile)
            wait(pe, "gates_sig")
            wait(pe, "part_copied", 13)
            for tt in range(TT):
                last = tr(bank[0][:, tt * 32:tt * 32 + N_GATES], gsig[:, tt * P:(tt + 1) * P], ident[0:N_GATES, 0:N_GATES])
            inc(last, "gates_T")

            def attention_tile(j):
                m, b = j % 4, TILE_BANKS[j % 4]
                if j >= 4:
                    wait(pe, "tile_taken", j - 3)
                elif b in (1, 2):
                    wait(pe, f"taken{b}", 5)
                elif b == 7:
                    wait(pe, "mod_copied", 13)
                else:
                    wait(pe, "gates_ready")
                t, s0 = SHORT_TURNS[j // 8], 2 * (j // 4 % 2)
                if j >= 12 and m >= 2:
                    fill_token_tile(s0, t, 2 * P, 2 * P, m - 2, b, None, m == 3, h_tile, "tile_full")
                else:
                    fill_feature_tile(s0, t, m * P, b, None, m == 3, "tile_full")

            def level(n):
                s = (LEVELS + [0])[n]
                if s > 0:
                    wait(pe, "factors", n + 1)
                z = zf[:, n % 2, :].rearrange("p (h t) -> p h t", h=NH)
                if n >= 2:
                    wait(pe, "products_used", (1, 1, 2, 2, 4, 5, 6)[n - 2])
                else:
                    for b in (3, 4) if n == 0 else (5, 6):
                        wait(pe, f"taken{b}", 5)
                if s == 128:
                    for h in range(NH):
                        last = mm(bank[3 + h // 4][:, (h % 4) * P:(h % 4 + 1) * P], z[:, h, 0:P], z[:, h, P:S], start=True, stop=True)
                elif s == 64:
                    for tt in range(TT):
                        for h in range(NH):
                            t0 = tt * P
                            last = mm(bank[5 + tt][0:64, h * 64:(h + 1) * 64], z[:, h, t0:t0 + 64], z[:, h, t0 + 64:t0 + P],
                                      start=True, stop=True)
                elif s == 32:
                    for h in range(NH):
                        for tt in range(TT):
                            for q in range(2):
                                t0 = tt * P + q * 64
                                last = mm(bank[3][64 * q:64 * q + 32, (tt * NH + h) * 32:(tt * NH + h + 1) * 32],
                                          z[:, h, t0:t0 + 32], z[:, h, t0 + 32:t0 + 64], start=True, stop=True,
                                          skip_group_check=True)
                else:
                    for h in range(NH):
                        for tt in range(TT):
                            for q in range(4):
                                t0 = tt * P + q * 32
                                kk = kT[:, h, t0:t0 + 32] if s == 0 else z[:, h, t0:t0 + 32]
                                qq = RT[:, THQ + h, t0:t0 + 32] if s == 0 else z[:, h, t0:t0 + 32]
                                last = mm(bank[4 + n % 3][32 * q:32 * q + 32, (tt * NH + h) * 32:(tt * NH + h + 1) * 32],
                                          kk, qq, start=True, stop=True, skip_group_check=True)
                last.then_inc(sig("products").sem, 1)

            def rec_out():
                wait(pe, "decay_ready")
                for tt in range(TT):
                    for h in range(NH):
                        o = bank[3 + 2 * tt + h // 4][:, (h % 4) * P:(h % 4 + 1) * P]
                        for jt in range(tt + 1):
                            aT = at[:, h, tt * P:(tt + 1) * P] if jt == 0 else at[:, h, S:S + P]
                            last = mm(o, aT, htok[:, h // 4, jt, (h % 4) * P:(h % 4 + 1) * P], start=jt == 0, stop=jt == tt)
                inc(last, "rec")

            def rec_T():
                for tt in range(TT):
                    for m in range(4):
                        wait(pe, "rec_gated", tt * NH + 4 * (m // 2) + 4)
                        for j in range(2):
                            h = 2 * m + j
                            last = tr(bank[3 + 2 * tt + m // 2][:, (m % 2) * 256 + j * P:(m % 2) * 256 + (j + 1) * P],
                                      orec[:, tt, h * P:(h + 1) * P], ident)
                        last.then_inc(sig("recT").sem, 1)

            after_tile = {LEVEL_TILES[n]: n for n in range(9)}
            for j in range(20):
                attention_tile(j)
                if j in after_tile:
                    level(after_tile[j])
                if j == REC_TILE:
                    rec_out()
            rec_T()

            wait(pe, "recT_copied", 4)
            for n, (c0, j) in enumerate(ROPE_TILES):
                wait(pe, "tile_taken", j + 1)
                if n >= 2:
                    wait(pe, "roped_mul", n - 1)
                last = mm(bank[3 + n % 2][:, :], cst[:, C_ROT:C_ROT + P], RT[:, c0:c0 + 2, :], start=True, stop=True)
                last.then_inc(sig("swapped").sem, 1)

            for v in range(2):
                landed(2 + v, 9)
                wait(pe, "blocks_ready", v + 1)
                blkv = RX[:, v * 1024:(v + 1) * 1024].rearrange("p (q c) -> p q c", q=CMP_LEN)
                w1v = ring[:, 2 + v, :, :].rearrange("p a b -> p (a b)").rearrange("p (q o) -> p q o", q=CMP_LEN)
                for r in range(8):
                    for j in range(4):
                        q = 4 * r + j
                        last = mm(bank[5 + v][32 * j:32 * j + 32, 0:P], blkv[:, q, :], w1v[:, q, :],
                                  start=r == 0, stop=r == 7, skip_group_check=True)
                used(last)
            def ada_block(t, slot, n):
                ada_sum(t, slot, n)
                ada_cols(n)

            ada_block(10, 0, 13)
            for v in range(2):
                wait(pe, "cmp_part", v + 1)
                last = mm(bank[5 + v][:, 256:256 + 160], RX[:, 2048 + v * P:2048 + (v + 1) * P], cst[:, C_SUM:C_SUM + 160], start=True, stop=True)
                last.then_inc(sig("cmp_hid").sem, 1)
            wait(pe, "cmp_silu")
            wait(pe, "cmp_w2_in", 32)
            wait(pe, "roped_mul", 7)
            last = mm(bank[3][:, 0:P], w2[:, 0, :], cmph[:, 0, 0:P], start=True, stop=True)
            for g in range(KVG):
                last = mm(bank[4][:, g * P:(g + 1) * P], cmph[:, 1, 16 * g:16 * g + P], w2[:, 1, :], start=True, stop=True)
            inc(last, "cmp_out")

            ada_block(10, 1, 14)

            wait(pe, "roped", 7)
            wait(pe, "tile_taken", 20)
            wait(pe, "kc_ready")
            wait(pe, "vc_ready")
            wait(pe, "gates_ready")
            for tt in range(TT):
                for h in range(NH):
                    last = mm(bank[2][:, (tt * NH + h) * 16:(tt * NH + h + 1) * 16], RT[:, TQ + h, tt * P:(tt + 1) * P],
                              kcT[:, h // 4, 0:16], start=True, stop=True)
            inc(last, "cmp_scores")

            def scores(h):
                g = h // 4
                for br, tk in enumerate((TKS, TKW)):
                    b = 3 + 2 * (h % 2) + br
                    if h >= 2:
                        wait(pe, "exps", 2 * (h - 2) + br + 1)
                    for tt in range(TT):
                        c0, n = (0, P) if tt == 0 else (P, 2 * P)
                        mm(bank[b][:, c0:c0 + n], RT[:, TQ + h, tt * P:(tt + 1) * P], RT[:, tk + g, 0:n], start=True, stop=False)
                        last = mm(bank[b][:, c0 + n - P:c0 + n], ident, cst[:, C_NEG:C_NEG + P], start=False, stop=True)
                    last.then_inc(sig("scores").sem, 1)

            def probs_T(h):
                for br in range(2):
                    wait(pe, "probs", 2 * h + br + 1)
                    if h > 0:
                        wait(pe, f"probsT_copied{br}", h)
                    if br == 1:
                        wait(pe, "mod_copied", 16 + h)
                    for c in range(3):
                        last = tr(bank[br + 1 if br == 0 else 7][:, c * P:(c + 1) * P], probs[:, h % 2, br, c * P:(c + 1) * P], ident)
                    last.then_inc(sig(f"probsT{br}").sem, 1)

            def values(h):
                g = h // 4
                if h >= 1:
                    wait(pe, "oT_copied", h)
                else:
                    wait(pe, "part_copied", 16)
                o = bank[0]
                mm(o[:, 0:S], vc4[32 * (h % 4):32 * (h % 4) + 32, g, :], pcT[32 * (h % 4):32 * (h % 4) + 32, g, :],
                   start=True, stop=False)
                for br in range(2):
                    wait(pe, f"probsT_copied{br}", h + 1)
                    v = vtok[:, br, :, g * P:(g + 1) * P]
                    mm(o[:, 0:S], v[:, 0, :], probsT[:, h % 2, br, 0:S], start=False, stop=False)
                    last = mm(o[:, P:S], v[:, 1, :], probsT[:, h % 2, br, S:S + P], start=False, stop=br == 1)
                last.then_inc(sig("oT").sem, 1)

            scores(0)
            ada_block(10, 2, 15)
            wait(pe, "pc_ready")
            for g in range(KVG):
                for tt in range(TT):
                    last = tr(bank[1][:, (2 * g + tt) * P:(2 * g + tt + 1) * P], pcp[:, tt, g * P:(g + 1) * P], ident)
            inc(last, "pcT")
            wait(pe, "pcT_copied")
            for h in range(NH):
                if h + 1 < NH:
                    scores(h + 1)
                probs_T(h)
                ada_sum(11 + h // 3, h % 3, 16 + h, b=2)
                if h > 0:
                    values(h - 1)
                wait(pe, "probsT_copied1", h + 1)
                ada_cols(16 + h)
            values(NH - 1)

            wait(pe, "oT_copied", NH)
            wait(pe, "probsT_copied0", NH)
            wait(pe, "part_copied", ADA_BLOCKS)

            def mixed(k):
                return RT[:, TQ + k, :] if k < NH else RT[:, THQ + k - NH, :]

            for n in range(4):
                t, s0 = (13, 4) if n == 0 else (14, 2 * (n - 1))
                for tt in range(TT):
                    b = 2 * n + tt
                    if b == 2:
                        wait(pe, "gains_ready")
                        inc(tr(bank[7][0:2 * KT, 0:P], gcol, ident), "gains_T")
                    if b == 7:
                        wait(pe, "gains_T_copied")
                    fill_token_tile(s0, t, 0, BLK, tt, b, None, tt == 1, mixed, "y_half")

            transpose_tokens("xn2_ready", xn2, "x2")
            wait(pe, "h2_ready_act")
            wait(pe, "h2_ready_dve")
            wait(pe, "router_in", 32)
            for k in range(KT):
                last = mm(bank[6][0:36, 0:S], wrt[:, k, :], h2T[:, k, :], start=k == 0, stop=k == KT - 1)
            inc(last, "logits_mm")
            wait(pe, "logits_biased")
            for tt in range(TT):
                last = tr(bank[7][:, tt * 64:tt * 64 + 36], part[0:36, tt * P:(tt + 1) * P], ident[0:36, 0:36])
            inc(last, "logits_T")
            wait(pe, "chosen")
            mm(bank[7][:, 128:160], cst[:, C_UP:C_UP + P], sel[:, 0, :], start=True, stop=True)
            mm(bank[7][:, 160:192], ones[:, :], sel[:, 0, :], start=True, stop=False)
            last = mm(bank[7][:, 160:192], cst[:, C_UP:C_UP + P], sel[:, 1, :], start=False, stop=True)
            inc(last, "ranks")
            wait(pe, "over_counted")
            inc(mm(bank[7][:, 192:193], ones[:, :], rt[:, 200:201], start=True, stop=True), "over_sum")

            def gather(n):
                pe.wait_ge(sig("onehot").sem, n)
                for m in range(4):
                    if m >= 3:
                        pe.wait_ge(sig("gathered_used").sem, (n - 1) * 4 + 1)
                    elif not isinstance(n, int):
                        pe.wait_ge(sig("gathered_used").sem, (n - 1) * 4)
                    for k in range(4 * m, 4 * m + 4):
                        for tt in range(TT):
                            last = mm(bank[GB[m % 3]][:, (k % 4) * P:(k % 4 + 1) * P], xn2[:, tt, k * P:(k + 1) * P],
                                      onehot[:, tt, :], start=tt == 0, stop=tt == TT - 1)
                    last.then_inc(sig("gathered").sem, 1)

            gather(1)
            wait(pe, "over_read")

            def scatter(n):
                pe.wait_ge(sig("ohwT_copied").sem, n)
                pe.wait_ge(sig("rows_copied").sem, n * 4 + 2)
                for i in range(8):
                    if i >= 4:
                        pe.wait_ge(sig("scatter_added").sem, (n - 1) * 8 + (i - 3))
                    tt, c = i // 4, i % 4
                    mm(bank[4 + i % 4][:, :], ohwT[:, tt * P:(tt + 1) * P], rows[:, c * BLK:(c + 1) * BLK],
                       start=True, stop=True).then_inc(sig("scattered").sem, 1)

            def pair(p, gather_next, scatter_last=True):
                for q in range(2):
                    e = p * 2 + q
                    if q == 0:
                        pe.wait_ge(sig("gathered_used").sem, p * 4 + 4)
                    for k in range(KT):
                        if k % 8 == 0:
                            for s in range(2):
                                pe.wait_ge(sig(f"expert_landed{2 * (k // 8) + s}").sem, e * 16 + 16)
                        for s in range(2):
                            last = mm(bank[0][64 * s:64 * s + 64, :], tokT[:, k, q * CAP:(q + 1) * CAP],
                                      ring[:, 2 * (k // 8) + s, k % 8, :], start=k == 0, stop=k == KT - 1, skip_group_check=True)
                            if k % 8 == 7:
                                last.then_inc(sig("expert_used").sem, 1)
                    if q == 0 and scatter_last:
                        scatter(p)
                    if q == 1 and scatter_last:
                        pe.wait_ge(sig("scatter_added").sem, p * 8)
                    if q == 1 and gather_next:
                        gather(p + 2)
                    if q == 1:
                        pe.wait_ge(sig("ohw").sem, p + 1)
                        for tt in range(TT):
                            last = tr(bank[7][:, tt * P:(tt + 1) * P], ohw[:, tt, :], ident)
                        last.then_inc(sig("ohwT").sem, 1)
                    pe.wait_ge(sig("hidden").sem, e + 1)
                    for f in range(4):
                        last = tr(bank[1][:, f * P:(f + 1) * P], hid[:, f * P:(f + 1) * P], ident)
                    last.then_inc(sig("hiddenT").sem, 1)
                    pe.wait_ge(sig("rows_copied").sem, e * 2 + 2)
                    pe.wait_ge(sig("hiddenT_copied").sem, e + 1)
                    for k in range(4):
                        if k % 2 == 0:
                            pe.wait_ge(sig(f"expert_landed{4 + k // 2}").sem, e * 16 + 16)
                        wdn = ring[:, 4 + k // 2, :, :].rearrange("p (k a) b -> p k (a b)", k=2)[:, k % 2, :]
                        for n in (0, 2, 1, 3):
                            last = mm(bank[2 + n % 2][64 * (n // 2):64 * (n // 2) + 64, :], hidT[:, k * CAP:(k + 1) * CAP],
                                      wdn[:, n * BLK:(n + 1) * BLK], start=k == 0, stop=k == 3, skip_group_check=True)
                        if k % 2 == 1:
                            last.then_inc(sig("expert_used").sem, 1)

            pair(0, True, False)
            with pe.Fori(1, NE // 2 - 1) as p:
                pair(p, True)
            pair(NE // 2 - 1, False)
            scatter(NE // 2)

            wait(pe, "flag_ready")
            over = nc.tensor.value_load(flag[0:1, 0:1], min_val=0, max_val=2 * S)
            with pe.If(over > 0):
                wait(pe, "rows_copied", 2 * NE + 2)
                wait(pe, "gathered_used", 4 * (NE // 2))
                wait(pe, "scatter_added", 8 * (NE // 2))
                pe.sem_inc(sig("dense_used").sem, 1)
                with pe.Fori(0, NE) as e:
                    pe.wait_ge(sig("dense_here").sem, e + 1)
                    for tt in range(TT):
                        c = e * 2 + tt
                        for s in range(2):
                            for k in range(KT):
                                last = mm(bank[s][:, :], h2T[:, k, tt * P:(tt + 1) * P], ring[:, 2 * (k // 8) + s, k % 8, :],
                                          start=k == 0, stop=k == KT - 1)
                        last.then_inc(sig("dense_gu").sem, 1)
                        pe.wait_ge(sig("dense_hid").sem, c + 1)
                        for f in range(4):
                            last = tr(bank[2][:, f * P:(f + 1) * P], dhid[:, f * P:(f + 1) * P], ident)
                        last.then_inc(sig("dense_T").sem, 1)
                        pe.wait_ge(sig("dense_T_copied").sem, c + 1)
                        for n in range(4):
                            for k in range(4):
                                wdn = ring[:, 4 + k // 2, :, :].rearrange("p (k a) b -> p k (a b)", k=2)[:, k % 2, :]
                                last = mm(bank[4 + n][:, :], dhidT[:, k * P:(k + 1) * P], wdn[:, n * BLK:(n + 1) * BLK],
                                          start=k == 0, stop=k == 3)
                        last.then_inc(sig("dense_down").sem, 1)
                        pe.wait_ge(sig("dense_added").sem, c + 1)
                    pe.sem_inc(sig("dense_used").sem, 1)
            with pe.Else():
                pe.nop()
            pe.nop()

        @block.scalar
        def _(act):
            lane = Lane(act, sig("act_steps"))
            do, settle = lane.do, lane.settle
            fn = nc.scalar.activation

            act.dma_start(cst[:, :], a["consts"]).then_inc(sig("consts_in").sem, 16)
            for v, rows_ in enumerate([
                [("c", V_C), ("b_ada", V_BADA), ("g_pre_mix", V_GPRE1)],
                [("g_pre_ffn", V_GPRE2), ("g_post_mix", V_GPOST1), ("g_post_ffn", V_GPOST1 + KT), ("lb0", V_LB0),
                 ("lb1", V_LB1), ("cmp_pe_k", V_PEK), ("cmp_pe_v", V_PEV)],
            ]):
                for name, r0 in rows_:
                    src = a[name]
                    act.dma_start(vrow[r0:r0 + src.shape[0], v, :], src).then_inc(sig("vectors_in").sem, 16)
            act.sem_inc(sig("small_loads_sent").sem, 1)
            for tt in range(TT):
                act.dma_start(x_t[:, tt, :], a["x"][tt * P:(tt + 1) * P, :]).then_inc(sig(f"x_in{tt}").sem, 16)
            act.dma_start(wg24[:, :, :], a["w_in"].rearrange("(k p) c -> p k c", p=P)[:, :, COL_GATES:COL_GATES + N_GATES])\
               .then_inc(sig("small_w_in").sem, 16)
            act.dma_start(brt[0:NGRP, :], a["b_group"]).then_inc(sig("brt_in").sem, 16)
            act.dma_start(brt[NGRP:36, :], a["b_router"]).then_inc(sig("brt_in").sem, 16)

            wait(act, "vec_ready")
            wait(act, "silc_zero")
            do(fn(silc[:, :, 0], vec[:, 0, V_C:V_C + KT], ACT.Silu), sig("silc_ready"))
            for tt in range(TT):
                wait(act, f"x_in{tt}", 16)
                do(fn(RH[:, tt * D:(tt + 1) * D], x_t[:, tt, :], ACT.Square, accum_out=st[:, tt:tt + 1]), sig("x_squares"))
            wait(act, "x_var")
            do(fn(st[:, 4:6], st[:, 2:4], ACT.Sqrt), sig("x_sd"))

            def copy_transposed(tag, dst):
                for m in range(0, 8, 2):
                    wait(act, f"{tag}_T", m + 1)
                    do(fn(dst[:, 2 * m:2 * m + 2, :], bank[1 + m % 4][:, :], ACT.Copy), sig(f"{tag}_copied0"))

            copy_transposed("x1", hT)
            def modulate(dst, which, ready):
                for k in (0, 1, 4, 5, 8, 9, 12, 13):
                    do(fn(dst[:, k, :], dst[:, k, :], ACT.Identity, bias=aff[:, 2 * which + 1, k:k + 1],
                          scale=aff[:, 2 * which, k:k + 1]), sig(ready) if k == 13 else None)

            wait(act, "aff1_ready")
            settle()
            modulate(hT, 0, "h_ready_act")
            for b in (1, 3):
                act.sem_inc(sig(f"taken{b}").sem, 1)
            wait(act, "gates_mm")
            do(fn(gsig, bank[5][0:N_GATES, 0:S], ACT.Sigmoid), sig("gates_sig"))
            settle()
            act.sem_inc(sig("taken5").sem, 1)
            wait(act, "lb_logits")
            do(fn(lbc[:, 0:2, :], lbc[:, 0:2, :], ACT.Exp), sig("lb_exp"))
            do(fn(sinT[:, :], sinT[:, :], ACT.Sin))
            do(fn(cosT[:, :], cosT[:, :], ACT.Sin), sig("trig"))



            def take(b, n, dst, src):
                act.wait_ge(sig(f"full{b}").sem, n + 1)
                fn(dst, src, ACT.Copy).then_inc(sig(f"taken{b}").sem, 1)

            def feature_tiles(base, n):
                for m in (0, 2):
                    take(1 + m, n, RT[:, bass.ds(base + m, 1), :], bank[1 + m][:, 0:S])

            with act.Fori(0, 4) as i:
                feature_tiles(i * 4 + THQ, i)
                take(5, i, htok[:, bass.ds(i, 1), 0, :], bank[5][:, :])

            def take_tile(j):
                blk, m = j // 4, j % 4
                if m == 3:
                    wait(act, "ring_used", used_count(SHORT_TURNS[j // 8], 2 * (blk % 2) + 1))
                else:
                    wait(act, "tile_full", 3 * blk + m + 1)
                dst = RT[:, j, :] if blk < 3 else RT[:, {3: TKS, 4: TKW}[blk] + m, :] if m < 2 else vtok[:, blk - 3, m - 2, :]
                do(fn(dst, bank[TILE_BANKS[m]][:, 0:S], ACT.Copy), sig("tile_taken"))

            for b in (1, 2, 3, 4):
                wait(act, f"taken{b}", 5)
            fT = RT[:, THF:THF + NH, :]
            do(fn(fT, fT, ACT.Sigmoid), sig("forget_sig"))
            do(fn(RT[:, THQ:THQ + NH, :], RT[:, THQ:THQ + NH, :], ACT.Silu))
            for b in (5, 6):
                wait(act, f"taken{b}", 5)
            do(fn(htok[:, 2:4, :, :], htok[:, 2:4, :, :], ACT.Silu), sig("q_and_g_silu"))
            wait(act, "forget_ready")
            do(fn(fT, fT, ACT.Ln), sig("forget_log"))
            exp_after = {LEVEL_TILES[n] - EXP_AHEAD: n for n in range(8)}
            for j in range(REC_TILE + 1):
                take_tile(j)
                if j in exp_after:
                    n = exp_after[j]
                    wait(act, "spans", n + 1)
                    do(fn(zf[:, n % 2, :], zf[:, n % 2, :], ACT.Exp), sig("decays"))
            wait(act, "rec")
            for tt in range(TT):
                for h in range(NH):
                    n = tt * NH + h
                    do(fn(scratch[:, n * P:(n + 1) * P], bank[3 + 2 * tt + h // 4][:, (h % 4) * P:(h % 4 + 1) * P], ACT.Square,
                          accum_out=st[:, n:n + 1]), sig("rec_squares") if n == 15 else None)
            wait(act, "rec_var")
            do(fn(st[:, 0:16], st[:, 0:16], ACT.Sqrt), sig("rec_sd"))
            for j in range(REC_TILE + 1, 20):
                take_tile(j)
            for tt in range(TT):
                wait(act, "recT", 4 * tt + 2)
                do(fn(RT[:, THQ:THQ + 4, tt * P:(tt + 1) * P], bank[3 + 2 * tt][:, :].rearrange("p (h t) -> p h t", h=4), ACT.Copy),
                   sig("recT_copied"))

            wait(act, "cmp_hid", 2)
            for v in range(2):
                do(fn(cmph[:, v, :], bank[5 + v][:, 256:416], ACT.Silu), sig("cmp_silu") if v else None)
            wait(act, "pc_shifted")
            do(fn(cmps, cmps, ACT.Exp, scale=SCALE), sig("pc_exp"))

            def exps(h):
                for br in range(2):
                    wait(act, "maxima", h + 1)
                    if h >= 2:
                        wait(act, f"probsT{br}", h - 1)
                    b = 3 + 2 * (h % 2) + br
                    for tt in range(TT):
                        c0, n = (0, P) if tt == 0 else (P, 2 * P)
                        s0 = 24 + 12 * (h % 2) + 2 * br + tt
                        do(fn(probs[:, h % 2, br, c0:c0 + n], bank[b][:, c0:c0 + n], ACT.Exp, bias=st[:, s0:s0 + 1],
                              scale=SCALE, accum_out=st[:, s0 + 4:s0 + 5]), sig("exps") if tt else None)

            exps(0)
            for h in range(NH):
                if h + 1 < NH:
                    exps(h + 1)
                wait(act, "probsT0", h + 1)
                do(fn(probsT[:, h % 2, 0, :], bank[1][:, 0:384], ACT.Copy), sig("probsT_copied0"))
                if h > 0:
                    wait(act, "oT", h)
                    do(fn(RT[:, TQ + h - 1, :], bank[0][:, 0:S], ACT.Copy), sig("oT_copied"))
            wait(act, "oT", NH)
            do(fn(RT[:, TQ + NH - 1, :], bank[0][:, 0:S], ACT.Copy), sig("oT_copied"))

            for n in range(4):
                for tt in range(TT):
                    wait(act, "y_copied", 2 * n + tt + 1)
                    c0 = 1024 + (2 * n + tt) * BLK
                    do(fn(RN[:, c0:c0 + BLK], y[:, tt, n * BLK:(n + 1) * BLK], ACT.Square, accum_out=st[:, 20 + 4 * tt + n:21 + 4 * tt + n]),
                       sig("y_squares") if n == 3 and tt == 1 else None)
            wait(act, "y_var")
            do(fn(st[:, 2:4], st[:, 2:4], ACT.Sqrt), sig("y_sd"))
            for tt in range(TT):
                wait(act, "x2_ready", tt + 1)
                do(fn(y[:, tt, :], x_t[:, tt, :], ACT.Square, accum_out=st[:, 4 + tt:5 + tt]), sig("x2_squares"))
            wait(act, "x2_var")
            do(fn(st[:, 4:6], st[:, 4:6], ACT.Sqrt), sig("x2_sd"))
            copy_transposed("x2", h2T)
            wait(act, "aff2_ready")
            settle()
            modulate(h2T, 1, "h2_ready_act")

            wait(act, "group_shift")
            for tt in range(TT):
                do(fn(rt[:, 208 + 4 * tt:212 + 4 * tt], rt[:, 36 * tt:36 * tt + 4], ACT.Exp, bias=rt[:, 216 + tt:217 + tt],
                      accum_out=rt[:, 218 + tt:219 + tt]))
            do(fn(rt[:, 220:222], rt[:, 220:222], ACT.Exp), sig("route_exp"))

            act.sem_inc(sig("rows_copied").sem, 1)

            with act.Fori(0, NE // 2) as p:
                for q in range(2):
                    e = p * 2 + q
                    act.wait_ge(sig("expert_used").sem, e * HB + 4)
                    fn(sil[64:128, :], bank[0][0:64, :], ACT.Silu).then_inc(sig("silu").sem, 1)
                    if q == 1:
                        act.wait_ge(sig("ohwT").sem, p + 1)
                        fn(ohwT, bank[7][:, 0:S], ACT.Copy).then_inc(sig("ohwT_copied").sem, 1)
                    act.wait_ge(sig("hiddenT").sem, e + 1)
                    fn(hidT.rearrange("p (f s) -> p f s", f=4), bank[1][:, :].rearrange("p (f s) -> p f s", f=4)[:, :, 0:CAP],
                       ACT.Copy).then_inc(sig("hiddenT_copied").sem, 1)
                    act.wait_ge(sig("expert_used").sem, e * HB + 6)
                    for n in range(2):
                        ins = fn(rows[64 * q:64 * q + 64, n * 1024:n * 1024 + BLK], bank[2][64 * n:64 * n + 64, :], ACT.Copy)
                    ins.then_inc(sig("rows_copied").sem, 1)

            wait(act, "flag_ready")
            over = nc.scalar.value_load(flag[0:1, 0:1], min_val=0, max_val=2 * S)
            with act.If(over > 0):
                with act.Fori(0, NE) as e:
                    for tt in range(TT):
                        act.wait_ge(sig("dense_gu").sem, e * 2 + (tt + 1))
                        fn(dsil[:, :], bank[0][:, :], ACT.Silu).then_inc(sig("dense_silu").sem, 1)
            with act.Else():
                act.nop()
            act.nop()
            wait(act, "ysum_ready")
            for tt in range(TT):
                do(fn(ring[:, 4, :, :].rearrange("p a b -> p (a b)")[:, tt * D:(tt + 1) * D], ysum[:, tt, :], ACT.Square,
                      accum_out=st[:, 8 + tt:9 + tt]), sig("ysum_squares"))
                wait(act, f"ysum_var{tt}")
                do(fn(st[:, 8 + tt:9 + tt], st[:, 8 + tt:9 + tt], ACT.Sqrt), sig(f"ysum_sd{tt}"))

        @block.gpsimd
        def _(pool):
            inc(nc.gpsimd.memset(silc[:, :, :], 0.0), "silc_zero")
            inc(nc.gpsimd.memset(ones[:, :], 1.0), "ones_ready")
            pool.dma_start(posi, a["positions"].to_broadcast([P, S])).then_inc(sig("positions_in").sem, 16)
            pool.dma_start(w2[:, 0, :], a["cmp_w2_k"]).then_inc(sig("cmp_w2_in").sem, 16)
            pool.dma_start(w2[:, 1, :], a["cmp_w2_v"]).then_inc(sig("cmp_w2_in").sem, 16)
            pool.dma_start(gnorm, a["hgrn_g_norm"].to_broadcast([P, 1024])).then_inc(sig("g_norm_in").sem, 16)
            wait(pool, "x1_T", 8)
            inc(nc.gpsimd.memset(at[:, :, :], 0.0), "at_zero")
            wait(pool, "gains_T_copied")
            pool.dma_start(gain_rows, part[0:2 * KT, 0:P]).then_inc(sig("gains_out").sem, 16)
            wait(pool, "probsT0", NH)
            wait(pool, "probsT1", NH)
            wait(pool, "oT", NH)
            wait(pool, "gains_out", 16)
            for n in range(2):
                src = gain_rows[n * KT:(n + 1) * KT, :].rearrange("(o k) p -> o (k p)", o=1).to_broadcast([P, D])
                pool.dma_start(RG[:, n, :], src).then_inc(sig("gains_in").sem, 16)
            for tt in range(TT):
                pool.dma_start(x_t[:, tt, :], a["x"][tt * P:(tt + 1) * P, :]).then_inc(sig(f"x_again{tt}").sem, 16)
            pool.dma_start(wrt[:, :, 0:NGRP], a["w_group"].rearrange("(k p) c -> p k c", p=P)).then_inc(sig("router_in").sem, 16)
            pool.dma_start(wrt[:, :, NGRP:36], a["w_router"].rearrange("(k p) c -> p k c", p=P)).then_inc(sig("router_in").sem, 16)
            wait(pool, "ring_used", used_count(TURNS - 1, HB - 1))
            inc(nc.gpsimd.memset(ysum, 0.0), "ysum_zero")

        @block.vector
        def _(dve):
            lane = Lane(dve, sig("dve_steps"))
            do, settle = lane.do, lane.settle
            v = nc.vector
            ts, tt_op, stt = v.tensor_scalar, v.tensor_tensor, v.scalar_tensor_tensor

            def step(ins, name=None):
                do(ins, sig(name) if name else None)
                settle()

            def rstd(dst, squares, n, var, sd):
                step(ts(dst, squares, 1.0 / n, EPS, ALU.mult, ALU.add), var)

            wait(dve, "vectors_T")
            do(v.tensor_copy(vec[:, :, :], bank[0][:, 0:2 * P]), sig("vec_ready"))
            for b in (2, 4, 6):
                dve.sem_inc(sig(f"taken{b}").sem, 1)
            def ada_part(n, used_value, b=0):
                dve.wait_ge(sig("ring_used").sem, used_value)
                if not isinstance(n, int) or n > 0:
                    dve.wait_ge(sig("mod_cols").sem, n)
                v.tensor_copy(part[:, :], bank[b][:, :]).then_inc(sig("part_copied").sem, 1)

            def ada_mod(n):
                dve.wait_ge(sig("mod_cols").sem, n + 1)
                v.tensor_copy(mod[:, bass.ds(n * 4, 4)], bank[7][:, :].rearrange("p (j c) -> p j c", j=4)[:, :, 0])\
                    .then_inc(sig("mod_copied").sem, 1)

            def copy_transposed(tag, dst):
                for m in range(1, 8, 2):
                    wait(dve, f"{tag}_T", m + 1)
                    do(v.tensor_copy(dst[:, 2 * m:2 * m + 2, :], bank[1 + m % 4][:, :]), sig(f"{tag}_copied1"))

            ada_part(0, 2)
            ada_mod(0)
            wait(dve, "x_squares", 2)
            step(ts(st[:, 2:4], st[:, 0:2], 1.0 / D, EPS, ALU.mult, ALU.add), "x_var")
            wait(dve, "x_sd")
            step(v.reciprocal(st[:, 6:8], st[:, 4:6]))
            ada_part(1, 4)
            ada_mod(1)
            for tt in range(TT):
                do(ts(x_t[:, tt, :], x_t[:, tt, :], st[:, 6 + tt:7 + tt], None, ALU.mult), sig("xn_ready") if tt else None)

            ada_part(2, 6)
            ada_mod(2)
            copy_transposed("x1", hT)
            with dve.Fori(1, 3) as t:
                for slot in range(3):
                    ada_part(t * 3 + slot, t * HB + (2 * slot + 2))
                    ada_mod(t * 3 + slot)

            def affine(which, gpre, c_shift, ready):
                bada = vec[:, 0, V_BADA:V_BADA + 6 * KT]
                scale, shift = aff[:, 2 * which, :], aff[:, 2 * which + 1, :]
                do(tt_op(shift, mod[:, c_shift:c_shift + KT], bada[:, c_shift:c_shift + KT], ALU.add))
                step(tt_op(scale, mod[:, c_shift + KT:c_shift + 2 * KT], bada[:, c_shift + KT:c_shift + 2 * KT], ALU.add))
                step(stt(scale, scale, 1.0, gpre, ALU.add, ALU.mult), ready)

            wait(dve, "mod_copied", 9)
            affine(0, vec[:, 0, V_GPRE1:V_GPRE1 + KT], 0, "aff1_ready")

            def modulate(dst, which, ready):
                for k in (2, 3, 6, 7, 10, 11, 14, 15):
                    do(ts(dst[:, k, :], dst[:, k, :], aff[:, 2 * which, k:k + 1], aff[:, 2 * which + 1, k:k + 1],
                          ALU.mult, ALU.add), sig(ready) if k == KT - 1 else None)

            modulate(hT, 0, "h_ready_dve")

            wait(dve, "positions_in", 16)
            settle()
            angf, turns, turni = RG[:, 0, 0:S], RG[:, 0, S:2 * S], RG[:, 0, 2 * S:3 * S].bitcast(I32)
            step(v.tensor_copy(angf, posi))
            step(ts(angf, angf, cst[:, C_INVF:C_INVF + 1], None, ALU.mult))
            for dst, quarter, shift in ((sinT, 0.0, 0.0), (cosT, 0.25, float(np.pi / 2))):
                step(ts(turns, angf, float(1.0 / (2 * np.pi)), quarter, ALU.mult, ALU.add))
                step(v.tensor_copy(turni, turns))
                step(v.tensor_copy(turns, turni))
                step(stt(dst[:, :], turns, -TWO_PI_HI, angf, ALU.mult, ALU.add))
                step(stt(dst[:, :], turns, -TWO_PI_MID, dst[:, :], ALU.mult, ALU.add))
                step(stt(dst[:, :], turns, -TWO_PI_LO, dst[:, :], ALU.mult, ALU.add))
                step(ts(dst[:, :], dst[:, :], shift, PI_SAFE, ALU.add, ALU.min))
                step(ts(dst[:, :], dst[:, :], -PI_SAFE, None, ALU.max), "angles" if quarter else None)

            l0, l1 = vec[:, 1, V_LB0:V_LB0 + NH], vec[:, 1, V_LB1:V_LB1 + NH]
            lb, lb1 = lbc[:, 0, :], lbc[:, 1, :]
            step(tt_op(lbc[:, 2, :], l0, l1, ALU.max))
            step(tt_op(lb, l0, lbc[:, 2, :], ALU.subtract))
            step(tt_op(lb1, l1, lbc[:, 2, :], ALU.subtract), "lb_logits")


            def take(b, value, dst, src):
                dve.wait_ge(sig("full2" if b == 2 else "ring_used").sem, value)
                v.tensor_copy(dst, src).then_inc(sig(f"taken{b}").sem, 1)

            def feature_tiles(base, n, t):
                take(2, n + 1, RT[:, bass.ds(base + 1, 1), :], bank[2][:, 0:S])
                take(4, t * HB + 4, RT[:, bass.ds(base + 3, 1), :], bank[4][:, 0:S])

            with dve.Fori(0, 4) as i:
                ada_part(i + 9, i * HB + (3 * HB + 2))
                feature_tiles(i * 4 + THQ, i, i + 3)
                ada_mod(i + 9)
                take(6, i * HB + (3 * HB + 6), htok[:, bass.ds(i, 1), 1, :], bank[6][:, :])

            wait(dve, "gates_T")
            step(v.tensor_copy(gts[:, :, :], bank[0][:, 0:64].rearrange("p (t c) -> p t c", t=TT)[:, :, 0:N_GATES]), "gates_ready")

            wait(dve, "lb_exp")
            step(tt_op(lbc[:, 2, :], lb, lb1, ALU.add))
            step(v.reciprocal(lbc[:, 2, :], lbc[:, 2, :]))
            step(tt_op(lb, lb, lbc[:, 2, :], ALU.mult))
            step(ts(lb1, lb, -1.0, 1.0, ALU.mult, ALU.add))
            wait(dve, "forget_sig")
            fT = RT[:, THF:THF + NH, :]
            for h in range(NH):
                do(ts(fT[:, h, :], fT[:, h, :], lb1[:, h:h + 1], lb[:, h:h + 1], ALU.mult, ALU.add))
            settle()
            step(ts(kT[:, :, :], fT, -1.0, 1.0, ALU.mult, ALU.add), "forget_ready")
            wait(dve, "forget_log")
            wait(dve, "ones_ready")
            for h in range(NH):
                do(v.tensor_tensor_scan(out=fT[:, h, :], data0=ones[:, 0:1].broadcast_to([P, S]), data1=fT[:, h, :],
                                        initial=0.0, op0=ALU.mult, op1=ALU.add))
            settle()
            wait(dve, "q_and_g_silu")
            wait(dve, "g_norm_in", 16)
            for tt in range(TT):
                g_t = htok[:, 2:4, tt, :]
                do(tt_op(g_t, g_t, gnorm.rearrange("p (i c) -> p i c", i=2), ALU.mult))

            bsum = fT.rearrange("p h t -> p (h t)")
            kflat = kT[:, :, :].rearrange("p h t -> p (h t)")
            qflat = RT[:, THQ:THQ + NH, :].rearrange("p h t -> p (h t)")

            def halves(w, s):
                w2_ = w.rearrange("p (x u s) -> p x u s", u=2, s=s)
                return w2_[:, :, 0, :], w2_[:, :, 1, :]

            def spans(n):
                s = LEVELS[n]
                zl, zr = halves(zf[:, n % 2, :], s)
                bl, br = halves(bsum, s)
                mid = bl[:, :, s - 1:s].broadcast_to([P, NH * S // (2 * s), s])
                if n >= 2:
                    wait(dve, "products", n - 1)
                do(tt_op(zl, mid, bl, ALU.subtract))
                do(tt_op(zr, br, mid, ALU.subtract), sig("spans"))

            def factors(n):
                s = LEVELS[n]
                zl, zr = halves(zf[:, n % 2, :], s)
                wait(dve, "decays", n + 1)
                do(tt_op(zl, zl, halves(kflat, s)[0], ALU.mult))
                do(tt_op(zr, zr, halves(qflat, s)[1], ALU.mult), sig("factors"))

            def products(n):
                wait(dve, "products", n + 1)
                if n == 0:
                    wait(dve, "at_zero")
                    for b in range(2):
                        do(v.tensor_copy(at[:, 4 * b:4 * b + 4, P:2 * P], bank[3 + b][:, :].rearrange("p (h i) -> p h i", h=4)),
                           sig("products_used") if b else None)
                elif n == 1:
                    for tt in range(TT):
                        do(v.tensor_copy(at[0:64, :, tt * S + 64:tt * S + P], bank[5 + tt][0:64, :].rearrange("p (h i) -> p h i", h=NH)),
                           sig("products_used") if tt else None)
                elif n == 2:
                    for tt in range(TT):
                        for q in range(2):
                            src = bank[3][64 * q:64 * q + 32, tt * 256:(tt + 1) * 256].rearrange("p (h i) -> p h i", h=NH)
                            c0 = tt * S + 64 * q + 32
                            do(v.tensor_copy(at[64 * q:64 * q + 32, :, c0:c0 + 32], src), sig("products_used") if tt and q else None)
                else:
                    c0 = C_LEV + 32 * (n - 3)
                    mask = cst[:, c0:c0 + 32].rearrange("p (o i) -> p o i", o=1).broadcast_to([P, 16, 32])
                    src = bank[4 + n % 3][:, :].rearrange("p (m i) -> p m i", m=16)
                    dst = (acc if n == 3 else acc_new).rearrange("p (m i) -> p m i", m=16)
                    step(tt_op(dst, src, mask, ALU.mult), "products_used")
                    if n > 3:
                        step(tt_op(acc, acc, acc_new, ALU.add))

            spans(0)
            for n in range(8):
                if n + 1 < 8:
                    spans(n + 1)
                factors(n)
                if n > 0:
                    products(n - 1)
            products(7)
            products(8)
            for tt in range(TT):
                for q in range(4):
                    c0 = tt * S + 32 * q
                    do(v.tensor_copy(at[32 * q:32 * q + 32, :, c0:c0 + 32],
                                     acc[32 * q:32 * q + 32, tt * 256:(tt + 1) * 256].rearrange("p (h i) -> p h i", h=NH)),
                       sig("decay_ready") if tt and q == 3 else None)
            wait(dve, "rec_squares")
            step(ts(st[:, 0:16], st[:, 0:16], 1.0 / HD, EPS, ALU.mult, ALU.add), "rec_var")
            wait(dve, "rec_sd")
            step(v.reciprocal(st[:, 0:16], st[:, 0:16]))
            for tt in range(TT):
                for h in range(NH):
                    n = tt * NH + h
                    do(stt(orec[:, tt, h * P:(h + 1) * P], bank[3 + 2 * tt + h // 4][:, (h % 4) * P:(h % 4 + 1) * P],
                           st[:, n:n + 1], htok[:, 2 + h // 4, tt, (h % 4) * P:(h % 4 + 1) * P], ALU.mult, ALU.mult), sig("rec_gated"))
            for tt in range(TT):
                wait(dve, "recT", 4 * tt + 4)
                do(v.tensor_copy(RT[:, THQ + 4:THQ + 8, tt * P:(tt + 1) * P], bank[4 + 2 * tt][:, :].rearrange("p (h t) -> p h t", h=4)),
                   sig("recT_copied"))

            wait(dve, "trig")
            sin2, cos2 = (w[:, :].rearrange("p (o t) -> p o t", o=1).broadcast_to([P, 2, S]) for w in (sinT, cosT))
            for n, (c0, j) in enumerate(ROPE_TILES):
                wait(dve, "tile_taken", j + 1)
                tmp = RX[:, 3072:3584].rearrange("p (a t) -> p a t", a=2)
                wait(dve, "swapped", n + 1)
                step(tt_op(tmp, bank[3 + n % 2][:, :].rearrange("p (a t) -> p a t", a=2), sin2, ALU.mult), "roped_mul")
                step(tt_op(RT[:, c0:c0 + 2, :], RT[:, c0:c0 + 2, :], cos2, ALU.mult))
                step(tt_op(RT[:, c0:c0 + 2, :], RT[:, c0:c0 + 2, :], tmp, ALU.add), "roped")

            wait(dve, "tile_taken", 12)
            for w, (src, pe0) in enumerate(((TKC, V_PEK), (TVC, V_PEV))):
                dst = RX[:, w * 1024:(w + 1) * 1024].rearrange("p (q g c) -> p q g c", q=CMP_LEN, g=KVG)
                step(v.memset(RX[:, w * 1024:(w + 1) * 1024], 0.0))
                for g in range(KVG):
                    strided = RT[:, src + g, :].rearrange("p (c q) -> p q c", q=CMP_STRIDE)
                    for hf in range(2):
                        pos = vec[:, 1, pe0 + 16 * hf:pe0 + 16 * hf + 16].rearrange("p (q o) -> p q o", o=1)\
                            .broadcast_to([P, CMP_STRIDE, NC_CMP])
                        do(tt_op(dst[:, 16 * hf:16 * hf + 16, g, 0:NC_CMP], strided[:, :, hf:hf + NC_CMP], pos, ALU.add),
                           sig("blocks_ready") if g == 1 and hf == 1 else None)
            def ada_block(n, t, slot):
                ada_part(n, used_count(t, 2 * slot + 1))
                ada_mod(n)

            for w in range(2):
                wait(dve, "ring_used", used_count(9, 2 + w))
                do(v.tensor_copy(RX[:, 2048 + w * P:2048 + (w + 1) * P], bank[5 + w][:, 0:P]), sig("cmp_part"))
            ada_block(13, 10, 0)
            wait(dve, "cmp_out")
            do(v.tensor_copy(kcT[:, :, :], bank[3][:, 0:32].rearrange("p (g c) -> p g c", g=KVG)), sig("kc_ready"))
            do(v.tensor_copy(vc4[:, :, :], bank[4][:, 0:2 * P].rearrange("p (g c) -> p g c", g=KVG)), sig("vc_ready"))

            ada_block(14, 10, 1)
            wait(dve, "cmp_scores")
            cs = cmps.rearrange("p (t h c) -> p t h c", t=TT, h=NH)
            cs2 = cmps.rearrange("p (n c) -> p n c", c=16)

            def per_block(c0):
                return cst[:, c0:c0 + 32].rearrange("p (t o c) -> p t o c", t=TT, o=1).broadcast_to([P, TT, NH, 16])

            def bcast(col):
                return st[:, col:col + 16].rearrange("p (n o) -> p n o", o=1).broadcast_to([P, 16, 16])

            step(tt_op(cs, bank[2][:, 0:256].rearrange("p (t h c) -> p t h c", t=TT, h=NH), per_block(C_CNEG), ALU.add))
            step(v.reduce_max(st[:, 48:64], cs2, AX))
            step(tt_op(cs2, cs2, bcast(48), ALU.subtract), "pc_shifted")
            wait(dve, "pc_exp")
            step(tt_op(cs, cs, per_block(C_C01), ALU.mult))
            step(v.reduce_sum(st[:, 48:64], cs2, AX))
            step(ts(st[:, 48:64], st[:, 48:64], 1e-30, None, ALU.max))
            step(v.reciprocal(st[:, 48:64], st[:, 48:64]))
            step(tt_op(st[:, 48:64].rearrange("p (t h) -> p t h", t=TT), st[:, 48:64].rearrange("p (t h) -> p t h", t=TT),
                       gts[:, :, :].rearrange("p t (h b) -> p t h b", b=3)[:, :, :, 0], ALU.mult))
            step(v.memset(pcp[:, :, :], 0.0))
            step(tt_op(pcp[:, :, :].rearrange("p t (h c) -> p (t h) c", c=32)[:, :, 0:16], cs2, bcast(48), ALU.mult), "pc_ready")
            ada_block(15, 10, 2)
            def maxima(h):
                s0 = 24 + 12 * (h % 2)
                for br in range(2):
                    wait(dve, "scores", 2 * h + br + 1)
                    b = bank[3 + 2 * (h % 2) + br]
                    for tt in range(TT):
                        c0, n = (0, P) if tt == 0 else (P, 2 * P)
                        do(v.tensor_reduce(st[:, s0 + 2 * br + tt:s0 + 2 * br + tt + 1], b[:, c0:c0 + n], AX, ALU.max, negate=True))
                settle()
                step(ts(st[:, s0:s0 + 4], st[:, s0:s0 + 4], SCALE, None, ALU.mult), "maxima")

            maxima(0)
            wait(dve, "pcT")
            do(v.tensor_copy(pcT[:, :, :], bank[1][:, :].rearrange("p (g t) -> p g t", g=KVG)), sig("pcT_copied"))
            for h in range(NH):
                if h + 1 < NH:
                    maxima(h + 1)
                if h > 0:
                    ada_mod(15 + h)
                s0 = 24 + 12 * (h % 2)
                wait(dve, "exps", 2 * h + 2)
                step(v.reciprocal(st[:, s0 + 8:s0 + 12], st[:, s0 + 4:s0 + 8]))
                step(tt_op(st[:, s0 + 8:s0 + 12].rearrange("p (b t) -> p b t", b=2), st[:, s0 + 8:s0 + 12].rearrange("p (b t) -> p b t", b=2),
                           gts[:, :, 3 * h + 1:3 * h + 3].rearrange("p t b -> p b t"), ALU.mult))
                for br in range(2):
                    for tt in range(TT):
                        c0, n = (0, P) if tt == 0 else (P, 2 * P)
                        w = probs[:, h % 2, br, c0:c0 + n]
                        do(ts(w, w, st[:, s0 + 8 + 2 * br + tt:s0 + 9 + 2 * br + tt], None, ALU.mult), sig("probs") if tt else None)
                wait(dve, "probsT1", h + 1)
                do(v.tensor_copy(probsT[:, h % 2, 1, :], bank[7][:, 0:384]), sig("probsT_copied1"))
                ada_part(16 + h, used_count(11 + h // 3, 2 * (h % 3) + 1), b=2)
            ada_mod(ADA_BLOCKS - 1)

            wait(dve, "mod_copied", ADA_BLOCKS)
            affine(1, vec[:, 1, V_GPRE2:V_GPRE2 + KT], 3 * KT, "aff2_ready")
            gain = gcol.rearrange("p (n k) -> p n k", n=2)
            both = mod[:, :].rearrange("p (n j) -> p n j", n=2)[:, :, 2 * KT:3 * KT]
            bada = vec[:, 0, V_BADA:V_BADA + 6 * KT].rearrange("p (n j) -> p n j", n=2)[:, :, 2 * KT:3 * KT]
            step(tt_op(gain, both, bada, ALU.add))
            step(tt_op(gain, gain, vec[:, 1, V_GPOST1:V_GPOST1 + 2 * KT].rearrange("p (n k) -> p n k", n=2), ALU.mult), "gains_ready")
            wait(dve, "gains_T")
            step(v.tensor_copy(part[0:2 * KT, 0:P], bank[7][0:2 * KT, 0:P]), "gains_T_copied")


            for n in range(4):
                for tt in range(TT):
                    if tt == 0:
                        wait(dve, "y_half", n + 1)
                    else:
                        wait(dve, "ring_used", used_count(13, 5) if n == 0 else used_count(14, 2 * n - 1))
                    do(v.tensor_copy(y[:, tt, n * BLK:(n + 1) * BLK], bank[2 * n + tt][:, :]), sig("y_copied"))
            wait(dve, "y_squares")
            step(v.reduce_sum(st[:, 2:4], st[:, 20:28].rearrange("p (t n) -> p t n", t=TT), AX))
            step(ts(st[:, 2:4], st[:, 2:4], 1.0 / D, EPS, ALU.mult, ALU.add), "y_var")
            wait(dve, "y_sd")
            step(v.reciprocal(st[:, 2:4], st[:, 2:4]))
            wait(dve, "gains_in", 32)
            for tt in range(TT):
                wait(dve, f"x_again{tt}", 16)
                step(stt(y[:, tt, :], y[:, tt, :], st[:, 2 + tt:3 + tt], RG[:, 0, :], ALU.mult, ALU.mult))
                step(tt_op(x_t[:, tt, :], x_t[:, tt, :], y[:, tt, :], ALU.add), "x2_ready")
            wait(dve, "x2_squares", 2)
            step(ts(st[:, 4:6], st[:, 4:6], 1.0 / D, EPS, ALU.mult, ALU.add), "x2_var")
            wait(dve, "x2_sd")
            step(v.reciprocal(st[:, 4:6], st[:, 4:6]))
            for tt in range(TT):
                do(ts(xn2[:, tt, :], x_t[:, tt, :], st[:, 4 + tt:5 + tt], None, ALU.mult), sig("xn2_ready") if tt else None)
            copy_transposed("x2", h2T)
            settle()
            modulate(h2T, 1, "h2_ready_dve")

            wait(dve, "logits_mm")
            wait(dve, "brt_in", 32)
            step(ts(part[0:36, 0:S], bank[6][0:36, 0:S], brt[:, 0:1], None, ALU.add), "logits_biased")
            wait(dve, "logits_T")
            step(v.tensor_copy(rt[:, 0:72].rearrange("p (t c) -> p t c", t=TT),
                               bank[7][:, 0:128].rearrange("p (t c) -> p t c", t=TT)[:, :, 0:36]))
            iota = cst[:, C_IOTA:C_IOTA + 64]
            step(v.memset(rt[:, 72:104], -3.0e38))
            top, sl = rt[:, 104:120], rt[:, 120:136]
            num = rt[:, 224:232]
            groups8 = rt[:, 72:88].rearrange("p (t c) -> p t c", t=TT)
            step(v.tensor_copy(groups8[:, :, 0:NGRP], rt[:, 0:72].rearrange("p (t c) -> p t c", t=TT)[:, :, 0:NGRP]))
            for tt in range(TT):
                do(v.max(top[:, 8 * tt:8 * tt + 8], groups8[:, tt, :]))
            settle()
            for tt in range(TT):
                do(v.max_index(rti[:, 8 * tt:8 * tt + 8], top[:, 8 * tt:8 * tt + 8], groups8[:, tt, :]))
            settle()
            two = top.rearrange("p (t c) -> p t c", t=TT)
            twoi = rti[:, :].rearrange("p (t c) -> p t c", t=TT)
            do(ts(rt[:, 216:218], two[:, :, 0], -1.0, None, ALU.mult))
            step(v.tensor_copy(num[:, 0:2], twoi[:, :, 0]))
            for tt in range(TT):
                le = rt[:, 36 * tt + 4:36 * tt + 36]
                step(ts(rt[:, 240:244], iota[:, 0:NGRP], num[:, tt:tt + 1], None, ALU.is_equal))
                step(ts(sl[:, 8 * tt:8 * tt + 8], le[:, 0:8], rt[:, 240:241], None, ALU.mult))
                for g in range(1, NGRP):
                    step(stt(sl[:, 8 * tt:8 * tt + 8], le[:, 8 * g:8 * g + 8], rt[:, 240 + g:241 + g], sl[:, 8 * tt:8 * tt + 8],
                             ALU.mult, ALU.add))
                step(v.max(top[:, 8 * tt:8 * tt + 8], sl[:, 8 * tt:8 * tt + 8]))
                step(v.max_index(rti[:, 8 * tt:8 * tt + 8], top[:, 8 * tt:8 * tt + 8], sl[:, 8 * tt:8 * tt + 8]))
            step(tt_op(rt[:, 220:222], two[:, :, 1], two[:, :, 0], ALU.subtract), "group_shift")
            for k in range(2):
                step(v.tensor_copy(num[:, 2 + 2 * k:4 + 2 * k], twoi[:, :, k]))
                step(stt(num[:, 2 + 2 * k:4 + 2 * k], num[:, 0:2], float(EPG), num[:, 2 + 2 * k:4 + 2 * k], ALU.mult, ALU.add))
            oh = onehots
            for tt in range(TT):
                for k in range(2):
                    do(ts(oh[:, tt, k, :], iota[:, 0:NE], num[:, 2 + 2 * k + tt:3 + 2 * k + tt], None, ALU.is_equal))
            settle()
            step(tt_op(sel[:, :, :], oh[:, :, 0, :], oh[:, :, 1, :], ALU.add), "chosen")
            wait(dve, "route_exp")
            step(v.reciprocal(rt[:, 218:220], rt[:, 218:220]))
            step(ts(rt[:, 222:224], rt[:, 220:222], 1.0, None, ALU.add))
            step(v.reciprocal(rt[:, 222:224], rt[:, 222:224]))
            step(tt_op(wk[:, :, 0], rt[:, 218:220], rt[:, 222:224], ALU.mult))
            step(tt_op(wk[:, :, 1], wk[:, :, 0], rt[:, 220:222], ALU.mult))
            wait(dve, "ranks")
            step(v.tensor_copy(rank[:, :, :], bank[7][:, 128:192].rearrange("p (t e) -> p t e", t=TT)))

            def onehot_pair(n, first):
                if not first:
                    dve.wait_ge(sig("gathered").sem, (n - 1) * 4)
                for tt in range(TT):
                    for q in range(2):
                        e = (n - 1) * 2 + q
                        ins = ts(onehot[:, tt, q * CAP:(q + 1) * CAP], iota, rank[:, tt, bass.ds(e, 1)], sel[:, tt, bass.ds(e, 1)],
                                 ALU.is_equal, ALU.mult)
                        if tt and q:
                            ins.then_inc(sig("onehot").sem, 1)

            onehot_pair(1, True)
            for tt in range(TT):
                step(ts(cw[:, tt, :], oh[:, tt, 0, :], wk[:, tt, 0:1], None, ALU.mult))
                step(stt(cw[:, tt, :], oh[:, tt, 1, :], wk[:, tt, 1:2], cw[:, tt, :], ALU.mult, ALU.add))
            over_rt = rt[:, 0:64].rearrange("p (t e) -> p t e", t=TT)
            step(stt(over_rt, rank[:, :, :], float(CAP), sel[:, :, :], ALU.is_ge, ALU.mult))
            step(v.reduce_sum(rt[:, 200:201], rt[:, 0:64], AX), "over_counted")
            step(stt(cwo[:, :, :], rank[:, :, :], float(CAP), cw, ALU.is_ge, ALU.mult))
            wait(dve, "over_sum")
            step(v.tensor_copy(flag[:, :], bank[7][:, 192:193]), "over_read")

            step(v.memset(hid[64:128, :], 0.0))
            dve.sem_inc(sig("rows_copied").sem, 1)
            dve.sem_inc(sig("flag_ready").sem, 1)

            def weighted_onehot(n):
                if not isinstance(n, int) or n > 1:
                    dve.wait_ge(sig("ohwT").sem, n - 1)
                for tt in range(TT):
                    for q in range(2):
                        e = (n - 1) * 2 + q
                        ins = ts(ohw[:, tt, q * CAP:(q + 1) * CAP], iota, rank[:, tt, bass.ds(e, 1)], cw[:, tt, bass.ds(e, 1)],
                                 ALU.is_equal, ALU.mult)
                ins.then_inc(sig("ohw").sem, 1)

            def add_scattered(n):
                for i in range(8):
                    dve.wait_ge(sig("scattered").sem, (n - 1) * 8 + (i + 1))
                    w = ysum[:, i // 4, (i % 4) * BLK:(i % 4 + 1) * BLK]
                    tt_op(w, w, bank[4 + i % 4][:, :], ALU.add).then_inc(sig("scatter_added").sem, 1)

            def tokens(n):
                for m in range(4):
                    dve.wait_ge(sig("gathered").sem, (n - 1) * 4 + (m + 1))
                    for k in range(4 * m, 4 * m + 4):
                        ins = ts(tokT[:, k, :], bank[GB[m % 3]][:, (k % 4) * P:(k % 4 + 1) * P], aff[:, 2, k:k + 1], aff[:, 3, k:k + 1],
                                 ALU.mult, ALU.add)
                    ins.then_inc(sig("gathered_used").sem, 1)

            def pair(p, gather_next, scatter_last=True):
                for q in range(2):
                    e = p * 2 + q
                    if q == 0:
                        weighted_onehot(p + 1)
                    if q == 1 and gather_next:
                        onehot_pair(p + 2, False)
                    dve.wait_ge(sig("silu").sem, e + 1)
                    tt_op(hid[0:64, :], bank[0][64:128, :], sil[64:128, :], ALU.mult).then_inc(sig("hidden").sem, 1)
                    if q == 0 and scatter_last:
                        add_scattered(p)
                    if q == 1 and gather_next:
                        tokens(p + 2)
                    dve.wait_ge(sig("expert_used").sem, e * HB + 6)
                    for n in range(2):
                        ins = v.tensor_copy(rows[64 * q:64 * q + 64, n * 1024 + BLK:(n + 1) * 1024], bank[3][64 * n:64 * n + 64, :])
                    ins.then_inc(sig("rows_copied").sem, 1)

            tokens(1)
            wait(dve, "ysum_zero")
            pair(0, True, False)
            with dve.Fori(1, NE // 2 - 1) as p:
                pair(p, True)
            pair(NE // 2 - 1, False)
            add_scattered(NE // 2)

            over = nc.vector.value_load(flag[0:1, 0:1], min_val=0, max_val=2 * S)
            with dve.If(over > 0):
                with dve.Fori(0, NE) as e:
                    for tt in range(TT):
                        c = e * 2 + tt
                        dve.wait_ge(sig("dense_silu").sem, c + 1)
                        stt(dhid[:, :], bank[1][:, :], cwo[:, tt, bass.ds(e, 1)], dsil[:, :], ALU.mult, ALU.mult)\
                            .then_inc(sig("dense_hid").sem, 1)
                        dve.wait_ge(sig("dense_T").sem, c + 1)
                        v.tensor_copy(dhidT[:, :], bank[2][:, :]).then_inc(sig("dense_T_copied").sem, 1)
                        dve.wait_ge(sig("dense_down").sem, c + 1)
                        for n in range(4):
                            w = ysum[:, tt, n * BLK:(n + 1) * BLK]
                            ins = tt_op(w, w, bank[4 + n][:, :], ALU.add)
                        ins.then_inc(sig("dense_added").sem, 1)
                dve.wait_ge(sig("dense_added").sem, 2 * NE)
            with dve.Else():
                dve.nop()
            dve.sem_inc(sig("ysum_ready").sem, 1)
            for tt in range(TT):
                r = st[:, 8 + tt:9 + tt]
                wait(dve, "ysum_squares", tt + 1)
                step(ts(r, r, 1.0 / D, EPS, ALU.mult, ALU.add), f"ysum_var{tt}")
                wait(dve, f"ysum_sd{tt}")
                step(v.reciprocal(r, r))
                step(stt(ysum[:, tt, :], ysum[:, tt, :], r, RG[:, 1, :], ALU.mult, ALU.mult))
                step(tt_op(x_t[:, tt, :], x_t[:, tt, :], ysum[:, tt, :], ALU.add), f"out{tt}")


def kernel(**inputs):
    import concourse.bacc as _bacc
    from concourse.bass_utils import run_bass_kernel_spmd as _run

    lay = {k: np.ascontiguousarray(v) for k, v in inputs.items()}
    arrays = {
        "x": lay["x"][0],
        "positions": lay["positions"],
        "w_ada": lay["w_ada"][0],
        "w_in": lay["w_in"][0],
        "w_out": lay["w_out"][0],
        "c": lay["c"].reshape(KT, P),
        "b_ada": lay["b_ada"].reshape(6 * KT, P),
        "lb0": lay["hgrn_lb_logits"][0].reshape(NH, P),
        "lb1": lay["hgrn_lb_logits"][1].reshape(NH, P),
        "hgrn_g_norm": lay["hgrn_g_norm"],
        "b_group": lay["b_group"].reshape(NGRP, 1),
        "b_router": lay["b_router"].reshape(NE, 1),
        "w_gate": lay["w_gate"].reshape(NE, D, FE),
        "w_up": lay["w_up"].reshape(NE, D, FE),
        "w_down": lay["w_down"].reshape(NE, FE, D),
        "consts": constant_table(),
    }
    for name in ("g_pre_mix", "g_post_mix", "g_pre_ffn", "g_post_ffn"):
        arrays[name] = lay[name].reshape(KT, P)
    for name in ("cmp_pe_k", "cmp_w1_k", "cmp_w2_k", "cmp_pe_v", "cmp_w1_v", "cmp_w2_v", "w_group", "w_router"):
        arrays[name] = lay[name][0]
    nc = _bacc.Bacc("TRN2", target_bir_lowering=False, num_devices=1)
    feeds, aps = {}, {}
    for name, arr in arrays.items():
        feeds[f"in_{name}"] = np.ascontiguousarray(arr)
        aps[name] = nc.dram_tensor(f"in_{name}", arr.shape, mybir.dt.from_np(arr.dtype), kind="ExternalInput").ap()
    out = nc.dram_tensor("out_0", (S, D), F32, kind="ExternalOutput").ap()
    block_kernel(nc, aps, out)
    r = _run(nc, [feeds], core_ids=[0])
    return r.results[0]["out_0"].reshape(1, S, D)
```

```python
from contextlib import ExitStack

import numpy as np

import concourse.bass as bass
from concourse import mybir

ALU = mybir.AluOpType
ACT = mybir.ActivationFunctionType
AX = mybir.AxisListType.X
F32 = mybir.dt.float32
I32 = mybir.dt.int32
U32 = mybir.dt.uint32

P = 128
D = 2048
S = 256
TT = S // P
KT = D // P
NH = 8
HD = 128
KVG = 2
BLK = 512
NC_CMP = 15
CMP_LEN, CMP_STRIDE = 32, 16
NGRP, EPG = 4, 8
NE = NGRP * EPG
FE = 512
CAP = 64
EPS = 1e-6
SCALE = float(HD) ** -0.5
NEG = -1.0e30
TWO_PI_HI, TWO_PI_MID, TWO_PI_LO = 6.28125, 0.0019350051879882812, 3.019916050561733e-07
PI_SAFE = 3.1415925

HB = 6
ADA_BLOCKS = 6 * D // BLK
COL_V_SLC, COL_HQ, COL_HI = 1792, 2584, 4632
COL_GATES = 2560
N_GATES = 3 * NH
TQ, TKC, TVC, THQ, THF, TKS, TKW = 0, 8, 10, 12, 20, 28, 30
LEVELS = [128, 64, 32, 16, 8, 4, 2, 1]
ROPE_TILES = [(TKC, 9), (0, 1), (2, 3), (4, 5), (6, 7), (TKS, 13), (TKW, 17)]
LEVEL_TILES = [3, 4, 5, 6, 7, 9, 10, 11, 12]
REC_TILE, REC_T_TILE = 13, 16
ROPE_AFTER = {17: (0, 1), 18: (2, 3, 4), 19: (5, 6)}
EXP_AHEAD = 3
TILE_BANKS = [1, 2, 0, 7]

C_ID, C_NEG, C_ROT, C_UP, C_LEV, C_CNEG, C_C01, C_IOTA, C_SUM, C_INVF = 0, 128, 256, 384, 512, 704, 736, 768, 832, 992
C_TWO, C_COLS = 993, 1029
V_C, V_BADA, V_GPRE1 = 0, 16, 112
V_GPRE2, V_GPOST1, V_LB0, V_LB1, V_PEK, V_PEV = 0, 16, 48, 56, 64, 96


def constant_table():
    t = np.zeros((P, C_COLS), np.float32)
    r = np.arange(P)
    t[:, C_ID:C_ID + P] = np.eye(P)
    t[:, C_NEG:C_NEG + P] = np.where(r[None, :] > r[:, None], NEG, 0.0)
    rot = np.zeros((P, P), np.float32)
    rot[r[64:], r[:64]] = -1.0
    rot[r[:64], r[64:]] = 1.0
    t[:, C_ROT:C_ROT + P] = rot
    t[:, C_UP:C_UP + P] = r[:, None] < r[None, :]
    j, i = (r % 32)[:, None], np.arange(32)[None, :]
    for n, s in enumerate([16, 8, 4, 2, 1]):
        t[:, C_LEV + 32 * n:C_LEV + 32 * n + 32] = (
            (j // (2 * s) == i // (2 * s)) & (j % (2 * s) < s) & (i % (2 * s) >= s))
    t[:, C_LEV + 160:C_LEV + 192] = i == j
    for tt in range(TT):
        tok = tt * P + r[:, None]
        c = np.arange(16)[None, :]
        seen = (c < NC_CMP) & (c * CMP_STRIDE + CMP_LEN - 1 <= tok)
        t[:, C_CNEG + 16 * tt:C_CNEG + 16 * tt + 16] = np.where(seen, 0.0, NEG)
        t[:, C_C01 + 16 * tt:C_C01 + 16 * tt + 16] = seen
    t[:, C_IOTA:C_IOTA + 64] = np.arange(64)[None, :]
    t[:, C_SUM:C_SUM + 160] = (r % 32)[:, None] == (np.arange(160) % 32)[None, :]
    t[:, C_TWO:C_TWO + 36] = r[:, None] % 64 == np.arange(36)[None, :]
    inv = (np.float32(10000.0) ** (-np.arange(0, HD, 2, dtype=np.float32) / np.float32(HD))).astype(np.float32)
    t[:, C_INVF] = np.concatenate([inv, inv])
    return t


STAGES = {
    "tensor_stages": ["vectors_T", "gates_mm", "gates_T", "rec", "cmp_out", "cmp_scores", "pcT", "gains_T", "logits_mm",
                      "logits_T", "ranks", "over_sum"],
    "scalar_stages": ["silc_ready", "x_sd", "lb_exp", "trig", "h_ready_act", "gates_sig", "forget_sig", "q_and_g_silu",
                      "forget_log", "rec_squares", "rec_sd", "cmp_silu", "pc_exp", "y_sd", "x2_sd",
                      "xn2_ready_act", "route_exp", "ysum_sd"],
    "vector_stages": ["vec_ready", "x_var", "xn_ready", "angles", "lb_logits", "aff1_ready", "h_ready_dve", "gates_ready",
                      "forget_ready", "decay_ready", "rec_var", "kc_ready", "vc_ready", "pc_shifted", "pc_ready",
                      "pcT_copied", "aff2_ready", "gains_ready", "gains_T_copied", "y_var", "x2_var", "x2_rstd", "xn2_ready",
                      "logits_biased", "group_shift", "chosen", "over_counted", "over_read", "ysum_var", "out0", "out1"],
    "gpsimd_stages": ["silc_zero", "ones_ready", "at_zero", "ysum_zero"],
}
STAGE_OF = {name: (sem, n + 1) for sem, names in STAGES.items() for n, name in enumerate(names)}


class Signal:

    def __init__(self, sem):
        self.sem = sem
        self.n = 0


class Lane:

    def __init__(self, eng, own):
        self.eng = eng
        self.own = own
        self.last = None

    def do(self, ins, sig=None):
        sig = sig or self.own
        ins.then_inc(sig.sem, 1)
        sig.n = sig.n + 1
        self.last = (sig, sig.n)

    def settle(self):
        sig, n = self.last
        self.eng.wait_ge(sig.sem, n)


def block_kernel(nc, a, out):
    gain_rows = nc.dram_tensor("gain_rows", [2 * KT, P], F32, kind="Internal").ap()

    with ExitStack() as ctx:
        def sb(name, shape, dt=F32):
            return ctx.enter_context(nc.sbuf_tensor(name, shape, dt))

        sems = {}

        def sig(name):
            if name in STAGE_OF:
                stages, n = STAGE_OF[name]
                counted = sig(stages)
                assert counted.n == n - 1, name
                return counted
            if name not in sems:
                sems[name] = Signal(ctx.enter_context(nc.semaphore(name)))
            return sems[name]

        def wait(eng, name, n=1):
            if name in STAGE_OF:
                name, n = STAGE_OF[name]
            eng.wait_ge(sig(name).sem, n)

        def inc(ins, name):
            counted = sig(name)
            ins.then_inc(counted.sem, 1)
            counted.n = counted.n + 1

        ring = sb("ring", [P, HB, 8, BLK])
        RX = sb("RX", [P, 4096])
        RH = sb("RH", [P, 4096])
        RT = sb("RT", [P, 32, 256])
        RN = sb("RN", [P, 5120])
        RG = sb("RG", [P, 2, D])
        cst = sb("cst", [P, C_COLS])
        vec = sb("vec", [P, 2, P])
        vrow = RN[:, 0:256].rearrange("p (a b) -> p a b", a=2)
        silc = sb("silc", [P, KT, 32])
        part = sb("part", [P, BLK])
        mod = sb("mod", [P, 6 * KT])
        ones = sb("ones", [P, P])
        st = sb("st", [P, 64])
        gts = sb("gts", [P, TT, N_GATES])
        aff = sb("aff", [P, 4, KT])
        lbc = sb("lbc", [P, 4, NH])
        brt = sb("brt", [36, 1])
        rti = sb("rti", [P, 16], U32)
        cwo = sb("cwo", [P, TT, NE])
        wk = sb("wk", [P, TT, 2])
        flag = sb("flag", [P, 1], I32)

        x_t = RX[:, :].rearrange("p (t d) -> p t d", t=TT)
        hT = RH[:, :].rearrange("p (k t) -> p k t", k=KT)
        ident = cst[:, C_ID:C_ID + P]
        cosT, sinT = RX[:, 3584:3840], RX[:, 3840:4096]
        wrt = RN[:, 0:576].rearrange("p (k c) -> p k c", k=KT)
        wg24 = RG[:, 0, 1024:1408].rearrange("p (k c) -> p k c", k=KT)
        silf = silc[:, :, :].rearrange("p k c -> p (k c)")
        rt = silf[:, 0:256]
        onehots = silf[:, 256:384].rearrange("p (t k e) -> p t k e", t=TT, k=2)
        sel = silf[:, 384:448].rearrange("p (t e) -> p t e", t=TT)
        rank = silf[:, 448:512].rearrange("p (t e) -> p t e", t=TT)
        vtok = RN[:, 0:1024].rearrange("p (b t c) -> p b t c", b=2, t=TT)
        probs = RX[:, 0:1536].rearrange("p (r b c) -> p r b c", r=2, b=2)
        probsT = RX[:, 1536:3072].rearrange("p (r b c) -> p r b c", r=2, b=2)
        pcT = RX[:, 3072:3584].rearrange("p (g t) -> p g t", g=KVG)
        pcp = RX[:, 3584:4096].rearrange("p (t c) -> p t c", t=TT)
        w2 = RG[:, 1, 1024:1280].rearrange("p (v o) -> p v o", v=2)
        cmph = RG[:, 1, 1280:1600].rearrange("p (v o) -> p v o", v=2)
        vc4 = RG[:, 1, 1600:1856].rearrange("p (g o) -> p g o", g=KVG)
        kcT = RG[:, 1, 1856:1888].rearrange("p (g c) -> p g c", g=KVG)
        gcol = RG[:, 1, 1888:1920]
        gnorm = RG[:, 1, 0:1024]
        cmps = RX[:, 2304:2560]
        gsig = RX[0:N_GATES, 3072:3072 + S]
        htok = RN[:, 1024:5120].rearrange("p (i t c) -> p i t c", i=4, t=TT)
        kT = RG[:, 0, :].rearrange("p (h t) -> p h t", h=NH)
        zf = ring[:, 5, :, :].rearrange("p a b -> p (a b)").rearrange("p (r c) -> p r c", r=2)
        slot4 = ring[:, 4, :, :].rearrange("p a b -> p (a b)")
        at = RX[:, 0:3072].rearrange("p (h c) -> p h c", h=NH)
        acc, acc_new, scratch = slot4[:, 0:512], slot4[:, 512:1024], slot4[:, 1024:3072]
        orec = zf[:, :, 0:1024]
        y = RH[:, :].rearrange("p (t d) -> p t d", t=TT)
        xn2 = y
        h2T = RT[:, 0:KT, :]
        ysum = RT[:, KT:2 * KT, :].rearrange("p a b -> p (a b)").rearrange("p (t d) -> p t d", t=TT)
        tokT = RN[:, 0:2048].rearrange("p (k s) -> p k s", k=KT)
        onehot = RN[:, 2048:2304].rearrange("p (t s) -> p t s", t=TT)
        hid = RN[:, 2304:2816]
        sil = RN[:, 2816:3328]
        hidT = RN[:, 3328:3584]
        ohw = RN[:, 3584:3840].rearrange("p (t s) -> p t s", t=TT)
        ohwT = RN[:, 3840:4096]
        rows = RG[:, 0, :]
        cw = part[:, 0:2 * NE].rearrange("p (t e) -> p t e", t=TT)
        dhid, dsil, dhidT = hid, sil, RN[:, 0:512]
        GB = [4, 5, 6]
        posi = RG[:, 0, 3 * S:4 * S].bitcast(I32)

        bank = [ctx.enter_context(nc.psum_tensor(f"bank{i}", [P, BLK], F32)) for i in range(8)]

        block = ctx.enter_context(nc.Block())

        ADA_DVE, ADA_LATE = 8, 16
        USED = {"HGRN": 16, "SHORT": 32, "FULL": 44}
        LAND = {"HGRN": (3, 3, 2), "SHORT": (11, 7), "FULL": (14, 10, 6)}
        OUT0 = ADA_BLOCKS - ADA_LATE

        def part_number(n):
            return n if not isinstance(n, int) or n <= ADA_DVE else n - (ADA_LATE - ADA_DVE)

        def cols(w, c0, n=BLK):
            v = w.rearrange("(k p) c -> p k c", p=P)
            return [v[:, 0:8, bass.ds(c0, n)], v[:, 8:16, bass.ds(c0, n)]]

        def half(s):
            return ring[:, s, :, :]

        @block.sync
        def _(sp):
            def send(s, src, name=None, value=0):
                if name:
                    wait(sp, name, value)
                dst = half(s)
                if src.shape[1] == CMP_LEN:
                    dst = ring[:, s, :, :].rearrange("p a b -> p (a b)").rearrange("p (a b) -> p a b", a=CMP_LEN)
                sp.dma_start(dst, src).then_inc(sig(f"landed{s}").sem, 16)

            ada, win, wout = a["w_ada"], a["w_in"], a["w_out"]

            def w1(w):
                return w.rearrange("(q p) o -> p q o", p=P)

            for s, src in enumerate(cols(ada, 0) + cols(ada, BLK) + cols(ada, 2 * BLK)):
                send(s, src, *(("small_loads_sent", 1) if s == 1 else ()))
            for n in range(3, ADA_DVE):
                for h, src in enumerate(cols(ada, n * BLK)):
                    send(2 * (n % 3) + h, src, "ring_used", 2 * (n - 3) + h + 1)

            def hgrn_blocks(i):
                first, used0 = isinstance(i, int), USED["HGRN"] - 4
                for h, src in enumerate(cols(ada, i * (2 * BLK) + ADA_DVE * BLK)):
                    if first:
                        send(h, src, "ring_used", 2 * 6 + h + 1)
                    else:
                        send(h, src, "ada_steps", i * 32 + (8 * (h + 1) - 16))
                for h, src in enumerate(cols(win, i * BLK + COL_HQ)):
                    send(2 + h, src, "ring_used", 2 * 7 + h + 1 if first else i * 4 + (used0 + h + 1))
                for h, src in enumerate(cols(ada, i * (2 * BLK) + (ADA_DVE + 1) * BLK)):
                    send(h, src, "ada_steps", i * 32 + 8 * (h + 1))
                for h, src in enumerate(cols(win, i * BLK + COL_HI)):
                    send(4 + h, src, "ring_used", 2 * 5 + h + 1 if first else i * 4 + (used0 + h + 3))

            hgrn_blocks(0)
            with sp.Fori(1, 4) as i:
                hgrn_blocks(i)
            short = [cols(win, n * BLK) for n in range(5)] + [[w1(a["cmp_w1_k"]), w1(a["cmp_w1_v"])]]
            for n, halves in enumerate(short):
                for h, src in enumerate(halves):
                    if n == 0:
                        send(h, src, "ada_steps", 32 * 4 - 16 + 8 * (h + 1))
                    elif n == 1:
                        send(2 + h, src, "ring_used", USED["SHORT"] - 4 + h + 1)
                    else:
                        send(2 * (n % 2) + h, src, "ring_used", USED["SHORT"] + 2 * (n - 2) + h + 1)
            full = [cols(ada, n * BLK) for n in range(ADA_LATE, ADA_BLOCKS)] + [cols(wout, n * BLK) for n in range(4)]
            for n, halves in enumerate(full):
                for h, src in enumerate(halves):
                    if n < 2:
                        send(2 * n + h, src, "ring_used", USED["FULL"] - 4 + 2 * n + h + 1)
                    elif n == 2:
                        send(4 + h, src, "recT_copied", 4)
                    else:
                        send(2 * (n % 3) + h, src, "ring_used", USED["FULL"] + 2 * (n - 3) + h + 1)

            wg = a["w_gate"].rearrange("e (k p) c -> e p k c", p=P)
            wu = a["w_up"].rearrange("e (k p) c -> e p k c", p=P)
            wd = a["w_down"].rearrange("e (k p) c -> e p k c", p=P)

            def expert_halves(e):
                g, u, d = (w[bass.ds(e, 1)].rearrange("o p k c -> p (o k) c") for w in (wg, wu, wd))
                return [g[:, 0:8, :], u[:, 0:8, :], g[:, 8:16, :], u[:, 8:16, :], d[:, 0:2, :], d[:, 2:4, :]]

            def dst_of(s):
                return half(s) if s < 4 else ring[:, s, :, :].rearrange("p (k a) b -> p k (a b)", k=2)

            for s, src in enumerate(expert_halves(0)):
                last = max(n for n in range(len(full)) if n % 3 == s // 2)
                wait(sp, "ring_used", USED["FULL"] + 2 * last + s % 2 + 1)
                sp.dma_start(dst_of(s), src).then_inc(sig(f"expert_landed{s}").sem, 16)
            with sp.Fori(1, NE) as e:
                for s, src in enumerate(expert_halves(e)):
                    wait(sp, "expert_used", (e - 1) * HB + (s + 1))
                    sp.dma_start(dst_of(s), src).then_inc(sig(f"expert_landed{s}").sem, 16)

            wait(sp, "flag_ready")
            over = nc.sync.value_load(flag[0:1, 0:1], min_val=0, max_val=2 * S)
            wait(sp, "expert_used", NE * HB)
            with sp.If(over > 0):
                with sp.Fori(0, NE) as e:
                    sp.wait_ge(sig("dense_used").sem, e + 1)
                    for s, src in enumerate(expert_halves(e)):
                        sp.dma_start(dst_of(s), src).then_inc(sig(f"dense_landed{s}").sem, 16)
                    for s in range(HB):
                        sp.wait_ge(sig(f"dense_landed{s}").sem, e * 16 + 16)
                    sp.sem_inc(sig("dense_here").sem, 1)
            with sp.Else():
                sp.nop()
            wait(sp, "out0")
            sp.dma_start(out[0:P, :], x_t[:, 0, :]).then_inc(sig("stored").sem, 16)
            wait(sp, "out1")
            sp.dma_start(out[P:S, :], x_t[:, 1, :]).then_inc(sig("stored").sem, 16)
            wait(sp, "stored", 32)

        @block.tensor
        def _(pe):
            mm = nc.tensor.matmul
            tr = nc.tensor.transpose

            def landed(s, t):
                pe.wait_ge(sig(f"landed{s}").sem, t * 16 + 16)

            def used(ins):
                ins.then_inc(sig("ring_used").sem, 1)

            wait(pe, "consts_in", 16)
            wait(pe, "vectors_in", 16 * 10)
            for v in range(2):
                last = tr(bank[0][:, v * P:(v + 1) * P], vrow[:, v, :], ident)
            inc(last, "vectors_T")

            def transpose_tokens(ready, src, tag):
                wait(pe, ready)
                for m in range(8):
                    if m >= 4:
                        wait(pe, f"{tag}_copied{m % 2}", (m - 4) // 2 + 1)
                    for j in range(4):
                        k, tt = 2 * m + j // 2, j % 2
                        last = tr(bank[1 + m % 4][:, j * P:(j + 1) * P], src[:, tt, k * P:(k + 1) * P], ident)
                    last.then_inc(sig(f"{tag}_T").sem, 1)

            wait(pe, "vec_ready")

            def ada_sum(t, slot, n, b=0):
                pe.wait_ge(sig("part_copied").sem, part_number(n)) if not isinstance(n, int) or n > 0 else None
                for r in range(4):
                    if r % 2 == 0:
                        landed(2 * slot + r // 2, t)
                    for j in range(4):
                        k = 4 * r + j
                        last = mm(bank[b][32 * j:32 * j + 32, :], silc[:, k, :], ring[:, 2 * slot + k // 8, k % 8, :],
                                  start=r == 0, stop=r == 3, skip_group_check=True)
                    if r == 1:
                        used(last)
                used(last)

            def ada_cols(n, steps=None):
                if steps is None:
                    pe.wait_ge(sig("part_copied").sem, part_number(n) + 1)
                else:
                    pe.wait_ge(sig("ada_steps").sem, steps)
                if not isinstance(n, int) or n > 0:
                    pe.wait_ge(sig("mod_copied").sem, n)
                for j in range(4):
                    last = mm(bank[7][:, j * P:(j + 1) * P], part[:, j * P:(j + 1) * P], ones[:, :], start=True, stop=True)
                last.then_inc(sig("mod_cols").sem, 1)

            wait(pe, "silc_ready")
            wait(pe, "ones_ready")
            for slot in range(3):
                ada_sum(0, slot, slot)
                ada_cols(slot)
            transpose_tokens("xn_ready", x_t, "x1")
            for n in range(3, ADA_DVE):
                ada_sum(n // 3, n % 3, n)
                ada_cols(n)

            wait(pe, "h_ready_act")
            wait(pe, "h_ready_dve")
            wait(pe, "small_w_in", 16)
            for k in range(KT):
                last = mm(bank[5][0:N_GATES, 0:S], wg24[:, k, :], hT[:, k, :], start=k == 0, stop=k == KT - 1)
            inc(last, "gates_mm")


            def fill_feature_tile(s0, t, c, b, n, release, full=None):
                if n is not None:
                    pe.wait_ge(sig(f"taken{b}").sem, n + 1)
                for k in range(KT):
                    if k % 8 == 0:
                        landed(s0 + k // 8, t)
                    last = mm(bank[b][:, 0:S], ring[:, s0 + k // 8, k % 8, c:c + P], hT[:, k, :], start=k == 0, stop=k == KT - 1)
                    if release and k == 7:
                        used(last)
                if not release:
                    last.then_inc(sig(full or f"full{b}").sem, 1)
                else:
                    used(last)

            def fill_token_tile(s0, t, c, w, tt, b, n, release, src, full=None):
                if n is not None:
                    pe.wait_ge(sig(f"taken{b}").sem, n + 1)
                for k in range(KT):
                    if k % 8 == 0:
                        landed(s0 + k // 8, t)
                    last = mm(bank[b][:, 0:w], src(k)[:, tt * P:(tt + 1) * P], ring[:, s0 + k // 8, k % 8, c:c + w],
                              start=k == 0, stop=k == KT - 1)
                    if release and k == 7:
                        used(last)
                if not release:
                    last.then_inc(sig(full or f"full{b}").sem, 1)
                else:
                    used(last)

            def h_tile(k):
                return hT[:, k, :]

            with pe.Fori(0, 4) as i:
                t = i + LAND["HGRN"][1]
                t2 = i + LAND["HGRN"][2]
                for m in range(4):
                    fill_feature_tile(2, t, m * P, 1 + m, i, m == 3)
                    if m == 1:
                        ada_cols(i * 2 + ADA_DVE, i * 32 + 16)
                for tt in range(TT):
                    fill_token_tile(4, t2, 0, BLK, tt, 5 + tt, i, tt == 1, h_tile)
                    if tt == 0:
                        ada_cols(i * 2 + (ADA_DVE + 1), i * 32 + 32)
            wait(pe, "gates_sig")
            wait(pe, "part_copied", ADA_DVE)
            for tt in range(TT):
                last = tr(bank[0][:, tt * 32:tt * 32 + N_GATES], gsig[:, tt * P:(tt + 1) * P], ident[0:N_GATES, 0:N_GATES])
            inc(last, "gates_T")

            def attention_tile(j):
                m, b = j % 4, TILE_BANKS[j % 4]
                if j >= 4:
                    wait(pe, "tile_taken", j - 3)
                elif b in (1, 2):
                    wait(pe, f"taken{b}", 5)
                elif b == 7:
                    wait(pe, "mod_copied", ADA_LATE)
                else:
                    wait(pe, "gates_ready")
                t, s0 = LAND["SHORT"][j // 4 % 2] + j // 8, 2 * (j // 4 % 2)
                if j >= 12 and m >= 2:
                    fill_token_tile(s0, t, 2 * P, 2 * P, m - 2, b, None, m == 3, h_tile, "tile_full")
                else:
                    fill_feature_tile(s0, t, m * P, b, None, m == 3, "tile_full")

            def level(n):
                s = (LEVELS + [0])[n]
                if s > 0:
                    wait(pe, "factors", n + 1)
                z = zf[:, n % 2, :].rearrange("p (h t) -> p h t", h=NH)
                if n >= 2:
                    wait(pe, "products_used", (1, 1, 2, 2, 4, 5, 6)[n - 2])
                else:
                    for b in (3, 4) if n == 0 else (5, 6):
                        wait(pe, f"taken{b}", 5)
                if s == 128:
                    for h in range(NH):
                        last = mm(bank[3 + h // 4][:, (h % 4) * P:(h % 4 + 1) * P], z[:, h, 0:P], z[:, h, P:S], start=True, stop=True)
                elif s == 64:
                    for tt in range(TT):
                        for h in range(NH):
                            t0 = tt * P
                            last = mm(bank[5 + tt][0:64, h * 64:(h + 1) * 64], z[:, h, t0:t0 + 64], z[:, h, t0 + 64:t0 + P],
                                      start=True, stop=True)
                elif s == 32:
                    for h in range(NH):
                        for tt in range(TT):
                            for q in range(2):
                                t0 = tt * P + q * 64
                                last = mm(bank[3][64 * q:64 * q + 32, (tt * NH + h) * 32:(tt * NH + h + 1) * 32],
                                          z[:, h, t0:t0 + 32], z[:, h, t0 + 32:t0 + 64], start=True, stop=True,
                                          skip_group_check=True)
                else:
                    for h in range(NH):
                        for tt in range(TT):
                            for q in range(4):
                                t0 = tt * P + q * 32
                                kk = kT[:, h, t0:t0 + 32] if s == 0 else z[:, h, t0:t0 + 32]
                                qq = RT[:, THQ + h, t0:t0 + 32] if s == 0 else z[:, h, t0:t0 + 32]
                                last = mm(bank[4 + n % 3][32 * q:32 * q + 32, (tt * NH + h) * 32:(tt * NH + h + 1) * 32],
                                          kk, qq, start=True, stop=True, skip_group_check=True)
                last.then_inc(sig("products").sem, 1)

            def rec_out():
                wait(pe, "decay_ready")
                for tt in range(TT):
                    for h in range(NH):
                        o = bank[3 + 2 * tt + h // 4][:, (h % 4) * P:(h % 4 + 1) * P]
                        for jt in range(tt + 1):
                            aT = at[:, h, tt * P:(tt + 1) * P] if jt == 0 else at[:, h, S:S + P]
                            last = mm(o, aT, htok[:, h // 4, jt, (h % 4) * P:(h % 4 + 1) * P], start=jt == 0, stop=jt == tt)
                inc(last, "rec")

            def rec_T():
                for tt in range(TT):
                    for m in range(4):
                        wait(pe, "rec_gated", tt * NH + 4 * (m // 2) + 4)
                        for j in range(2):
                            h = 2 * m + j
                            last = tr(bank[3 + 2 * tt + m // 2][:, (m % 2) * 256 + j * P:(m % 2) * 256 + (j + 1) * P],
                                      orec[:, tt, h * P:(h + 1) * P], ident)
                        last.then_inc(sig("recT").sem, 1)

            def rope(n):
                c0, j = ROPE_TILES[n]
                if n == 0:
                    wait(pe, "recT_copied", 4)
                wait(pe, "tile_taken", j + 1)
                if n >= 2:
                    wait(pe, "roped_mul", n - 1)
                last = mm(bank[3 + n % 2][:, :], cst[:, C_ROT:C_ROT + P], RT[:, c0:c0 + 2, :], start=True, stop=True)
                last.then_inc(sig("swapped").sem, 1)

            after_tile = {LEVEL_TILES[n]: n for n in range(9)}
            for j in range(20):
                attention_tile(j)
                if j in after_tile:
                    level(after_tile[j])
                if j == REC_TILE:
                    rec_out()
                if j == REC_T_TILE:
                    rec_T()
                for n in ROPE_AFTER.get(j, ()):
                    rope(n)

            wait(pe, "tile_taken", 20)
            for v in range(2):
                landed(2 + v, LAND["SHORT"][1] + 2)
                wait(pe, "blocks_ready", v + 1)
                blkv = RX[:, v * 1024:(v + 1) * 1024].rearrange("p (q c) -> p q c", q=CMP_LEN)
                w1v = ring[:, 2 + v, :, :].rearrange("p a b -> p (a b)").rearrange("p (q o) -> p q o", q=CMP_LEN)
                for r in range(8):
                    for j in range(4):
                        q = 4 * r + j
                        last = mm(bank[5 + v][32 * j:32 * j + 32, 0:P], blkv[:, q, :], w1v[:, q, :],
                                  start=r == 0, stop=r == 7, skip_group_check=True)
                used(last)
            def full_block(n):
                return LAND["FULL"][n % 3] + n // 3, n % 3

            def ada_block(n):
                ada_sum(*full_block(n), ADA_LATE + n)
                ada_cols(ADA_LATE + n)

            ada_block(0)
            for v in range(2):
                wait(pe, "cmp_part", v + 1)
                last = mm(bank[5 + v][:, 256:256 + 160], RX[:, 2048 + v * P:2048 + (v + 1) * P], cst[:, C_SUM:C_SUM + 160], start=True, stop=True)
                last.then_inc(sig("cmp_hid").sem, 1)
            wait(pe, "cmp_silu")
            wait(pe, "cmp_w2_in", 32)
            wait(pe, "roped_mul", 7)
            last = mm(bank[3][:, 0:P], w2[:, 0, :], cmph[:, 0, 0:P], start=True, stop=True)
            for g in range(KVG):
                last = mm(bank[4][:, g * P:(g + 1) * P], cmph[:, 1, 16 * g:16 * g + P], w2[:, 1, :], start=True, stop=True)
            inc(last, "cmp_out")

            ada_block(1)

            wait(pe, "roped", 7)
            wait(pe, "tile_taken", 20)
            wait(pe, "kc_ready")
            wait(pe, "vc_ready")
            wait(pe, "gates_ready")
            for tt in range(TT):
                for h in range(NH):
                    last = mm(bank[2][:, (tt * NH + h) * 16:(tt * NH + h + 1) * 16], RT[:, TQ + h, tt * P:(tt + 1) * P],
                              kcT[:, h // 4, 0:16], start=True, stop=True)
            inc(last, "cmp_scores")

            def scores(h):
                g = h // 4
                for br, tk in enumerate((TKS, TKW)):
                    b = 3 + 2 * (h % 2) + br
                    if h >= 2:
                        wait(pe, "exps", 2 * (h - 2) + br + 1)
                    for tt in range(TT):
                        c0, n = (0, P) if tt == 0 else (P, 2 * P)
                        mm(bank[b][:, c0:c0 + n], RT[:, TQ + h, tt * P:(tt + 1) * P], RT[:, tk + g, 0:n], start=True, stop=False)
                        last = mm(bank[b][:, c0 + n - P:c0 + n], ident, cst[:, C_NEG:C_NEG + P], start=False, stop=True)
                    last.then_inc(sig("scores").sem, 1)

            def probs_T(h):
                for br in range(2):
                    wait(pe, "probs", 2 * h + br + 1)
                    if h > 0:
                        wait(pe, f"probsT_copied{br}", h)
                    if br == 1:
                        wait(pe, "mod_copied", min(ADA_LATE + 3 + h, ADA_BLOCKS))
                    for c in range(3):
                        last = tr(bank[br + 1 if br == 0 else 7][:, c * P:(c + 1) * P], probs[:, h % 2, br, c * P:(c + 1) * P], ident)
                    last.then_inc(sig(f"probsT{br}").sem, 1)

            def values(h):
                g = h // 4
                if h >= 1:
                    wait(pe, "oT_copied", h)
                else:
                    wait(pe, "part_copied", part_number(ADA_LATE + 3))
                o = bank[0]
                mm(o[:, 0:S], vc4[32 * (h % 4):32 * (h % 4) + 32, g, :], pcT[32 * (h % 4):32 * (h % 4) + 32, g, :],
                   start=True, stop=False)
                for br in range(2):
                    wait(pe, f"probsT_copied{br}", h + 1)
                    v = vtok[:, br, :, g * P:(g + 1) * P]
                    mm(o[:, 0:S], v[:, 0, :], probsT[:, h % 2, br, 0:S], start=False, stop=False)
                    last = mm(o[:, P:S], v[:, 1, :], probsT[:, h % 2, br, S:S + P], start=False, stop=br == 1)
                last.then_inc(sig("oT").sem, 1)

            scores(0)
            ada_block(2)
            wait(pe, "pc_ready")
            for g in range(KVG):
                for tt in range(TT):
                    last = tr(bank[1][:, (2 * g + tt) * P:(2 * g + tt + 1) * P], pcp[:, tt, g * P:(g + 1) * P], ident)
            inc(last, "pcT")
            wait(pe, "pcT_copied")
            for h in range(NH):
                if h + 1 < NH:
                    scores(h + 1)
                if h > 0:
                    values(h - 1)
                probs_T(h)
                late = h + 3
                if late < OUT0:
                    ada_sum(*full_block(late), ADA_LATE + late, b=2)
                    wait(pe, "probsT_copied1", h + 1)
                    ada_cols(ADA_LATE + late)
            values(NH - 1)

            wait(pe, "oT_copied", NH)
            wait(pe, "probsT_copied0", NH)

            def mixed(k):
                return RT[:, TQ + k, :] if k < NH else RT[:, THQ + k - NH, :]

            for n in range(4):
                t, pair_ = full_block(OUT0 + n)
                for tt in range(TT):
                    b = 2 * n + tt
                    if b == 2:
                        wait(pe, "gains_ready")
                        inc(tr(bank[7][0:2 * KT, 0:P], gcol, ident), "gains_T")
                    if b == 7:
                        wait(pe, "gains_T_copied")
                    fill_token_tile(2 * pair_, t, 0, BLK, tt, b, None, tt == 1, mixed, "y_half")

            wait(pe, "xn2_ready_act")
            transpose_tokens("xn2_ready", xn2, "x2")
            for half_ in range(2):
                wait(pe, f"x2_copied{half_}", 4)
            wait(pe, "router_in", 32)
            for k in range(KT):
                r0 = 64 * (k % 2)
                last = mm(bank[6][r0:r0 + 36, 0:S], wrt[:, k, :], h2T[:, k, :], start=k < 2, stop=k >= KT - 2,
                          skip_group_check=True)
            inc(last, "logits_mm")
            wait(pe, "logits_biased")
            for tt in range(TT):
                last = mm(bank[7][:, tt * 64:tt * 64 + 36], part[:, tt * P:(tt + 1) * P], cst[:, C_TWO:C_TWO + 36], start=True, stop=True)
            inc(last, "logits_T")
            wait(pe, "chosen")
            mm(bank[7][:, 128:160], cst[:, C_UP:C_UP + P], sel[:, 0, :], start=True, stop=True)
            mm(bank[7][:, 160:192], ones[:, :], sel[:, 0, :], start=True, stop=False)
            last = mm(bank[7][:, 160:192], cst[:, C_UP:C_UP + P], sel[:, 1, :], start=False, stop=True)
            inc(last, "ranks")

            def gather(n):
                pe.wait_ge(sig("onehot").sem, n)
                for m in range(4):
                    if m >= 3:
                        pe.wait_ge(sig("gathered_used").sem, (n - 1) * 4 + 1)
                    elif not isinstance(n, int):
                        pe.wait_ge(sig("gathered_used").sem, (n - 1) * 4)
                    for k in range(4 * m, 4 * m + 4):
                        for tt in range(TT):
                            last = mm(bank[GB[m % 3]][:, (k % 4) * P:(k % 4 + 1) * P], xn2[:, tt, k * P:(k + 1) * P],
                                      onehot[:, tt, :], start=tt == 0, stop=tt == TT - 1)
                    last.then_inc(sig("gathered").sem, 1)

            gather(1)
            wait(pe, "over_counted")
            inc(mm(bank[7][:, 192:193], ones[:, :], rt[:, 200:201], start=True, stop=True), "over_sum")
            wait(pe, "over_read")

            def scatter(n):
                pe.wait_ge(sig("ohwT_copied").sem, n)
                pe.wait_ge(sig("rows_copied").sem, n * 4 + 2)
                for i in range(8):
                    if i >= 4:
                        pe.wait_ge(sig("scatter_added").sem, (n - 1) * 8 + (i - 3))
                    tt, c = i // 4, i % 4
                    mm(bank[4 + i % 4][:, :], ohwT[:, tt * P:(tt + 1) * P], rows[:, c * BLK:(c + 1) * BLK],
                       start=True, stop=True).then_inc(sig("scattered").sem, 1)

            def pair(p, gather_next, scatter_last=True):
                for q in range(2):
                    e = p * 2 + q
                    for k in range(KT):
                        if q == 0 and k % 4 == 0:
                            pe.wait_ge(sig("gathered_used").sem, p * 4 + (k // 4 + 1))
                        if k % 8 == 0:
                            for s in range(2):
                                pe.wait_ge(sig(f"expert_landed{2 * (k // 8) + s}").sem, e * 16 + 16)
                        for s in range(2):
                            last = mm(bank[0][64 * s:64 * s + 64, :], tokT[:, k, q * CAP:(q + 1) * CAP],
                                      ring[:, 2 * (k // 8) + s, k % 8, :], start=k == 0, stop=k == KT - 1, skip_group_check=True)
                            if k % 8 == 7:
                                last.then_inc(sig("expert_used").sem, 1)
                    if q == 0 and scatter_last:
                        scatter(p)
                    if q == 1 and scatter_last:
                        pe.wait_ge(sig("scatter_added").sem, p * 8)
                    if q == 1 and gather_next:
                        gather(p + 2)
                    if q == 1:
                        pe.wait_ge(sig("ohw").sem, p + 1)
                        for tt in range(TT):
                            last = tr(bank[7][:, tt * P:(tt + 1) * P], ohw[:, tt, :], ident)
                        last.then_inc(sig("ohwT").sem, 1)
                    pe.wait_ge(sig("hidden").sem, e + 1)
                    for f in range(4):
                        last = tr(bank[1][:, f * P:(f + 1) * P], hid[:, f * P:(f + 1) * P], ident)
                    last.then_inc(sig("hiddenT").sem, 1)
                    pe.wait_ge(sig("rows_copied").sem, e * 2 + 2)
                    pe.wait_ge(sig("hiddenT_copied").sem, e + 1)
                    for k in range(4):
                        if k % 2 == 0:
                            pe.wait_ge(sig(f"expert_landed{4 + k // 2}").sem, e * 16 + 16)
                        wdn = ring[:, 4 + k // 2, :, :].rearrange("p (k a) b -> p k (a b)", k=2)[:, k % 2, :]
                        for n in (0, 2, 1, 3):
                            last = mm(bank[2 + n % 2][64 * (n // 2):64 * (n // 2) + 64, :], hidT[:, k * CAP:(k + 1) * CAP],
                                      wdn[:, n * BLK:(n + 1) * BLK], start=k == 0, stop=k == 3, skip_group_check=True)
                        if k % 2 == 1:
                            last.then_inc(sig("expert_used").sem, 1)

            pair(0, True, False)
            with pe.Fori(1, NE // 2 - 1) as p:
                pair(p, True)
            pair(NE // 2 - 1, False)
            scatter(NE // 2)

            wait(pe, "flag_ready")
            over = nc.tensor.value_load(flag[0:1, 0:1], min_val=0, max_val=2 * S)
            with pe.If(over > 0):
                wait(pe, "rows_copied", 2 * NE + 2)
                wait(pe, "gathered_used", 4 * (NE // 2))
                wait(pe, "scatter_added", 8 * (NE // 2))
                pe.sem_inc(sig("dense_used").sem, 1)
                with pe.Fori(0, NE) as e:
                    pe.wait_ge(sig("dense_here").sem, e + 1)
                    for tt in range(TT):
                        c = e * 2 + tt
                        for s in range(2):
                            for k in range(KT):
                                last = mm(bank[s][:, :], h2T[:, k, tt * P:(tt + 1) * P], ring[:, 2 * (k // 8) + s, k % 8, :],
                                          start=k == 0, stop=k == KT - 1)
                        last.then_inc(sig("dense_gu").sem, 1)
                        pe.wait_ge(sig("dense_hid").sem, c + 1)
                        for f in range(4):
                            last = tr(bank[2][:, f * P:(f + 1) * P], dhid[:, f * P:(f + 1) * P], ident)
                        last.then_inc(sig("dense_T").sem, 1)
                        pe.wait_ge(sig("dense_T_copied").sem, c + 1)
                        for n in range(4):
                            for k in range(4):
                                wdn = ring[:, 4 + k // 2, :, :].rearrange("p (k a) b -> p k (a b)", k=2)[:, k % 2, :]
                                last = mm(bank[4 + n][:, :], dhidT[:, k * P:(k + 1) * P], wdn[:, n * BLK:(n + 1) * BLK],
                                          start=k == 0, stop=k == 3)
                        last.then_inc(sig("dense_down").sem, 1)
                        pe.wait_ge(sig("dense_added").sem, c + 1)
                    pe.sem_inc(sig("dense_used").sem, 1)
            with pe.Else():
                pe.nop()
            pe.nop()

        @block.scalar
        def _(act):
            lane = Lane(act, sig("act_steps"))
            do, settle = lane.do, lane.settle
            fn = nc.scalar.activation

            act.dma_start(cst[:, :], a["consts"]).then_inc(sig("consts_in").sem, 16)
            for v, rows_ in enumerate([
                [("c", V_C), ("b_ada", V_BADA), ("g_pre_mix", V_GPRE1)],
                [("g_pre_ffn", V_GPRE2), ("g_post_mix", V_GPOST1), ("g_post_ffn", V_GPOST1 + KT), ("lb0", V_LB0),
                 ("lb1", V_LB1), ("cmp_pe_k", V_PEK), ("cmp_pe_v", V_PEV)],
            ]):
                for name, r0 in rows_:
                    src = a[name]
                    act.dma_start(vrow[r0:r0 + src.shape[0], v, :], src).then_inc(sig("vectors_in").sem, 16)
            act.sem_inc(sig("small_loads_sent").sem, 1)
            for tt in range(TT):
                act.dma_start(x_t[:, tt, :], a["x"][tt * P:(tt + 1) * P, :]).then_inc(sig(f"x_in{tt}").sem, 16)
            act.dma_start(wg24[:, :, :], a["w_in"].rearrange("(k p) c -> p k c", p=P)[:, :, COL_GATES:COL_GATES + N_GATES])\
               .then_inc(sig("small_w_in").sem, 16)
            act.dma_start(brt[0:NGRP, :], a["b_group"]).then_inc(sig("brt_in").sem, 16)
            act.dma_start(brt[NGRP:36, :], a["b_router"]).then_inc(sig("brt_in").sem, 16)

            wait(act, "vec_ready")
            wait(act, "silc_zero")
            do(fn(silc[:, :, 0], vec[:, 0, V_C:V_C + KT], ACT.Silu), sig("silc_ready"))
            for tt in range(TT):
                wait(act, f"x_in{tt}", 16)
                do(fn(RH[:, tt * D:(tt + 1) * D], x_t[:, tt, :], ACT.Square, accum_out=st[:, tt:tt + 1]), sig("x_squares"))
            wait(act, "x_var")
            do(fn(st[:, 4:6], st[:, 2:4], ACT.Sqrt), sig("x_sd"))

            def copy_transposed(tag, dst):
                for m in range(0, 8, 2):
                    wait(act, f"{tag}_T", m + 1)
                    do(fn(dst[:, 2 * m:2 * m + 2, :], bank[1 + m % 4][:, :], ACT.Copy), sig(f"{tag}_copied0"))

            copy_transposed("x1", hT)
            def modulate(dst, which, ready):
                for k in (0, 1, 4, 5, 8, 9, 12, 13):
                    do(fn(dst[:, k, :], dst[:, k, :], ACT.Identity, bias=aff[:, 2 * which + 1, k:k + 1],
                          scale=aff[:, 2 * which, k:k + 1]), sig(ready) if k == 13 else None)

            wait(act, "lb_logits")
            do(fn(lbc[:, 0:2, :], lbc[:, 0:2, :], ACT.Exp), sig("lb_exp"))
            do(fn(sinT[:, :], sinT[:, :], ACT.Sin))
            do(fn(cosT[:, :], cosT[:, :], ACT.Sin), sig("trig"))
            wait(act, "aff1_ready")
            settle()
            modulate(hT, 0, "h_ready_act")
            for b in (1, 3):
                act.sem_inc(sig(f"taken{b}").sem, 1)
            wait(act, "gates_mm")
            do(fn(gsig, bank[5][0:N_GATES, 0:S], ACT.Sigmoid), sig("gates_sig"))
            settle()
            act.sem_inc(sig("taken5").sem, 1)


            def take(b, name, value, dst, src):
                act.wait_ge(sig(name).sem, value)
                fn(dst, src, ACT.Copy).then_inc(sig(f"taken{b}").sem, 1)

            def take_mod(n):
                act.wait_ge(sig("mod_cols").sem, n + 1)
                fn(mod[:, bass.ds(n * 4, 4)], bank[7][:, :].rearrange("p (j c) -> p j c", j=4)[:, :, 0], ACT.Copy)\
                    .then_inc(sig("mod_copied").sem, 1)

            with act.Fori(0, 4) as i:
                for m in range(4):
                    dst = RT[:, bass.ds(i * 4 + THQ + m, 1), :]
                    if m < 3:
                        take(1 + m, f"full{1 + m}", i + 1, dst, bank[1 + m][:, 0:S])
                    else:
                        take(4, "ring_used", i * 4 + (USED["HGRN"] + 2), dst, bank[4][:, 0:S])
                    if m == 1:
                        take_mod(i * 2 + ADA_DVE)
                take(5, "full5", i + 1, htok[:, bass.ds(i, 1), 0, :], bank[5][:, :])
                take_mod(i * 2 + (ADA_DVE + 1))
                take(6, "ring_used", i * 4 + (USED["HGRN"] + 4), htok[:, bass.ds(i, 1), 1, :], bank[6][:, :])

            def take_tile(j):
                blk, m = j // 4, j % 4
                if m == 3:
                    wait(act, "ring_used", USED["SHORT"] + 2 * blk + 2)
                else:
                    wait(act, "tile_full", 3 * blk + m + 1)
                dst = RT[:, j, :] if blk < 3 else RT[:, {3: TKS, 4: TKW}[blk] + m, :] if m < 2 else vtok[:, blk - 3, m - 2, :]
                do(fn(dst, bank[TILE_BANKS[m]][:, 0:S], ACT.Copy), sig("tile_taken"))

            for b in (1, 2, 3, 4):
                wait(act, f"taken{b}", 5)
            fT = RT[:, THF:THF + NH, :]
            do(fn(fT, fT, ACT.Sigmoid), sig("forget_sig"))
            do(fn(RT[:, THQ:THQ + NH, :], RT[:, THQ:THQ + NH, :], ACT.Silu))
            for b in (5, 6):
                wait(act, f"taken{b}", 5)
            do(fn(htok[:, 2:4, :, :], htok[:, 2:4, :, :], ACT.Silu), sig("q_and_g_silu"))
            wait(act, "forget_ready")
            do(fn(fT, fT, ACT.Ln), sig("forget_log"))
            exp_after = {LEVEL_TILES[n] - EXP_AHEAD: n for n in range(8)}
            for j in range(REC_TILE + 1):
                take_tile(j)
                if j in exp_after:
                    n = exp_after[j]
                    wait(act, "spans", n + 1)
                    do(fn(zf[:, n % 2, :], zf[:, n % 2, :], ACT.Exp), sig("decays"))
            wait(act, "rec")
            for tt in range(TT):
                for h in range(NH):
                    n = tt * NH + h
                    do(fn(scratch[:, n * P:(n + 1) * P], bank[3 + 2 * tt + h // 4][:, (h % 4) * P:(h % 4 + 1) * P], ACT.Square,
                          accum_out=st[:, n:n + 1]), sig("rec_squares") if n == 15 else None)
            wait(act, "rec_var")
            do(fn(st[:, 0:16], st[:, 0:16], ACT.Sqrt), sig("rec_sd"))
            for j in range(REC_TILE + 1, REC_T_TILE + 1):
                take_tile(j)
            for tt in range(TT):
                wait(act, "recT", 4 * tt + 2)
                do(fn(RT[:, THQ:THQ + 4, tt * P:(tt + 1) * P], bank[3 + 2 * tt][:, :].rearrange("p (h t) -> p h t", h=4), ACT.Copy),
                   sig("recT_copied"))
            for j in range(REC_T_TILE + 1, 20):
                take_tile(j)

            wait(act, "cmp_hid", 2)
            for v in range(2):
                do(fn(cmph[:, v, :], bank[5 + v][:, 256:416], ACT.Silu), sig("cmp_silu") if v else None)
            wait(act, "pc_shifted")
            do(fn(cmps, cmps, ACT.Exp, scale=SCALE), sig("pc_exp"))

            def exps(h):
                for br in range(2):
                    wait(act, "maxima", h + 1)
                    if h >= 2:
                        wait(act, f"probsT{br}", h - 1)
                    b = 3 + 2 * (h % 2) + br
                    for tt in range(TT):
                        c0, n = (0, P) if tt == 0 else (P, 2 * P)
                        s0 = 24 + 12 * (h % 2) + 2 * br + tt
                        do(fn(probs[:, h % 2, br, c0:c0 + n], bank[b][:, c0:c0 + n], ACT.Exp, bias=st[:, s0:s0 + 1],
                              scale=SCALE, accum_out=st[:, s0 + 4:s0 + 5]), sig("exps") if tt else None)

            exps(0)
            for h in range(NH):
                if h + 1 < NH:
                    exps(h + 1)
                if h > 0:
                    wait(act, "oT", h)
                    do(fn(RT[:, TQ + h - 1, :], bank[0][:, 0:S], ACT.Copy), sig("oT_copied"))
                wait(act, "probsT0", h + 1)
                do(fn(probsT[:, h % 2, 0, :], bank[1][:, 0:384], ACT.Copy), sig("probsT_copied0"))
            wait(act, "oT", NH)
            do(fn(RT[:, TQ + NH - 1, :], bank[0][:, 0:S], ACT.Copy), sig("oT_copied"))

            for n in range(4):
                for tt in range(TT):
                    if tt == 0:
                        wait(act, "y_half", n + 1)
                    else:
                        wait(act, "ring_used", USED["FULL"] + 2 * (OUT0 + n) + 2)
                    c0 = 1024 + (2 * n + tt) * BLK
                    do(fn(RN[:, c0:c0 + BLK], bank[2 * n + tt][:, :], ACT.Square, accum_out=st[:, 20 + 4 * tt + n:21 + 4 * tt + n]),
                       sig("y_squares"))
            wait(act, "y_var")
            do(fn(st[:, 2:4], st[:, 2:4], ACT.Sqrt), sig("y_sd"))
            for tt in range(TT):
                wait(act, "x2_ready", tt + 1)
                do(fn(y[:, tt, :], x_t[:, tt, :], ACT.Square, accum_out=st[:, 4 + tt:5 + tt]), sig("x2_squares"))
            wait(act, "x2_var")
            do(fn(st[:, 4:6], st[:, 4:6], ACT.Sqrt), sig("x2_sd"))
            wait(act, "x2_rstd")
            do(fn(xn2[:, 1, :], x_t[:, 1, :], ACT.Copy, scale=st[:, 5:6]), sig("xn2_ready_act"))
            wait(act, "aff2_ready")
            for m in range(0, 8, 2):
                wait(act, "x2_T", m + 1)
                for k in (2 * m, 2 * m + 1):
                    do(fn(h2T[:, k, :], bank[1 + m % 4][:, (k % 2) * S:(k % 2 + 1) * S], ACT.Identity, bias=aff[:, 3, k:k + 1],
                          scale=aff[:, 2, k:k + 1]), sig("x2_copied0") if k % 2 else None)

            wait(act, "group_shift")
            for tt in range(TT):
                do(fn(rt[:, 208 + 4 * tt:212 + 4 * tt], rt[:, 36 * tt:36 * tt + 4], ACT.Exp, bias=rt[:, 216 + tt:217 + tt],
                      accum_out=rt[:, 218 + tt:219 + tt]))
            do(fn(rt[:, 220:222], rt[:, 220:222], ACT.Exp), sig("route_exp"))

            act.sem_inc(sig("rows_copied").sem, 1)

            with act.Fori(0, NE // 2) as p:
                for q in range(2):
                    e = p * 2 + q
                    act.wait_ge(sig("expert_used").sem, e * HB + 4)
                    fn(sil[64:128, :], bank[0][0:64, :], ACT.Silu).then_inc(sig("silu").sem, 1)
                    if q == 1:
                        act.wait_ge(sig("ohwT").sem, p + 1)
                        fn(ohwT, bank[7][:, 0:S], ACT.Copy).then_inc(sig("ohwT_copied").sem, 1)
                    act.wait_ge(sig("hiddenT").sem, e + 1)
                    fn(hidT.rearrange("p (f s) -> p f s", f=4), bank[1][:, :].rearrange("p (f s) -> p f s", f=4)[:, :, 0:CAP],
                       ACT.Copy).then_inc(sig("hiddenT_copied").sem, 1)
                    act.wait_ge(sig("expert_used").sem, e * HB + 6)
                    for n in range(2):
                        ins = fn(rows[64 * q:64 * q + 64, n * 1024:n * 1024 + BLK], bank[2][64 * n:64 * n + 64, :], ACT.Copy)
                    ins.then_inc(sig("rows_copied").sem, 1)

            wait(act, "flag_ready")
            over = nc.scalar.value_load(flag[0:1, 0:1], min_val=0, max_val=2 * S)
            with act.If(over > 0):
                with act.Fori(0, NE) as e:
                    for tt in range(TT):
                        act.wait_ge(sig("dense_gu").sem, e * 2 + (tt + 1))
                        fn(dsil[:, :], bank[0][:, :], ACT.Silu).then_inc(sig("dense_silu").sem, 1)
            with act.Else():
                act.nop()
            act.nop()
            wait(act, "ysum_ready")
            for tt in range(TT):
                do(fn(ring[:, 4, :, :].rearrange("p a b -> p (a b)")[:, tt * D:(tt + 1) * D], ysum[:, tt, :], ACT.Square,
                      accum_out=st[:, 8 + tt:9 + tt]), sig("ysum_squares"))
            wait(act, "ysum_var")
            do(fn(st[:, 8:10], st[:, 8:10], ACT.Sqrt), sig("ysum_sd"))

        @block.gpsimd
        def _(pool):
            inc(nc.gpsimd.memset(silc[:, :, :], 0.0), "silc_zero")
            inc(nc.gpsimd.memset(ones[:, :], 1.0), "ones_ready")
            pool.dma_start(posi, a["positions"].to_broadcast([P, S])).then_inc(sig("positions_in").sem, 16)
            pool.dma_start(w2[:, 0, :], a["cmp_w2_k"]).then_inc(sig("cmp_w2_in").sem, 16)
            pool.dma_start(w2[:, 1, :], a["cmp_w2_v"]).then_inc(sig("cmp_w2_in").sem, 16)
            pool.dma_start(gnorm, a["hgrn_g_norm"].to_broadcast([P, 1024])).then_inc(sig("g_norm_in").sem, 16)
            wait(pool, "x1_T", 8)
            inc(nc.gpsimd.memset(at[:, :, :], 0.0), "at_zero")
            wait(pool, "gains_T_copied")
            pool.dma_start(gain_rows, part[0:2 * KT, 0:P]).then_inc(sig("gains_out").sem, 16)
            wait(pool, "probsT0", NH)
            wait(pool, "probsT1", NH)
            wait(pool, "oT", NH)
            wait(pool, "gains_out", 16)
            for n in range(2):
                src = gain_rows[n * KT:(n + 1) * KT, :].rearrange("(o k) p -> o (k p)", o=1).to_broadcast([P, D])
                pool.dma_start(RG[:, n, :], src).then_inc(sig("gains_in").sem, 16)
            for tt in range(TT):
                pool.dma_start(x_t[:, tt, :], a["x"][tt * P:(tt + 1) * P, :]).then_inc(sig(f"x_again{tt}").sem, 16)
            pool.dma_start(wrt[:, :, 0:NGRP], a["w_group"].rearrange("(k p) c -> p k c", p=P)).then_inc(sig("router_in").sem, 16)
            pool.dma_start(wrt[:, :, NGRP:36], a["w_router"].rearrange("(k p) c -> p k c", p=P)).then_inc(sig("router_in").sem, 16)
            wait(pool, "ring_used", USED["FULL"] + 2 * (OUT0 + 4))
            inc(nc.gpsimd.memset(ysum, 0.0), "ysum_zero")

        @block.vector
        def _(dve):
            lane = Lane(dve, sig("dve_steps"))
            do, settle = lane.do, lane.settle
            v = nc.vector
            ts, tt_op, stt = v.tensor_scalar, v.tensor_tensor, v.scalar_tensor_tensor

            def step(ins, name=None):
                do(ins, sig(name) if name else None)
                settle()

            wait(dve, "vectors_T")
            do(v.tensor_copy(vec[:, :, :], bank[0][:, 0:2 * P]), sig("vec_ready"))
            for b in (2, 4, 6):
                dve.sem_inc(sig(f"taken{b}").sem, 1)
            def ada_part(n, used_value, b=0):
                dve.wait_ge(sig("ring_used").sem, used_value)
                if not isinstance(n, int) or n > 0:
                    dve.wait_ge(sig("mod_cols").sem, n)
                v.tensor_copy(part[:, :], bank[b][:, :]).then_inc(sig("part_copied").sem, 1)

            def ada_mod(n):
                dve.wait_ge(sig("mod_cols").sem, n + 1)
                v.tensor_copy(mod[:, bass.ds(n * 4, 4)], bank[7][:, :].rearrange("p (j c) -> p j c", j=4)[:, :, 0])\
                    .then_inc(sig("mod_copied").sem, 1)

            def copy_transposed(tag, dst):
                for m in range(1, 8, 2):
                    wait(dve, f"{tag}_T", m + 1)
                    do(v.tensor_copy(dst[:, 2 * m:2 * m + 2, :], bank[1 + m % 4][:, :]), sig(f"{tag}_copied1"))

            ada_part(0, 2)
            ada_mod(0)
            wait(dve, "x_squares", 2)
            step(ts(st[:, 2:4], st[:, 0:2], 1.0 / D, EPS, ALU.mult, ALU.add), "x_var")
            wait(dve, "x_sd")
            step(v.reciprocal(st[:, 6:8], st[:, 4:6]))
            ada_part(1, 4)
            ada_mod(1)
            for tt in range(TT):
                do(ts(x_t[:, tt, :], x_t[:, tt, :], st[:, 6 + tt:7 + tt], None, ALU.mult), sig("xn_ready") if tt else None)

            ada_part(2, 6)
            ada_mod(2)
            copy_transposed("x1", hT)
            wait(dve, "positions_in", 16)
            settle()
            angf, turns, turni = RG[:, 0, 0:S], RG[:, 0, S:2 * S], RG[:, 0, 2 * S:3 * S].bitcast(I32)
            step(v.tensor_copy(angf, posi))
            step(ts(angf, angf, cst[:, C_INVF:C_INVF + 1], None, ALU.mult))
            for dst, quarter, shift in ((sinT, 0.0, 0.0), (cosT, 0.25, float(np.pi / 2))):
                step(ts(turns, angf, float(1.0 / (2 * np.pi)), quarter, ALU.mult, ALU.add))
                step(v.tensor_copy(turni, turns))
                step(v.tensor_copy(turns, turni))
                step(stt(dst[:, :], turns, -TWO_PI_HI, angf, ALU.mult, ALU.add))
                step(stt(dst[:, :], turns, -TWO_PI_MID, dst[:, :], ALU.mult, ALU.add))
                step(stt(dst[:, :], turns, -TWO_PI_LO, dst[:, :], ALU.mult, ALU.add))
                step(ts(dst[:, :], dst[:, :], shift, PI_SAFE, ALU.add, ALU.min))
                step(ts(dst[:, :], dst[:, :], -PI_SAFE, None, ALU.max), "angles" if quarter else None)

            l0, l1 = vec[:, 1, V_LB0:V_LB0 + NH], vec[:, 1, V_LB1:V_LB1 + NH]
            lb, lb1 = lbc[:, 0, :], lbc[:, 1, :]
            step(tt_op(lbc[:, 2, :], l0, l1, ALU.max))
            step(tt_op(lb, l0, lbc[:, 2, :], ALU.subtract))
            step(tt_op(lb1, l1, lbc[:, 2, :], ALU.subtract), "lb_logits")


            for n in range(3, ADA_DVE):
                ada_part(n, 2 * n + 2)
                ada_mod(n)

            def affine(which, gpre, c_shift, ready):
                bada = vec[:, 0, V_BADA:V_BADA + 6 * KT]
                scale, shift = aff[:, 2 * which, :], aff[:, 2 * which + 1, :]
                do(tt_op(shift, mod[:, c_shift:c_shift + KT], bada[:, c_shift:c_shift + KT], ALU.add))
                step(tt_op(scale, mod[:, c_shift + KT:c_shift + 2 * KT], bada[:, c_shift + KT:c_shift + 2 * KT], ALU.add))
                step(stt(scale, scale, 1.0, gpre, ALU.add, ALU.mult), ready)

            wait(dve, "mod_copied", ADA_DVE)
            affine(0, vec[:, 0, V_GPRE1:V_GPRE1 + KT], 0, "aff1_ready")

            def modulate(dst, which, ready):
                for k in (2, 3, 6, 7, 10, 11, 14, 15):
                    do(ts(dst[:, k, :], dst[:, k, :], aff[:, 2 * which, k:k + 1], aff[:, 2 * which + 1, k:k + 1],
                          ALU.mult, ALU.add), sig(ready) if k == KT - 1 else None)

            modulate(hT, 0, "h_ready_dve")

            with dve.Fori(0, 4) as i:
                for j in range(2):
                    t = i * 2 + (LAND["HGRN"][0] + j)
                    dve.wait_ge(sig("mod_cols").sem, i * 2 + (ADA_DVE + j))
                    for k in range(KT):
                        w = ring[:, k // 8, k % 8, :]
                        if k % 8 == 0:
                            dve.wait_ge(sig(f"landed{k // 8}").sem, t * 16 + 16)
                        if k == 0:
                            ins = ts(part[:, :], w, silc[:, k, 0:1], None, ALU.mult)
                        else:
                            dve.wait_ge(sig("ada_steps").sem, i * 32 + (16 * j + k))
                            ins = stt(part[:, :], w, silc[:, k, 0:1], part[:, :], ALU.mult, ALU.add)
                        ins.then_inc(sig("ada_steps").sem, 1)

            wait(dve, "gates_T")
            step(v.tensor_copy(gts[:, :, :], bank[0][:, 0:64].rearrange("p (t c) -> p t c", t=TT)[:, :, 0:N_GATES]), "gates_ready")

            wait(dve, "lb_exp")
            step(tt_op(lbc[:, 2, :], lb, lb1, ALU.add))
            step(v.reciprocal(lbc[:, 2, :], lbc[:, 2, :]))
            step(tt_op(lb, lb, lbc[:, 2, :], ALU.mult))
            step(ts(lb1, lb, -1.0, 1.0, ALU.mult, ALU.add))
            wait(dve, "forget_sig")
            fT = RT[:, THF:THF + NH, :]
            for h in range(NH):
                do(ts(fT[:, h, :], fT[:, h, :], lb1[:, h:h + 1], lb[:, h:h + 1], ALU.mult, ALU.add))
            settle()
            step(ts(kT[:, :, :], fT, -1.0, 1.0, ALU.mult, ALU.add), "forget_ready")
            wait(dve, "forget_log")
            wait(dve, "ones_ready")
            for h in range(NH):
                do(v.tensor_tensor_scan(out=fT[:, h, :], data0=ones[:, 0:1].broadcast_to([P, S]), data1=fT[:, h, :],
                                        initial=0.0, op0=ALU.mult, op1=ALU.add))
            settle()
            wait(dve, "q_and_g_silu")
            wait(dve, "g_norm_in", 16)
            for tt in range(TT):
                g_t = htok[:, 2:4, tt, :]
                do(tt_op(g_t, g_t, gnorm.rearrange("p (i c) -> p i c", i=2), ALU.mult))

            bsum = fT.rearrange("p h t -> p (h t)")
            kflat = kT[:, :, :].rearrange("p h t -> p (h t)")
            qflat = RT[:, THQ:THQ + NH, :].rearrange("p h t -> p (h t)")

            def halves(w, s):
                w2_ = w.rearrange("p (x u s) -> p x u s", u=2, s=s)
                return w2_[:, :, 0, :], w2_[:, :, 1, :]

            def spans(n):
                s = LEVELS[n]
                zl, zr = halves(zf[:, n % 2, :], s)
                bl, br = halves(bsum, s)
                mid = bl[:, :, s - 1:s].broadcast_to([P, NH * S // (2 * s), s])
                if n >= 2:
                    wait(dve, "products", n - 1)
                do(tt_op(zl, mid, bl, ALU.subtract))
                do(tt_op(zr, br, mid, ALU.subtract), sig("spans"))

            def factors(n):
                s = LEVELS[n]
                zl, zr = halves(zf[:, n % 2, :], s)
                wait(dve, "decays", n + 1)
                do(tt_op(zl, zl, halves(kflat, s)[0], ALU.mult))
                do(tt_op(zr, zr, halves(qflat, s)[1], ALU.mult), sig("factors"))

            def products(n):
                wait(dve, "products", n + 1)
                if n == 0:
                    wait(dve, "at_zero")
                    for b in range(2):
                        do(v.tensor_copy(at[:, 4 * b:4 * b + 4, P:2 * P], bank[3 + b][:, :].rearrange("p (h i) -> p h i", h=4)),
                           sig("products_used") if b else None)
                elif n == 1:
                    for tt in range(TT):
                        do(v.tensor_copy(at[0:64, :, tt * S + 64:tt * S + P], bank[5 + tt][0:64, :].rearrange("p (h i) -> p h i", h=NH)),
                           sig("products_used") if tt else None)
                elif n == 2:
                    for tt in range(TT):
                        for q in range(2):
                            src = bank[3][64 * q:64 * q + 32, tt * 256:(tt + 1) * 256].rearrange("p (h i) -> p h i", h=NH)
                            c0 = tt * S + 64 * q + 32
                            do(v.tensor_copy(at[64 * q:64 * q + 32, :, c0:c0 + 32], src), sig("products_used") if tt and q else None)
                else:
                    c0 = C_LEV + 32 * (n - 3)
                    mask = cst[:, c0:c0 + 32].rearrange("p (o i) -> p o i", o=1).broadcast_to([P, 16, 32])
                    src = bank[4 + n % 3][:, :].rearrange("p (m i) -> p m i", m=16)
                    dst = (acc if n == 3 else acc_new).rearrange("p (m i) -> p m i", m=16)
                    step(tt_op(dst, src, mask, ALU.mult), "products_used")
                    if n > 3:
                        step(tt_op(acc, acc, acc_new, ALU.add))

            spans(0)
            for n in range(8):
                if n + 1 < 8:
                    spans(n + 1)
                factors(n)
                if n > 0:
                    products(n - 1)
            products(7)
            products(8)
            for tt in range(TT):
                for q in range(4):
                    c0 = tt * S + 32 * q
                    do(v.tensor_copy(at[32 * q:32 * q + 32, :, c0:c0 + 32],
                                     acc[32 * q:32 * q + 32, tt * 256:(tt + 1) * 256].rearrange("p (h i) -> p h i", h=NH)),
                       sig("decay_ready") if tt and q == 3 else None)
            wait(dve, "rec_squares")
            step(ts(st[:, 0:16], st[:, 0:16], 1.0 / HD, EPS, ALU.mult, ALU.add), "rec_var")
            wait(dve, "rec_sd")
            step(v.reciprocal(st[:, 0:16], st[:, 0:16]))
            for tt in range(TT):
                for h in range(NH):
                    n = tt * NH + h
                    do(stt(orec[:, tt, h * P:(h + 1) * P], bank[3 + 2 * tt + h // 4][:, (h % 4) * P:(h % 4 + 1) * P],
                           st[:, n:n + 1], htok[:, 2 + h // 4, tt, (h % 4) * P:(h % 4 + 1) * P], ALU.mult, ALU.mult), sig("rec_gated"))
            for tt in range(TT):
                wait(dve, "recT", 4 * tt + 4)
                do(v.tensor_copy(RT[:, THQ + 4:THQ + 8, tt * P:(tt + 1) * P], bank[4 + 2 * tt][:, :].rearrange("p (h t) -> p h t", h=4)),
                   sig("recT_copied"))

            wait(dve, "trig")
            sin2, cos2 = (w[:, :].rearrange("p (o t) -> p o t", o=1).broadcast_to([P, 2, S]) for w in (sinT, cosT))
            for n, (c0, j) in enumerate(ROPE_TILES):
                wait(dve, "tile_taken", j + 1)
                tmp = RX[:, 3072:3584].rearrange("p (a t) -> p a t", a=2)
                wait(dve, "swapped", n + 1)
                step(tt_op(tmp, bank[3 + n % 2][:, :].rearrange("p (a t) -> p a t", a=2), sin2, ALU.mult), "roped_mul")
                step(tt_op(RT[:, c0:c0 + 2, :], RT[:, c0:c0 + 2, :], cos2, ALU.mult))
                step(tt_op(RT[:, c0:c0 + 2, :], RT[:, c0:c0 + 2, :], tmp, ALU.add), "roped")

            wait(dve, "tile_taken", 12)
            for w, (src, pe0) in enumerate(((TKC, V_PEK), (TVC, V_PEV))):
                dst = RX[:, w * 1024:(w + 1) * 1024].rearrange("p (q g c) -> p q g c", q=CMP_LEN, g=KVG)
                step(v.memset(dst[:, :, :, NC_CMP:16], 0.0))
                for g in range(KVG):
                    strided = RT[:, src + g, :].rearrange("p (c q) -> p q c", q=CMP_STRIDE)
                    for hf in range(2):
                        pos = vec[:, 1, pe0 + 16 * hf:pe0 + 16 * hf + 16].rearrange("p (q o) -> p q o", o=1)\
                            .broadcast_to([P, CMP_STRIDE, NC_CMP])
                        do(tt_op(dst[:, 16 * hf:16 * hf + 16, g, 0:NC_CMP], strided[:, :, hf:hf + NC_CMP], pos, ALU.add),
                           sig("blocks_ready") if g == 1 and hf == 1 else None)
            def ada_block(n):
                ada_part(ADA_LATE + n, USED["FULL"] + 2 * n + 2)
                ada_mod(ADA_LATE + n)

            for w in range(2):
                wait(dve, "ring_used", USED["SHORT"] + 10 + 1 + w)
                do(v.tensor_copy(RX[:, 2048 + w * P:2048 + (w + 1) * P], bank[5 + w][:, 0:P]), sig("cmp_part"))
            ada_block(0)
            wait(dve, "cmp_out")
            do(v.tensor_copy(kcT[:, :, :], bank[3][:, 0:32].rearrange("p (g c) -> p g c", g=KVG)), sig("kc_ready"))
            do(v.tensor_copy(vc4[:, :, :], bank[4][:, 0:2 * P].rearrange("p (g c) -> p g c", g=KVG)), sig("vc_ready"))

            ada_block(1)
            wait(dve, "cmp_scores")
            cs = cmps.rearrange("p (t h c) -> p t h c", t=TT, h=NH)
            cs2 = cmps.rearrange("p (n c) -> p n c", c=16)

            def per_block(c0):
                return cst[:, c0:c0 + 32].rearrange("p (t o c) -> p t o c", t=TT, o=1).broadcast_to([P, TT, NH, 16])

            def bcast(col):
                return st[:, col:col + 16].rearrange("p (n o) -> p n o", o=1).broadcast_to([P, 16, 16])

            step(tt_op(cs, bank[2][:, 0:256].rearrange("p (t h c) -> p t h c", t=TT, h=NH), per_block(C_CNEG), ALU.add))
            step(v.reduce_max(st[:, 48:64], cs2, AX))
            step(tt_op(cs2, cs2, bcast(48), ALU.subtract), "pc_shifted")
            wait(dve, "pc_exp")
            step(tt_op(cs, cs, per_block(C_C01), ALU.mult))
            step(v.reduce_sum(st[:, 48:64], cs2, AX))
            step(ts(st[:, 48:64], st[:, 48:64], 1e-30, None, ALU.max))
            step(v.reciprocal(st[:, 48:64], st[:, 48:64]))
            step(tt_op(st[:, 48:64].rearrange("p (t h) -> p t h", t=TT), st[:, 48:64].rearrange("p (t h) -> p t h", t=TT),
                       gts[:, :, :].rearrange("p t (h b) -> p t h b", b=3)[:, :, :, 0], ALU.mult))
            step(v.memset(pcp[:, :, :], 0.0))
            step(tt_op(pcp[:, :, :].rearrange("p t (h c) -> p (t h) c", c=32)[:, :, 0:16], cs2, bcast(48), ALU.mult), "pc_ready")
            ada_block(2)
            def maxima(h):
                s0 = 24 + 12 * (h % 2)
                for br in range(2):
                    wait(dve, "scores", 2 * h + br + 1)
                    b = bank[3 + 2 * (h % 2) + br]
                    for tt in range(TT):
                        c0, n = (0, P) if tt == 0 else (P, 2 * P)
                        do(v.tensor_reduce(st[:, s0 + 2 * br + tt:s0 + 2 * br + tt + 1], b[:, c0:c0 + n], AX, ALU.max, negate=True))
                settle()
                step(ts(st[:, s0:s0 + 4], st[:, s0:s0 + 4], SCALE, None, ALU.mult), "maxima")

            maxima(0)
            wait(dve, "pcT")
            do(v.tensor_copy(pcT[:, :, :], bank[1][:, :].rearrange("p (g t) -> p g t", g=KVG)), sig("pcT_copied"))
            for h in range(NH):
                late = h + 3
                if 3 < late <= OUT0:
                    ada_mod(ADA_LATE + late - 1)
                s0 = 24 + 12 * (h % 2)
                wait(dve, "exps", 2 * h + 2)
                step(v.reciprocal(st[:, s0 + 8:s0 + 12], st[:, s0 + 4:s0 + 8]))
                step(tt_op(st[:, s0 + 8:s0 + 12].rearrange("p (b t) -> p b t", b=2), st[:, s0 + 8:s0 + 12].rearrange("p (b t) -> p b t", b=2),
                           gts[:, :, 3 * h + 1:3 * h + 3].rearrange("p t b -> p b t"), ALU.mult))
                for br in range(2):
                    for tt in range(TT):
                        c0, n = (0, P) if tt == 0 else (P, 2 * P)
                        w = probs[:, h % 2, br, c0:c0 + n]
                        do(ts(w, w, st[:, s0 + 8 + 2 * br + tt:s0 + 9 + 2 * br + tt], None, ALU.mult), sig("probs") if tt else None)
                if h + 1 < NH:
                    maxima(h + 1)
                wait(dve, "probsT1", h + 1)
                do(v.tensor_copy(probsT[:, h % 2, 1, :], bank[7][:, 0:384]), sig("probsT_copied1"))
                if late < OUT0:
                    ada_part(ADA_LATE + late, USED["FULL"] + 2 * late + 2, b=2)

            wait(dve, "mod_copied", ADA_BLOCKS)
            affine(1, vec[:, 1, V_GPRE2:V_GPRE2 + KT], 3 * KT, "aff2_ready")
            gain = gcol.rearrange("p (n k) -> p n k", n=2)
            both = mod[:, :].rearrange("p (n j) -> p n j", n=2)[:, :, 2 * KT:3 * KT]
            bada = vec[:, 0, V_BADA:V_BADA + 6 * KT].rearrange("p (n j) -> p n j", n=2)[:, :, 2 * KT:3 * KT]
            step(tt_op(gain, both, bada, ALU.add))
            step(tt_op(gain, gain, vec[:, 1, V_GPOST1:V_GPOST1 + 2 * KT].rearrange("p (n k) -> p n k", n=2), ALU.mult), "gains_ready")
            wait(dve, "gains_T")
            step(v.tensor_copy(part[0:2 * KT, 0:P], bank[7][0:2 * KT, 0:P]), "gains_T_copied")


            wait(dve, "gains_in", 32)
            for n in range(4):
                for tt in range(TT):
                    wait(dve, "y_squares", 2 * n + tt + 1)
                    if n == 3 and tt == 1:
                        step(v.reduce_sum(st[:, 2:4], st[:, 20:28].rearrange("p (t n) -> p t n", t=TT), AX))
                        step(ts(st[:, 2:4], st[:, 2:4], 1.0 / D, EPS, ALU.mult, ALU.add), "y_var")
                    w = slice(n * BLK, (n + 1) * BLK)
                    do(tt_op(y[:, tt, w], bank[2 * n + tt][:, :], RG[:, 0, w], ALU.mult), sig("y_copied"))
            wait(dve, "y_sd")
            step(v.reciprocal(st[:, 2:4], st[:, 2:4]))
            for tt in range(TT):
                wait(dve, f"x_again{tt}", 16)
                do(stt(x_t[:, tt, :], y[:, tt, :], st[:, 2 + tt:3 + tt], x_t[:, tt, :], ALU.mult, ALU.add), sig("x2_ready"))
            wait(dve, "x2_squares", 2)
            step(ts(st[:, 4:6], st[:, 4:6], 1.0 / D, EPS, ALU.mult, ALU.add), "x2_var")
            wait(dve, "x2_sd")
            step(v.reciprocal(st[:, 4:6], st[:, 4:6]), "x2_rstd")
            do(ts(xn2[:, 0, :], x_t[:, 0, :], st[:, 4:5], None, ALU.mult), sig("xn2_ready"))
            for m in range(1, 8, 2):
                wait(dve, "x2_T", m + 1)
                for k in (2 * m, 2 * m + 1):
                    do(ts(h2T[:, k, :], bank[1 + m % 4][:, (k % 2) * S:(k % 2 + 1) * S], aff[:, 2, k:k + 1], aff[:, 3, k:k + 1],
                          ALU.mult, ALU.add), sig("x2_copied1") if k % 2 else None)

            wait(dve, "brt_in", 32)
            step(v.memset(part[:, 0:S], 0.0))
            wait(dve, "logits_mm")
            do(v.tensor_copy(part[64:100, 0:S], bank[6][64:100, 0:S]))
            step(ts(part[0:36, 0:S], bank[6][0:36, 0:S], brt[:, 0:1], None, ALU.add), "logits_biased")
            wait(dve, "logits_T")
            step(v.tensor_copy(rt[:, 0:72].rearrange("p (t c) -> p t c", t=TT),
                               bank[7][:, 0:128].rearrange("p (t c) -> p t c", t=TT)[:, :, 0:36]))
            iota = cst[:, C_IOTA:C_IOTA + 64]
            step(v.memset(rt[:, 72:104], -3.0e38))
            top, sl = rt[:, 104:120], rt[:, 120:136]
            num = rt[:, 224:232]
            groups8 = rt[:, 72:88].rearrange("p (t c) -> p t c", t=TT)
            step(v.tensor_copy(groups8[:, :, 0:NGRP], rt[:, 0:72].rearrange("p (t c) -> p t c", t=TT)[:, :, 0:NGRP]))
            for tt in range(TT):
                do(v.max(top[:, 8 * tt:8 * tt + 8], groups8[:, tt, :]))
            settle()
            for tt in range(TT):
                do(v.max_index(rti[:, 8 * tt:8 * tt + 8], top[:, 8 * tt:8 * tt + 8], groups8[:, tt, :]))
            settle()
            two = top.rearrange("p (t c) -> p t c", t=TT)
            twoi = rti[:, :].rearrange("p (t c) -> p t c", t=TT)
            do(ts(rt[:, 216:218], two[:, :, 0], -1.0, None, ALU.mult))
            step(v.tensor_copy(num[:, 0:2], twoi[:, :, 0]))
            le = [rt[:, 36 * tt + 4:36 * tt + 36] for tt in range(TT)]
            is_group = [rt[:, 240 + 4 * tt:244 + 4 * tt] for tt in range(TT)]
            chosen_le = [sl[:, 8 * tt:8 * tt + 8] for tt in range(TT)]
            for tt in range(TT):
                do(ts(is_group[tt], iota[:, 0:NGRP], num[:, tt:tt + 1], None, ALU.is_equal))
            settle()
            for g in range(NGRP):
                for tt in range(TT):
                    x8, here = le[tt][:, 8 * g:8 * g + 8], is_group[tt][:, g:g + 1]
                    do(ts(chosen_le[tt], x8, here, None, ALU.mult) if g == 0 else
                       stt(chosen_le[tt], x8, here, chosen_le[tt], ALU.mult, ALU.add))
                settle()
            for tt in range(TT):
                do(v.max(top[:, 8 * tt:8 * tt + 8], chosen_le[tt]))
            settle()
            for tt in range(TT):
                do(v.max_index(rti[:, 8 * tt:8 * tt + 8], top[:, 8 * tt:8 * tt + 8], chosen_le[tt]))
            settle()
            step(tt_op(rt[:, 220:222], two[:, :, 1], two[:, :, 0], ALU.subtract), "group_shift")
            for k in range(2):
                step(v.tensor_copy(num[:, 2 + 2 * k:4 + 2 * k], twoi[:, :, k]))
                step(stt(num[:, 2 + 2 * k:4 + 2 * k], num[:, 0:2], float(EPG), num[:, 2 + 2 * k:4 + 2 * k], ALU.mult, ALU.add))
            oh = onehots
            for tt in range(TT):
                for k in range(2):
                    do(ts(oh[:, tt, k, :], iota[:, 0:NE], num[:, 2 + 2 * k + tt:3 + 2 * k + tt], None, ALU.is_equal))
            settle()
            step(tt_op(sel[:, :, :], oh[:, :, 0, :], oh[:, :, 1, :], ALU.add), "chosen")
            wait(dve, "ranks")
            step(v.tensor_copy(rank[:, :, :], bank[7][:, 128:192].rearrange("p (t e) -> p t e", t=TT)))

            def onehot_pair(n, first):
                if not first:
                    dve.wait_ge(sig("gathered").sem, (n - 1) * 4)
                for tt in range(TT):
                    for q in range(2):
                        e = (n - 1) * 2 + q
                        ins = ts(onehot[:, tt, q * CAP:(q + 1) * CAP], iota, rank[:, tt, bass.ds(e, 1)], sel[:, tt, bass.ds(e, 1)],
                                 ALU.is_equal, ALU.mult)
                        if tt and q:
                            ins.then_inc(sig("onehot").sem, 1)

            onehot_pair(1, True)
            wait(dve, "route_exp")
            step(v.reciprocal(rt[:, 218:220], rt[:, 218:220]))
            step(ts(rt[:, 222:224], rt[:, 220:222], 1.0, None, ALU.add))
            step(v.reciprocal(rt[:, 222:224], rt[:, 222:224]))
            step(tt_op(wk[:, :, 0], rt[:, 218:220], rt[:, 222:224], ALU.mult))
            step(tt_op(wk[:, :, 1], wk[:, :, 0], rt[:, 220:222], ALU.mult))
            for tt in range(TT):
                step(ts(cw[:, tt, :], oh[:, tt, 0, :], wk[:, tt, 0:1], None, ALU.mult))
                step(stt(cw[:, tt, :], oh[:, tt, 1, :], wk[:, tt, 1:2], cw[:, tt, :], ALU.mult, ALU.add))
            over_rt = rt[:, 0:64].rearrange("p (t e) -> p t e", t=TT)
            step(stt(over_rt, rank[:, :, :], float(CAP), sel[:, :, :], ALU.is_ge, ALU.mult))
            step(v.reduce_sum(rt[:, 200:201], rt[:, 0:64], AX), "over_counted")
            step(stt(cwo[:, :, :], rank[:, :, :], float(CAP), cw, ALU.is_ge, ALU.mult))
            def weighted_onehot(n):
                if not isinstance(n, int) or n > 1:
                    dve.wait_ge(sig("ohwT").sem, n - 1)
                for tt in range(TT):
                    for q in range(2):
                        e = (n - 1) * 2 + q
                        ins = ts(ohw[:, tt, q * CAP:(q + 1) * CAP], iota, rank[:, tt, bass.ds(e, 1)], cw[:, tt, bass.ds(e, 1)],
                                 ALU.is_equal, ALU.mult)
                ins.then_inc(sig("ohw").sem, 1)

            def add_scattered(n):
                for i in range(8):
                    dve.wait_ge(sig("scattered").sem, (n - 1) * 8 + (i + 1))
                    w = ysum[:, i // 4, (i % 4) * BLK:(i % 4 + 1) * BLK]
                    tt_op(w, w, bank[4 + i % 4][:, :], ALU.add).then_inc(sig("scatter_added").sem, 1)

            def tokens(n):
                for m in range(4):
                    dve.wait_ge(sig("gathered").sem, (n - 1) * 4 + (m + 1))
                    for k in range(4 * m, 4 * m + 4):
                        ins = ts(tokT[:, k, :], bank[GB[m % 3]][:, (k % 4) * P:(k % 4 + 1) * P], aff[:, 2, k:k + 1], aff[:, 3, k:k + 1],
                                 ALU.mult, ALU.add)
                    ins.then_inc(sig("gathered_used").sem, 1)

            def pair(p, gather_next, scatter_last=True):
                for q in range(2):
                    e = p * 2 + q
                    if q == 0:
                        weighted_onehot(p + 1)
                    if q == 1 and gather_next:
                        onehot_pair(p + 2, False)
                    dve.wait_ge(sig("silu").sem, e + 1)
                    tt_op(hid[0:64, :], bank[0][64:128, :], sil[64:128, :], ALU.mult).then_inc(sig("hidden").sem, 1)
                    if q == 0 and scatter_last:
                        add_scattered(p)
                    if q == 1 and gather_next:
                        tokens(p + 2)
                    dve.wait_ge(sig("expert_used").sem, e * HB + 6)
                    for n in range(2):
                        ins = v.tensor_copy(rows[64 * q:64 * q + 64, n * 1024 + BLK:(n + 1) * 1024], bank[3][64 * n:64 * n + 64, :])
                    ins.then_inc(sig("rows_copied").sem, 1)

            tokens(1)
            wait(dve, "over_sum")
            step(v.tensor_copy(flag[:, :], bank[7][:, 192:193]), "over_read")

            step(v.memset(hid[64:128, :], 0.0))
            dve.sem_inc(sig("rows_copied").sem, 1)
            dve.sem_inc(sig("flag_ready").sem, 1)
            wait(dve, "ysum_zero")
            pair(0, True, False)
            with dve.Fori(1, NE // 2 - 1) as p:
                pair(p, True)
            pair(NE // 2 - 1, False)
            add_scattered(NE // 2)
            wait(dve, "scatter_added", 8 * (NE // 2))

            over = nc.vector.value_load(flag[0:1, 0:1], min_val=0, max_val=2 * S)
            with dve.If(over > 0):
                with dve.Fori(0, NE) as e:
                    for tt in range(TT):
                        c = e * 2 + tt
                        dve.wait_ge(sig("dense_silu").sem, c + 1)
                        stt(dhid[:, :], bank[1][:, :], cwo[:, tt, bass.ds(e, 1)], dsil[:, :], ALU.mult, ALU.mult)\
                            .then_inc(sig("dense_hid").sem, 1)
                        dve.wait_ge(sig("dense_T").sem, c + 1)
                        v.tensor_copy(dhidT[:, :], bank[2][:, :]).then_inc(sig("dense_T_copied").sem, 1)
                        dve.wait_ge(sig("dense_down").sem, c + 1)
                        for n in range(4):
                            w = ysum[:, tt, n * BLK:(n + 1) * BLK]
                            ins = tt_op(w, w, bank[4 + n][:, :], ALU.add)
                        ins.then_inc(sig("dense_added").sem, 1)
                dve.wait_ge(sig("dense_added").sem, 2 * NE)
            with dve.Else():
                dve.nop()
            dve.sem_inc(sig("ysum_ready").sem, 1)
            for tt in range(TT):
                do(tt_op(y[:, tt, :], ysum[:, tt, :], RG[:, 1, :], ALU.mult))
            wait(dve, "ysum_squares", 2)
            step(ts(st[:, 8:10], st[:, 8:10], 1.0 / D, EPS, ALU.mult, ALU.add), "ysum_var")
            wait(dve, "ysum_sd")
            step(v.reciprocal(st[:, 8:10], st[:, 8:10]))
            for tt in range(TT):
                do(stt(x_t[:, tt, :], y[:, tt, :], st[:, 8 + tt:9 + tt], x_t[:, tt, :], ALU.mult, ALU.add), sig(f"out{tt}"))


def kernel(**inputs):
    import concourse.bacc as _bacc
    from concourse.bass_utils import run_bass_kernel_spmd as _run

    lay = {k: np.ascontiguousarray(v) for k, v in inputs.items()}
    arrays = {
        "x": lay["x"][0],
        "positions": lay["positions"],
        "w_ada": lay["w_ada"][0],
        "w_in": lay["w_in"][0],
        "w_out": lay["w_out"][0],
        "c": lay["c"].reshape(KT, P),
        "b_ada": lay["b_ada"].reshape(6 * KT, P),
        "lb0": lay["hgrn_lb_logits"][0].reshape(NH, P),
        "lb1": lay["hgrn_lb_logits"][1].reshape(NH, P),
        "hgrn_g_norm": lay["hgrn_g_norm"],
        "b_group": lay["b_group"].reshape(NGRP, 1),
        "b_router": lay["b_router"].reshape(NE, 1),
        "w_gate": lay["w_gate"].reshape(NE, D, FE),
        "w_up": lay["w_up"].reshape(NE, D, FE),
        "w_down": lay["w_down"].reshape(NE, FE, D),
        "consts": constant_table(),
    }
    for name in ("g_pre_mix", "g_post_mix", "g_pre_ffn", "g_post_ffn"):
        arrays[name] = lay[name].reshape(KT, P)
    for name in ("cmp_pe_k", "cmp_w1_k", "cmp_w2_k", "cmp_pe_v", "cmp_w1_v", "cmp_w2_v", "w_group", "w_router"):
        arrays[name] = lay[name][0]
    nc = _bacc.Bacc("TRN2", target_bir_lowering=False, num_devices=1)
    feeds, aps = {}, {}
    for name, arr in arrays.items():
        feeds[f"in_{name}"] = np.ascontiguousarray(arr)
        aps[name] = nc.dram_tensor(f"in_{name}", arr.shape, mybir.dt.from_np(arr.dtype), kind="ExternalInput").ap()
    out = nc.dram_tensor("out_0", (S, D), F32, kind="ExternalOutput").ap()
    block_kernel(nc, aps, out)
    r = _run(nc, [feeds], core_ids=[0])
    return r.results[0]["out_0"].reshape(1, S, D)
```
